# Optimizing a Trainium2 kernel written in Bass

```python
import jax
import jax.numpy as jnp
from jax import lax
import numpy as np
import jax, jax.numpy as jnp

D_MODEL = 1024
BATCH = 1
SEQ = 256
DEPTH = 2

GRID_W = 64
CTX_LEN = 256
N_MIXERS = 4
BLOCK = 128
WINDOW = 128
WIN_HEADS = 16
WIN_KV = 4
WIN_HD = 64
AX_HEADS = 8
AX_KV = 2
AX_HD = 128
ML_HEADS = 4
ML_DK = 128
ML_DV = 256
ML_CHUNK = 128
D_FF = 2816
ROPE_THETA = 10000.0
EPS = 1e-6
NEG = -1e30


def rms_norm(x, g):
    xf = x.astype(jnp.float32)
    y = xf * lax.rsqrt(jnp.mean(xf * xf, axis=-1, keepdims=True) + EPS)
    return (y * g.astype(jnp.float32)).astype(x.dtype)

def dwconv3(x, w):
    xp = jnp.pad(x, ((0, 0), (1, 1), (0, 0)))
    return xp[:, :-2] * w[0] + xp[:, 1:-1] * w[1] + xp[:, 2:] * w[2]

def adaln(cvec, w, b):
    m = (jax.nn.silu(cvec) @ w + b)[..., None, :]
    return jnp.split(m, 6, axis=-1)

def modulate(x, shift, scale):
    return x * (1 + scale) + shift

def axial_rope(n_tok, hd):
    rows = n_tok // GRID_W
    row = jnp.repeat(jnp.arange(rows, dtype=jnp.float32), GRID_W)
    col = jnp.tile(jnp.arange(GRID_W, dtype=jnp.float32), rows)
    n_freq = hd // 4
    inv = jnp.power(ROPE_THETA, -jnp.arange(n_freq, dtype=jnp.float32) / n_freq)
    ang = jnp.concatenate([row[:, None] * inv, col[:, None] * inv], axis=-1)
    return jnp.cos(ang), jnp.sin(ang)

def apply_rope(t, cos, sin):
    t1, t2 = jnp.split(t, 2, axis=-1)
    cos = cos.astype(t.dtype)
    sin = sin.astype(t.dtype)
    return jnp.concatenate([t1 * cos - t2 * sin, t2 * cos + t1 * sin], axis=-1)

def split_heads(t, n_heads, hd):
    b, s, _ = t.shape
    return t.reshape(b, s, n_heads, hd).transpose(0, 2, 1, 3)

def merge_heads(o):
    b, _, _, s, _ = o.shape
    return o.transpose(0, 3, 1, 2, 4).reshape(b, s, -1)

def qkv_heads(a, w_qkv, q_norm, k_norm, n_heads, n_kv, hd):
    b, s, _ = a.shape
    q, k, v = jnp.split(a @ w_qkv, [n_heads * hd, (n_heads + n_kv) * hd], axis=-1)
    q = rms_norm(split_heads(q, n_heads, hd), q_norm).reshape(b, n_kv, n_heads // n_kv, s, hd)
    k = rms_norm(split_heads(k, n_kv, hd), k_norm)
    v = split_heads(v, n_kv, hd)
    return q, k, v

def gqa_softmax(q, k, v, mask, sink):
    s = jnp.einsum('bkgqd,bkjd->bkgqj', q, k, preferred_element_type=jnp.float32) * (q.shape[-1] ** -0.5)
    if mask is not None:
        s = jnp.where(mask, s, NEG)
    if sink is None:
        p = jax.nn.softmax(s, axis=-1)
    else:
        sk = sink.astype(jnp.float32)[None, :, :, None, None]
        m = jnp.maximum(s.max(axis=-1, keepdims=True), sk)
        e = jnp.exp(s - m)
        p = e / (e.sum(axis=-1, keepdims=True) + jnp.exp(sk - m))
    return jnp.einsum('bkgqj,bkjd->bkgqd', p.astype(v.dtype), v)

def window_attention_mixer(a_lat, a_ctx, w_qkv, q_norm, k_norm, sink, w_o, ctx_out):
    b, s, _ = a_lat.shape
    nb = s // BLOCK
    g = WIN_HEADS // WIN_KV
    span = BLOCK + 2 * WINDOW
    q, k, v = qkv_heads(a_lat, w_qkv, q_norm, k_norm, WIN_HEADS, WIN_KV, WIN_HD)
    qc, kc, vc = qkv_heads(a_ctx, w_qkv, q_norm, k_norm, WIN_HEADS, WIN_KV, WIN_HD)
    cos, sin = axial_rope(s, WIN_HD)
    q = apply_rope(q, cos, sin)
    k = apply_rope(k, cos, sin)
    sink = sink.reshape(WIN_KV, g)
    kp = jnp.pad(k, ((0, 0), (0, 0), (WINDOW, WINDOW), (0, 0)))
    vp = jnp.pad(v, ((0, 0), (0, 0), (WINDOW, WINDOW), (0, 0)))
    qb = jnp.moveaxis(q.reshape(b, WIN_KV, g, nb, BLOCK, WIN_HD), 3, 0)
    offs = jnp.arange(span) - WINDOW
    ctx_cols = jnp.ones((BLOCK, kc.shape[2]), bool)

    def block(args):
        bi, qblk = args
        start = bi * BLOCK
        kw = jnp.concatenate([lax.dynamic_slice_in_dim(kp, start, span, axis=2), kc], axis=2)
        vw = jnp.concatenate([lax.dynamic_slice_in_dim(vp, start, span, axis=2), vc], axis=2)
        qpos = start + jnp.arange(BLOCK)
        kpos = start + offs
        band = (jnp.abs(qpos[:, None] - kpos[None, :]) <= WINDOW) & (kpos >= 0)[None, :] & (kpos < s)[None, :]
        return gqa_softmax(qblk, kw, vw, jnp.concatenate([band, ctx_cols], axis=1), sink)

    o = lax.map(block, (jnp.arange(nb), qb))
    o = jnp.moveaxis(o, 0, 3).reshape(b, WIN_KV, g, s, WIN_HD)
    y_lat = merge_heads(o) @ w_o
    y_ctx = merge_heads(gqa_softmax(qc, kc, vc, None, sink)) @ w_o if ctx_out else None
    return y_lat, y_ctx

def short_conv_mixer(a, w_in, conv_w, w_out):
    gate_b, gate_c, u = jnp.split(a @ w_in, 3, axis=-1)
    return (gate_b * dwconv3(gate_c * u, conv_w)) @ w_out

def axial_attention_mixer(a_lat, a_ctx, w_qkv, q_norm, k_norm, w_o, ctx_out):
    b, s, _ = a_lat.shape
    nb = s // BLOCK
    g = AX_HEADS // AX_KV
    q, k, v = qkv_heads(a_lat, w_qkv, q_norm, k_norm, AX_HEADS, AX_KV, AX_HD)
    qc, kc, vc = qkv_heads(a_ctx, w_qkv, q_norm, k_norm, AX_HEADS, AX_KV, AX_HD)
    cos, sin = axial_rope(s, AX_HD)
    q = apply_rope(q, cos, sin)
    k = apply_rope(k, cos, sin)
    k_all = jnp.concatenate([k, kc], axis=2)
    v_all = jnp.concatenate([v, vc], axis=2)
    qb = jnp.moveaxis(q.reshape(b, AX_KV, g, nb, BLOCK, AX_HD), 3, 0)

    def block(qblk):
        return gqa_softmax(qblk, k_all, v_all, None, None)

    o = lax.map(block, qb)
    o = jnp.moveaxis(o, 0, 3).reshape(b, AX_KV, g, s, AX_HD)
    y_lat = merge_heads(o) @ w_o
    y_ctx = merge_heads(gqa_softmax(qc, kc, vc, None, None)) @ w_o if ctx_out else None
    return y_lat, y_ctx

def mlstm_chunk_summary(k, v, log_i, log_f):
    cum = jnp.cumsum(log_f, axis=-1)
    a = cum[..., -1:] - cum + log_i
    m = a.max(axis=-1)
    w = jnp.exp(a - m[..., None])
    c_bar = jnp.einsum('...lv,...lk->...vk', v * w[..., None], k)
    n_bar = jnp.einsum('...l,...lk->...k', w, k)
    return c_bar, n_bar, m, cum

def mlstm_final_state(k, v, log_i, log_f):
    c_bar, n_bar, m, _ = mlstm_chunk_summary(k, v, log_i, log_f)
    return (c_bar, n_bar, m)

def mlstm_chunkwise(q, k, v, log_i, log_f, state):
    b, h, s, dk = q.shape
    dv = v.shape[-1]
    nc = s // ML_CHUNK
    qc = q.reshape(b, h, nc, ML_CHUNK, dk)
    kc = k.reshape(b, h, nc, ML_CHUNK, dk)
    vc = v.reshape(b, h, nc, ML_CHUNK, dv)
    lic = log_i.reshape(b, h, nc, ML_CHUNK)
    lfc = log_f.reshape(b, h, nc, ML_CHUNK)
    c_bar, n_bar, m_bar, cum = mlstm_chunk_summary(kc, vc, lic, lfc)

    def step(carry, xs):
        c_prev, n_prev, m_prev = carry
        cb, nb_, mb, gb = xs
        m_new = jnp.maximum(gb + m_prev, mb)
        decay = jnp.exp(gb + m_prev - m_new)
        inj = jnp.exp(mb - m_new)
        c_new = decay[..., None, None] * c_prev + inj[..., None, None] * cb
        n_new = decay[..., None] * n_prev + inj[..., None] * nb_
        return (c_new, n_new, m_new), (c_prev, n_prev, m_prev)

    xs = (jnp.moveaxis(c_bar, 2, 0), jnp.moveaxis(n_bar, 2, 0), jnp.moveaxis(m_bar, 2, 0), jnp.moveaxis(cum[..., -1], 2, 0))
    final, (c_start, n_start, m_start) = lax.scan(step, state, xs)
    c_start = jnp.moveaxis(c_start, 0, 2)
    n_start = jnp.moveaxis(n_start, 0, 2)
    m_start = jnp.moveaxis(m_start, 0, 2)
    tri = jnp.tril(jnp.ones((ML_CHUNK, ML_CHUNK), bool))
    d = jnp.where(tri, cum[..., :, None] - cum[..., None, :] + lic[..., None, :], NEG)
    inter = cum + m_start[..., None]
    m_t = jnp.maximum(inter, d.max(axis=-1))
    w_intra = jnp.exp(d - m_t[..., None])
    w_inter = jnp.exp(inter - m_t)
    qk = jnp.einsum('bhcld,bhcsd->bhcls', qc, kc) * w_intra
    num = jnp.einsum('bhcls,bhcsv->bhclv', qk, vc) + w_inter[..., None] * jnp.einsum('bhcld,bhcvd->bhclv', qc, c_start)
    den = qk.sum(axis=-1) + w_inter * jnp.einsum('bhcld,bhcd->bhcl', qc, n_start)
    out = num / jnp.maximum(jnp.abs(den), jnp.exp(-m_t))[..., None]
    return out.reshape(b, h, s, dv), final

def mlstm_mixer(a_lat, a_ctx, w_in, b_gate, h_norm, w_out, ctx_out):
    qk_w = ML_HEADS * ML_DK
    v_w = ML_HEADS * ML_DV

    def proj(a):
        b, s, _ = a.shape
        q, k, v, o, gates = jnp.split(a @ w_in, [qk_w, 2 * qk_w, 2 * qk_w + v_w, 2 * qk_w + 2 * v_w], axis=-1)
        q = split_heads(q, ML_HEADS, ML_DK).astype(jnp.float32) * (ML_DK ** -0.5)
        k = split_heads(k, ML_HEADS, ML_DK).astype(jnp.float32)
        v = split_heads(v, ML_HEADS, ML_DV).astype(jnp.float32)
        gates = (gates + b_gate).astype(jnp.float32).reshape(b, s, 4, ML_HEADS).transpose(2, 0, 3, 1)
        fwd = (gates[0], jax.nn.log_sigmoid(gates[1]))
        bwd = (gates[2], jax.nn.log_sigmoid(gates[3]))
        return q, k, v, o, fwd, bwd

    def flip(t):
        return jnp.flip(t, axis=2)

    def readout(h_f, h_b, o):
        hs = rms_norm(h_f + flip(h_b), h_norm)
        b, h, s, dv = hs.shape
        hs = hs.transpose(0, 2, 1, 3).reshape(b, s, h * dv).astype(o.dtype)
        return (jax.nn.sigmoid(o) * hs) @ w_out

    qc, kc, vc, oc, gfc, gbc = proj(a_ctx)
    bsz = a_ctx.shape[0]
    zero = (jnp.zeros((bsz, ML_HEADS, ML_DV, ML_DK), jnp.float32),
            jnp.zeros((bsz, ML_HEADS, ML_DK), jnp.float32),
            jnp.full((bsz, ML_HEADS), NEG, jnp.float32))
    if ctx_out:
        hc_f, st_f = mlstm_chunkwise(qc, kc, vc, gfc[0], gfc[1], zero)
        hc_b, st_b = mlstm_chunkwise(flip(qc), flip(kc), flip(vc), flip(gbc[0]), flip(gbc[1]), zero)
        y_ctx = readout(hc_f, hc_b, oc)
    else:
        st_f = mlstm_final_state(kc, vc, gfc[0], gfc[1])
        st_b = mlstm_final_state(flip(kc), flip(vc), flip(gbc[0]), flip(gbc[1]))
        y_ctx = None
    ql, kl, vl, ol, gfl, gbl = proj(a_lat)
    hl_f, _ = mlstm_chunkwise(ql, kl, vl, gfl[0], gfl[1], st_f)
    hl_b, _ = mlstm_chunkwise(flip(ql), flip(kl), flip(vl), flip(gbl[0]), flip(gbl[1]), st_b)
    return readout(hl_f, hl_b, ol), y_ctx

def conv_ffn(a, w_up, conv_w, w_down):
    g, u = jnp.split(dwconv3(a @ w_up, conv_w), 2, axis=-1)
    return (jax.nn.silu(g) * u) @ w_down

def first_inputs(seed: int = 0) -> dict:
    d = D_MODEL
    n_win, n_sc, n_ax, n_ml = [len(range(kind, DEPTH, N_MIXERS)) for kind in range(N_MIXERS)]
    keys = iter(jax.random.split(jax.random.key(seed), 40))

    def normal(shape, std):
        return std * jax.random.normal(next(keys), shape, jnp.float32)

    def gain(shape):
        return 1.0 + normal(shape, 0.1)

    ml_in = 2 * ML_HEADS * ML_DK + 2 * ML_HEADS * ML_DV + 4 * ML_HEADS
    f_base = jnp.linspace(3.0, 6.0, ML_HEADS, dtype=jnp.float32)
    zeros_h = jnp.zeros((ML_HEADS,), jnp.float32)
    gate_base = jnp.concatenate([zeros_h, f_base, zeros_h, f_base])
    return {
        'x': normal((BATCH, SEQ, d), 1.0),
        'c': normal((BATCH, d), 1.0),
        'ctx': normal((BATCH, CTX_LEN, d), 1.0),
        'c_ctx': normal((d,), 1.0),
        'ada_w': normal((DEPTH, d, 6 * d), 0.5 * d ** -0.5),
        'ada_b': normal((DEPTH, 6 * d), 0.02),
        'norm_mix': gain((DEPTH, d)),
        'norm_ffn': gain((DEPTH, d)),
        'ffn_w_up': normal((DEPTH, d, 2 * D_FF), d ** -0.5),
        'ffn_conv': normal((DEPTH, 3, 2 * D_FF), 3 ** -0.5),
        'ffn_w_down': normal((DEPTH, D_FF, d), D_FF ** -0.5),
        'win_w_qkv': normal((n_win, d, (WIN_HEADS + 2 * WIN_KV) * WIN_HD), d ** -0.5),
        'win_q_norm': gain((n_win, WIN_HD)),
        'win_k_norm': gain((n_win, WIN_HD)),
        'win_sink': normal((n_win, WIN_HEADS), 0.5),
        'win_w_o': normal((n_win, WIN_HEADS * WIN_HD, d), (WIN_HEADS * WIN_HD) ** -0.5),
        'sc_w_in': normal((n_sc, d, 3 * d), d ** -0.5),
        'sc_conv': normal((n_sc, 3, d), 3 ** -0.5),
        'sc_w_out': normal((n_sc, d, d), d ** -0.5),
        'ax_w_qkv': normal((n_ax, d, (AX_HEADS + 2 * AX_KV) * AX_HD), d ** -0.5),
        'ax_q_norm': gain((n_ax, AX_HD)),
        'ax_k_norm': gain((n_ax, AX_HD)),
        'ax_w_o': normal((n_ax, AX_HEADS * AX_HD, d), (AX_HEADS * AX_HD) ** -0.5),
        'ml_w_in': normal((n_ml, d, ml_in), d ** -0.5),
        'ml_b_gate': gate_base + normal((n_ml, 4 * ML_HEADS), 0.1),
        'ml_h_norm': gain((n_ml, ML_DV)),
        'ml_w_out': normal((n_ml, ML_HEADS * ML_DV, d), (ML_HEADS * ML_DV) ** -0.5),
    }

def first_block(x, c, ctx, c_ctx, ada_w, ada_b, norm_mix, norm_ffn, ffn_w_up, ffn_conv, ffn_w_down,
              win_w_qkv, win_q_norm, win_k_norm, win_sink, win_w_o,
              sc_w_in, sc_conv, sc_w_out,
              ax_w_qkv, ax_q_norm, ax_k_norm, ax_w_o,
              ml_w_in, ml_b_gate, ml_h_norm, ml_w_out):
    h, hc = x, ctx
    for i in range(DEPTH):
        kind, j = i % N_MIXERS, i // N_MIXERS
        ctx_out = i < DEPTH - 1
        sh1, sc1, g1, sh2, sc2, g2 = adaln(c, ada_w[i], ada_b[i])
        a_lat = modulate(rms_norm(h, norm_mix[i]), sh1, sc1)
        if ctx_out or kind != 1:
            csh1, csc1, cg1, csh2, csc2, cg2 = adaln(c_ctx, ada_w[i], ada_b[i])
            a_ctx = modulate(rms_norm(hc, norm_mix[i]), csh1, csc1)
        if kind == 0:
            y_lat, y_ctx = window_attention_mixer(a_lat, a_ctx, win_w_qkv[j], win_q_norm[j], win_k_norm[j],
                                                  win_sink[j], win_w_o[j], ctx_out)
        elif kind == 1:
            y_lat = short_conv_mixer(a_lat, sc_w_in[j], sc_conv[j], sc_w_out[j])
            y_ctx = short_conv_mixer(a_ctx, sc_w_in[j], sc_conv[j], sc_w_out[j]) if ctx_out else None
        elif kind == 2:
            y_lat, y_ctx = axial_attention_mixer(a_lat, a_ctx, ax_w_qkv[j], ax_q_norm[j], ax_k_norm[j],
                                                 ax_w_o[j], ctx_out)
        else:
            y_lat, y_ctx = mlstm_mixer(a_lat, a_ctx, ml_w_in[j], ml_b_gate[j], ml_h_norm[j], ml_w_out[j], ctx_out)
        h = h + g1 * y_lat
        h = h + g2 * conv_ffn(modulate(rms_norm(h, norm_ffn[i]), sh2, sc2), ffn_w_up[i], ffn_conv[i], ffn_w_down[i])
        if ctx_out:
            hc = hc + cg1 * y_ctx
            hc = hc + cg2 * conv_ffn(modulate(rms_norm(hc, norm_ffn[i]), csh2, csc2),
                                     ffn_w_up[i], ffn_conv[i], ffn_w_down[i])
    return h


DEPTH_2 = 1

HEAD_DIM = 64
N_NSA_HEADS = 8
N_NSA_KV = 2
NSA_GROUP = N_NSA_HEADS // N_NSA_KV
N_FOX_HEADS = 8
D_NSA = N_NSA_HEADS * HEAD_DIM
D_FOX = N_FOX_HEADS * HEAD_DIM
D_MIX = D_NSA + D_FOX
D_KV = N_NSA_KV * HEAD_DIM
D_PROJ = D_NSA + 6 * D_KV + 3 * N_NSA_HEADS + 3 * D_FOX + N_FOX_HEADS
CMP_BLOCK = 32
CMP_STRIDE = 16
CMP_HIDDEN = 128
SEL_BLOCK = 64
SEL_TOPK = 16
WINDOW_2 = 512
Q_BLOCK = 128
N_EXPERTS = 32
TOP_K = 4
D_FF_2 = D_MODEL
SWIGLU_LIMIT = 7.0
SWIGLU_ALPHA = 1.702
PLE_DIM = 256
NEG_2 = -1e30
FORCED_SCORE = 1e9


def rmsnorm(x, g):
    xf = x.astype(jnp.float32)
    y = xf * lax.rsqrt(jnp.mean(xf * xf, axis=-1, keepdims=True) + EPS)
    return (y * g.astype(jnp.float32)).astype(x.dtype)

def masked_softmax(logits, mask):
    logits = jnp.where(mask, logits.astype(jnp.float32), NEG_2)
    m = jnp.max(logits, axis=-1, keepdims=True)
    e = jnp.exp(logits - m) * mask
    return e / jnp.maximum(jnp.sum(e, axis=-1, keepdims=True), 1e-30)

def alibi_slopes(n):
    return jnp.exp2(-8.0 * jnp.arange(1, n + 1, dtype=jnp.float32) / n)

def proj_split_points():
    sizes = [D_NSA, D_KV, D_KV, D_KV, D_KV, D_KV, D_KV, 3 * N_NSA_HEADS,
             D_FOX, D_FOX, D_FOX, N_FOX_HEADS]
    pts, acc = [], 0
    for s in sizes[:-1]:
        acc += s
        pts.append(acc)
    return pts

def compress(kv, w1, w2, pe):
    B, T, G, Dh = kv.shape
    nc = (T - CMP_BLOCK) // CMP_STRIDE + 1
    idx = jnp.arange(nc)[:, None] * CMP_STRIDE + jnp.arange(CMP_BLOCK)[None, :]
    blocks = kv[:, idx] + pe[None, None, :, None, :]
    blocks = jnp.swapaxes(blocks, 2, 3).reshape(B, nc, G, CMP_BLOCK * Dh)
    return jax.nn.gelu(blocks @ w1) @ w2

def nsa_attention(q, k_c, v_c, k_s, v_s, k_w, v_w, gate_logits, slopes):
    B, T, H, Dh = q.shape
    G = k_s.shape[2]
    R = H // G
    scale = Dh ** -0.5
    nc = k_c.shape[1]
    ns = T // SEL_BLOCK
    topk = min(SEL_TOPK, ns)
    cmp_start = jnp.arange(nc) * CMP_STRIDE
    cmp_end = cmp_start + CMP_BLOCK - 1
    sel_start = jnp.arange(ns) * SEL_BLOCK
    overlap = ((cmp_start[:, None] < sel_start[None, :] + SEL_BLOCK)
               & (cmp_end[:, None] >= sel_start[None, :])).astype(jnp.float32)
    ks_blocks = k_s.reshape(B, ns, SEL_BLOCK, G, Dh).transpose(0, 3, 1, 2, 4)
    vs_blocks = v_s.reshape(B, ns, SEL_BLOCK, G, Dh).transpose(0, 3, 1, 2, 4)
    pad = jnp.zeros((B, WINDOW_2, G, Dh), k_w.dtype)
    kw_pad = jnp.concatenate([pad, k_w], axis=1)
    vw_pad = jnp.concatenate([pad, v_w], axis=1)
    qg = q.reshape(B, T, G, R, Dh)
    gates = jax.nn.sigmoid(gate_logits.reshape(B, T, G, R, 3))
    sl = slopes.reshape(G, R)
    b_ix = jnp.arange(B)[:, None, None, None]
    g_ix = jnp.arange(G)[None, None, :, None]
    j_sel = jnp.arange(ns)
    l_sel = jnp.arange(SEL_BLOCK)

    def block(start):
        qb = lax.dynamic_slice_in_dim(qg, start, Q_BLOCK, 1)
        gb = lax.dynamic_slice_in_dim(gates, start, Q_BLOCK, 1)
        t = start + jnp.arange(Q_BLOCK)
        lc = jnp.einsum('bqgrd,bcgd->bqgrc', qb, k_c).astype(jnp.float32) * scale
        dist_c = (t[:, None] - cmp_end[None, :]).astype(jnp.float32)
        lc = lc - sl[None, None, :, :, None] * dist_c[None, :, None, None, :]
        mask_c = (cmp_end[None, :] <= t[:, None])[None, :, None, None, :]
        p_c = masked_softmax(lc, mask_c)
        o_c = jnp.einsum('bqgrc,bcgd->bqgrd', p_c.astype(v_c.dtype), v_c)
        imp = jnp.einsum('bqgrc,cn->bqgn', p_c, overlap)
        cur = t // SEL_BLOCK
        valid = j_sel[None, :] <= cur[:, None]
        forced = valid & ((j_sel[None, :] == 0) | (j_sel[None, :] == cur[:, None])
                          | (j_sel[None, :] == cur[:, None] - 1))
        score = jnp.where(forced[None, :, None, :], FORCED_SCORE,
                          jnp.where(valid[None, :, None, :], imp, -1.0))
        _, idx = lax.top_k(score, topk)
        ks = ks_blocks[b_ix, g_ix, idx]
        vs = vs_blocks[b_ix, g_ix, idx]
        ls = jnp.einsum('bqgrd,bqgkld->bqgrkl', qb, ks).astype(jnp.float32) * scale
        pos = idx[..., None] * SEL_BLOCK + l_sel
        dist_s = (t[None, :, None, None, None] - pos)[:, :, :, None]
        ls = ls - sl[None, None, :, :, None, None] * dist_s.astype(jnp.float32)
        mask_s = jnp.broadcast_to(dist_s >= 0, ls.shape)
        flat = (B, Q_BLOCK, G, R, topk * SEL_BLOCK)
        p_s = masked_softmax(ls.reshape(flat), mask_s.reshape(flat)).reshape(ls.shape)
        o_s = jnp.einsum('bqgrkl,bqgkld->bqgrd', p_s.astype(vs.dtype), vs)
        kw = lax.dynamic_slice_in_dim(kw_pad, start, Q_BLOCK + WINDOW_2, 1)
        vw = lax.dynamic_slice_in_dim(vw_pad, start, Q_BLOCK + WINDOW_2, 1)
        s = start - WINDOW_2 + jnp.arange(Q_BLOCK + WINDOW_2)
        dist_w = t[:, None] - s[None, :]
        lw = jnp.einsum('bqgrd,bsgd->bqgrs', qb, kw).astype(jnp.float32) * scale
        lw = lw - sl[None, None, :, :, None] * dist_w.astype(jnp.float32)[None, :, None, None, :]
        mask_w = ((dist_w >= 0) & (dist_w < WINDOW_2) & (s[None, :] >= 0))[None, :, None, None, :]
        p_w = masked_softmax(lw, mask_w)
        o_w = jnp.einsum('bqgrs,bsgd->bqgrd', p_w.astype(vw.dtype), vw)
        o = gb[..., 0:1] * o_c + gb[..., 1:2] * o_s + gb[..., 2:3] * o_w
        return o.reshape(B, Q_BLOCK, H * Dh)

    starts = jnp.arange(T // Q_BLOCK) * Q_BLOCK
    out = lax.map(block, starts)
    return out.transpose(1, 0, 2, 3).reshape(B, T, H * Dh)

def fox_attention(q, k, v, f_logit):
    B, T, H, Dh = q.shape
    scale = Dh ** -0.5
    c = jnp.cumsum(jax.nn.log_sigmoid(f_logit.astype(jnp.float32)), axis=1).transpose(0, 2, 1)
    kpos = jnp.arange(T)

    def block(start):
        qb = lax.dynamic_slice_in_dim(q, start, Q_BLOCK, 1)
        cb = lax.dynamic_slice_in_dim(c, start, Q_BLOCK, 2)
        t = start + jnp.arange(Q_BLOCK)
        l = jnp.einsum('bqhd,bshd->bhqs', qb, k).astype(jnp.float32) * scale
        l = l + (cb[..., None] - c[:, :, None, :])
        mask = (kpos[None, :] <= t[:, None])[None, None]
        pr = masked_softmax(l, mask)
        o = jnp.einsum('bhqs,bshd->bqhd', pr.astype(v.dtype), v)
        return o.reshape(B, Q_BLOCK, H * Dh)

    starts = jnp.arange(T // Q_BLOCK) * Q_BLOCK
    out = lax.map(block, starts)
    return out.transpose(1, 0, 2, 3).reshape(B, T, H * Dh)

def moe(x, w_router, b_router, w_up, b_up, w_down, b_down):
    B, T, D = x.shape
    xf = x.reshape(-1, D)
    n = xf.shape[0]
    logits = (xf @ w_router + b_router).astype(jnp.float32)
    top_v, top_i = lax.top_k(logits, TOP_K)
    w = jax.nn.softmax(top_v, axis=-1)
    flat_e = top_i.reshape(-1)
    order = jnp.argsort(flat_e)
    sorted_e = flat_e[order]
    tok = order // TOP_K
    sizes = jnp.bincount(flat_e, length=N_EXPERTS).astype(jnp.int32)
    xs = xf[tok]
    h = lax.ragged_dot(xs, w_up, sizes) + b_up[sorted_e]
    g, lin = jnp.split(h, 2, axis=-1)
    g = jnp.minimum(g, SWIGLU_LIMIT)
    lin = jnp.clip(lin, -SWIGLU_LIMIT, SWIGLU_LIMIT)
    act = g * jax.nn.sigmoid(SWIGLU_ALPHA * g) * (lin + 1.0)
    y = lax.ragged_dot(act, w_down, sizes) + b_down[sorted_e]
    y = y * w.reshape(-1)[order][:, None].astype(y.dtype)
    return jax.ops.segment_sum(y, tok, num_segments=n).reshape(B, T, D)

def second_inputs(seed: int = 0) -> dict:
    key = jax.random.key(seed)
    ks = jax.random.split(key, 32)
    L, D, E, F = DEPTH_2, D_MODEL, N_EXPERTS, D_FF_2
    nrm = lambda k, shape, fan: jax.random.normal(k, shape, jnp.float32) * (fan ** -0.5)
    gain = lambda k, shape: 1.0 + 0.02 * jax.random.normal(k, shape, jnp.float32)
    small = lambda k, shape, s: s * jax.random.normal(k, shape, jnp.float32)
    return {
        "x": jax.random.normal(ks[0], (BATCH, SEQ, D), jnp.float32),
        "p": jax.random.normal(ks[1], (L, BATCH, SEQ, PLE_DIM), jnp.float32),
        "ln1": gain(ks[2], (L, D)),
        "w_in": nrm(ks[3], (L, D, D_PROJ), D),
        "b_fg": jax.random.uniform(ks[4], (L, N_FOX_HEADS), jnp.float32, 1.0, 5.0),
        "w_cmp1_k": nrm(ks[5], (L, CMP_BLOCK * HEAD_DIM, CMP_HIDDEN), CMP_BLOCK * HEAD_DIM),
        "w_cmp2_k": nrm(ks[6], (L, CMP_HIDDEN, HEAD_DIM), CMP_HIDDEN),
        "pe_cmp_k": small(ks[7], (L, CMP_BLOCK, HEAD_DIM), 0.1),
        "w_cmp1_v": nrm(ks[8], (L, CMP_BLOCK * HEAD_DIM, CMP_HIDDEN), CMP_BLOCK * HEAD_DIM),
        "w_cmp2_v": nrm(ks[9], (L, CMP_HIDDEN, HEAD_DIM), CMP_HIDDEN),
        "pe_cmp_v": small(ks[10], (L, CMP_BLOCK, HEAD_DIM), 0.1),
        "gn_nsa": gain(ks[11], (L, D_NSA)),
        "gn_fox": gain(ks[12], (L, D_FOX)),
        "w_out": nrm(ks[13], (L, D_MIX, D), D_MIX),
        "ln2": gain(ks[14], (L, D)),
        "w_router": nrm(ks[15], (L, D, E), D),
        "b_router": small(ks[16], (L, E), 0.01),
        "w_up": nrm(ks[17], (L, E, D, 2 * F), D),
        "b_up": small(ks[18], (L, E, 2 * F), 0.01),
        "w_down": nrm(ks[19], (L, E, F, D), F),
        "b_down": small(ks[20], (L, E, D), 0.01),
        "ln_ple": gain(ks[21], (L, D)),
        "w_ple": nrm(ks[22], (L, PLE_DIM, D), PLE_DIM),
        "w_ple_gate": nrm(ks[23], (L, D, D), D),
        "ln_f": gain(ks[24], (D,)),
    }

def second_block(x, p, ln1, w_in, b_fg, w_cmp1_k, w_cmp2_k, pe_cmp_k, w_cmp1_v, w_cmp2_v,
              pe_cmp_v, gn_nsa, gn_fox, w_out, ln2, w_router, b_router, w_up, b_up,
              w_down, b_down, ln_ple, w_ple, w_ple_gate, ln_f):
    B, T, _ = x.shape
    G, Dh = N_NSA_KV, HEAD_DIM
    slopes = alibi_slopes(N_NSA_HEADS)
    pts = proj_split_points()
    h = x
    for i in range(DEPTH_2):
        u = rmsnorm(h, ln1[i])
        proj = u @ w_in[i]
        (q_n, k_c, v_c, k_s, v_s, k_w, v_w, g_n,
         q_f, k_f, v_f, f_f) = jnp.split(proj, pts, axis=-1)
        kc = compress(k_c.reshape(B, T, G, Dh), w_cmp1_k[i], w_cmp2_k[i], pe_cmp_k[i])
        vc = compress(v_c.reshape(B, T, G, Dh), w_cmp1_v[i], w_cmp2_v[i], pe_cmp_v[i])
        o_nsa = nsa_attention(q_n.reshape(B, T, N_NSA_HEADS, Dh), kc, vc,
                              k_s.reshape(B, T, G, Dh), v_s.reshape(B, T, G, Dh),
                              k_w.reshape(B, T, G, Dh), v_w.reshape(B, T, G, Dh),
                              g_n.reshape(B, T, N_NSA_HEADS, 3), slopes)
        o_fox = fox_attention(q_f.reshape(B, T, N_FOX_HEADS, Dh),
                              k_f.reshape(B, T, N_FOX_HEADS, Dh),
                              v_f.reshape(B, T, N_FOX_HEADS, Dh),
                              f_f + b_fg[i])
        mix = jnp.concatenate([rmsnorm(o_nsa, gn_nsa[i]), rmsnorm(o_fox, gn_fox[i])], axis=-1)
        h = h + mix @ w_out[i]
        h = h + moe(rmsnorm(h, ln2[i]), w_router[i], b_router[i], w_up[i], b_up[i],
                    w_down[i], b_down[i])
        h = h + (p[i] @ w_ple[i]) * jax.nn.sigmoid(rmsnorm(h, ln_ple[i]) @ w_ple_gate[i])
    return rmsnorm(h, ln_f)


def setup_inputs(seed=0):
    out = dict(first_inputs(seed))
    for name, value in second_inputs(seed + 1).items():
        if name != "x":
            out[name + "_2"] = value
    return out


def reference(
    x, c, ctx, c_ctx, ada_w, ada_b, norm_mix, norm_ffn, ffn_w_up, ffn_conv, ffn_w_down,
    win_w_qkv, win_q_norm, win_k_norm, win_sink, win_w_o, sc_w_in, sc_conv, sc_w_out, ax_w_qkv,
    ax_q_norm, ax_k_norm, ax_w_o, ml_w_in, ml_b_gate, ml_h_norm, ml_w_out, p_2, ln1_2, w_in_2,
    b_fg_2, w_cmp1_k_2, w_cmp2_k_2, pe_cmp_k_2, w_cmp1_v_2, w_cmp2_v_2, pe_cmp_v_2, gn_nsa_2,
    gn_fox_2, w_out_2, ln2_2, w_router_2, b_router_2, w_up_2, b_up_2, w_down_2, b_down_2,
    ln_ple_2, w_ple_2, w_ple_gate_2, ln_f_2,
):
    x = first_block(
        x, c, ctx, c_ctx, ada_w, ada_b, norm_mix, norm_ffn, ffn_w_up, ffn_conv, ffn_w_down,
        win_w_qkv, win_q_norm, win_k_norm, win_sink, win_w_o, sc_w_in, sc_conv, sc_w_out,
        ax_w_qkv, ax_q_norm, ax_k_norm, ax_w_o, ml_w_in, ml_b_gate, ml_h_norm, ml_w_out,
    )
    return second_block(
        x, p_2, ln1_2, w_in_2, b_fg_2, w_cmp1_k_2, w_cmp2_k_2, pe_cmp_k_2, w_cmp1_v_2,
        w_cmp2_v_2, pe_cmp_v_2, gn_nsa_2, gn_fox_2, w_out_2, ln2_2, w_router_2, b_router_2,
        w_up_2, b_up_2, w_down_2, b_down_2, ln_ple_2, w_ple_2, w_ple_gate_2, ln_f_2,
    )


_drawn_inputs = setup_inputs


def setup_inputs(seed=0):
    import zlib

    import numpy as np

    out = dict(_drawn_inputs(seed))
    spreads = {}
    factors = {'win_q_norm': 4.206,
     'win_k_norm': 3.993,
     'win_sink': 8.0,
     'pe_cmp_k_2': 3.532,
     'b_router_2': 3.022,
     'b_up_2': 8.0,
     'b_down_2': 8.0,
     'ln_ple_2': 150.082,
     'ln_f_2': 22.85}
    for name, (base, spread) in spreads.items():
        noise = np.random.default_rng([zlib.crc32(name.encode()), seed]).standard_normal(out[name].shape)
        drawn = base * np.exp(spread * noise) if base else spread * noise
        out[name] = jnp.asarray(drawn.astype(out[name].dtype))
    for name, factor in factors.items():
        out[name] = (out[name] * factor).astype(out[name].dtype)
    return out
```

```python
import concourse.bass as bass
from concourse import mybir
from concourse.alu_op_type import AluOpType as ALU
from contextlib import ExitStack
import numpy as np

F32 = mybir.dt.float32
F32R = mybir.dt.float32r
BF16 = mybir.dt.bfloat16
ACT = mybir.ActivationFunctionType
AX = mybir.AxisListType

KB = 1024
BASE = 16 * KB + 128
EPS = 1e-6
NEG = -1e30


class Line:

    def __init__(self, sem):
        self.sem = sem
        self.count = 0
        self.ops = []
        self.seen = {}

    def do(self, f):
        self.ops.append(f)

    def mark(self, f):
        self.count += 1
        self.ops.append(lambda e: f(e).then_inc(self.sem, 1))
        return (self.sem, self.count)

    def wait(self, *marks):
        for sem, value in marks:
            if self.seen.get(id(sem), 0) < value:
                self.seen[id(sem)] = value
                self.ops.append(lambda e, s=sem, v=value: e.wait_ge(s, v))

    def run(self, e):
        for f in self.ops:
            f(e)


class Branch:

    def __init__(self, lines, count, limit):
        self.lines, self.count, self.limit = lines, count, limit

    def __enter__(self):
        self.before = [(L.ops, L.count, dict(L.seen)) for L in self.lines]
        for L in self.lines:
            L.ops = []

    def __exit__(self, *_):
        for L, (ops, before, seen) in zip(self.lines, self.before):
            body, L.ops, L.seen = L.ops, ops, seen
            L.ops.append(self.both(L, body, before, L.count - before))

    def both(self, L, body, before, added):
        def f(e):
            with e.If(self.count[id(L)] > self.limit):
                for g in body:
                    g(e)
            with e.Else():
                e.wait_ge(L.sem, before)
                e.sem_inc(L.sem, added)
        return f


def act(out, in_, func, **kw):
    return lambda e: e.activation(out, in_, func, **kw)


def tt(out, a, b, op):
    return lambda e: e.tensor_tensor(out, a, b, op)


def ts(out, a, s1, op0, s2=None, op1=None, **kw):
    if op1 is None:
        return lambda e: e.tensor_scalar(out, a, s1, None, op0, **kw)
    return lambda e: e.tensor_scalar(out, a, s1, s2, op0, op1, **kw)


def stt(out, a, s, b, op0, op1, **kw):
    return lambda e: e.scalar_tensor_tensor(out, a, s, b, op0, op1, **kw)


def cp(out, a):
    return lambda e: e.tensor_copy(out, a)


def fill(out, v):
    return lambda e: e.memset(out, v)


def red(out, a, op, **kw):
    return lambda e: e.tensor_reduce(out, a, AX.X, op, **kw)


def recip(out, a):
    return lambda e: e.reciprocal(out, a)


def mm(out, w, x, start, stop, skip=False):
    return lambda e: e.matmul(out, w, x, start=start, stop=stop, skip_group_check=skip)


def tp(out, a, ident):
    return lambda e: e.transpose(out, a, ident)


def dma(out, in_):
    return lambda e: e.dma_start(out, in_)


def layout(parts):
    at, out = 0, {}
    for name, n in parts:
        out[name] = (at, at + n)
        at += n
    return out, at


CST1, N1 = layout([("blk", 128), ("perm", 128), ("cos", 256), ("sin", 256), ("m01", 128), ("m10", 128), ("hd", 32)])
CST2, N2 = layout([("zto", 384), ("cbias", 256), ("cmask", 256), ("hrow", 8), ("alibi", 256), ("pick", 8), ("iota", 256)])
NC = max(N1, N2)
VEC, NVEC = layout([("cc", 256), ("nm0", 8), ("nm1", 8), ("nf0", 8), ("nf1", 8), ("ada_b0", 48), ("ada_b1", 48),
                    ("qn", 1), ("kn", 1), ("sink", 16), ("conv0", 132), ("conv1", 132), ("scconv", 24),
                    ("ln1", 8), ("ln2", 8), ("lnp", 8), ("lnf", 8), ("gn", 8), ("pe0", 32), ("pe1", 32), ("bfg", 8),
                    ("w2k", 128), ("w2v", 64)])


def program(nc, xT, ctxT, cid, cst1, cst2, vec, ada_w, w_qkv, w_o, w_up, w_down, sc_in, sc_out, w_in, w_cmp1, w_out, moe_up, moe_down,
            b_up, b_down, w_router, b_router, pT, w_ple, w_gate, ln_f, out):
    ctx = ExitStack()
    with ctx:
        def at(name, shape, dt, off):
            return nc.alloc_sbuf_tensor_at(name, shape, dt, offset=BASE + off)

        def sem(name):
            return ctx.enter_context(nc.semaphore(name))

        PE, SC, VE, GP, SP = [Line(sem("s_" + n)) for n in ("pe", "act", "dve", "pool", "sp")]

        BK = [ctx.enter_context(nc.psum_tensor(f"B{i}", [128, 512], F32)) for i in range(8)]
        free = [()] * 8
        rot = [0]

        def bank(n=4, first=0):
            rot[0] += 1
            return first + rot[0] % n

        def Y(dc):
            return BK[4 + dc // 2][:, 256 * (dc % 2):256 * (dc % 2) + 256]

        used, offset = [0], {}

        def put(name, shape, dt):
            size = 2 if dt == BF16 else 4
            for s in shape[1:]:
                size *= s
            t = at(name, shape, dt, used[0])
            offset[name] = used[0]
            used[0] += (size + 31) // 32 * 32
            return t

        ID = put("ID", [128, 160], F32)
        C = put("C", [128, NC], F32)
        V = put("V", [128, NVEC], F32)
        hT = put("hT", [128, 8, 256], F32)
        identb = put("identb", [128, 128], BF16)
        alibi = put("alibi", [128, 256], BF16)
        slopes = put("slopes", [128, 8, 128], BF16)
        pick = put("pick", [128, 8, 128], BF16)
        maskb = put("maskb", [128, 2, 128], BF16)
        sums = put("sums", [128, 128], F32)
        ones = put("ones", [128, 32], F32)
        cols = put("cols", [128, 2], F32)
        adaT = put("adaT", [128, 2, 48], F32)
        adaC = put("adaC", [128, 16], F32)
        modA = put("modA", [128, 2, 8], F32)
        small = put("small", [128, 4, 8], F32)
        nsink = put("nsink", [128, 16], F32)
        NR, NS = 6, 4
        RAW = put("RAW", [128, NR, 2048], F32)
        SH = put("SH", [128, NS, 1024], F32R)
        SL = put("SL", [128, NS, 1024], F32R)
        B2 = used[0]

        def cst_(n, i=0, w=None):
            a, b = CST1[n] if n in CST1 else CST2[n]
            return C[:, a + i:(b if w is None else a + i + w)]

        def vec_(n, i=0, w=None):
            a, b = VEC[n]
            return V[:, a + i:(b if w is None else a + i + w)]

        ident = ID[:, 0:128]
        sel32 = ID[:, 128:160]
        eps = cols[:, 0:1]

        tasks = []

        def tick():
            for g in list(tasks):
                if next(g, tasks) is tasks:
                    tasks.remove(g)

        def drain():
            while tasks:
                tick()

        loads, place, raw_count, raw_free = [], [], {}, {}
        halves, half_ready, half_free = [], {}, {}
        BUF = [offset["RAW"] + 8 * KB * i for i in range(NR)]
        BUF += [B2 + (55 + 8 * i) * KB for i in range(6)]
        BUF += [offset["SH"], offset["SH"] + 8 * KB, offset["SL"], offset["SL"] + 8 * KB, offset["hT"]]
        slots = {dt: [at(f"{n}{i}", [128, 2048], dt, o) for i, o in enumerate(BUF)] for n, dt in (("R", F32), ("RR", F32R))}
        s_raw = [sem(f"s_raw{i}") for i in range(len(BUF))]
        order = [list(range(NR))]

        def load(*pieces):
            i = len(loads)
            r = order[0].pop(0)
            order[0].append(r)
            place.append(r)
            raw_count[r] = raw_count.get(r, 0) + 16 * len(pieces)
            loads.append((pieces, raw_count[r]))
            return i

        def loaded(i):
            return (s_raw[place[i]], loads[i][1])

        def slot(i, dt=F32):
            return slots[dt][place[i]]

        def cols_slot(w, c0, c1=None, by_rows=False):
            c1 = c0 + 128 if c1 is None else c1
            src = w.rearrange("(k p) n -> p k n", p=128)
            view = lambda s: s.rearrange("p (k n) -> p k n", k=8)
            if c1 == c0 + 128:
                i = load((view, src[:, :, c0:c0 + 256]))
            else:
                i = load((lambda s: view(s)[:, :, 0:128], src[:, :, c0:c0 + 128]),
                         (lambda s: view(s)[:, :, 128:256], src[:, :, c1:c1 + 128]))
            for c in range(2):
                halves.append((i, c, not by_rows))

        def rows_slot(w, r0):
            i = load((lambda s: s.rearrange("p (k n) -> p k n", k=2),
                      w[r0:r0 + 256, :].rearrange("(k p) n -> p k n", p=128)))
            for c in range(2):
                halves.append((i, c, False))

        ada_at = {}

        def ada_slot(layer, n):
            ada_at[layer, n] = load((lambda s: s, ada_w[layer, 128 * (n % 8):128 * (n % 8) + 128,
                                                        2048 * (n // 8):2048 * (n // 8) + 2048]))

        prepared, taken, ahead = [0], [0], [NS]

        def prepare(upto):
            while prepared[0] < min(upto, len(halves)):
                j = prepared[0]
                i, c, strided = halves[j]
                hi, lo = SH[:, j % NS, :], SL[:, j % NS, :]
                if c == "gf":
                    src = slot(i)[:, 0:256]
                    hi, lo = hi[:, 0:256], lo[:, 0:256]
                elif strided:
                    src = slot(i)[:, :].rearrange("p (k n) -> p k n", k=8)[:, :, 128 * c:128 * c + 128]
                    hi, lo = [x.rearrange("p (k n) -> p k n", k=8) for x in (hi, lo)]
                else:
                    src = slot(i)[:, 1024 * c:1024 * c + 1024]
                SC.wait(loaded(i), *half_free.get(j - NS, ()))
                m = SC.mark(act(hi, src, ACT.Copy))
                VE.wait(loaded(i), m, *half_free.get(j - NS, ()))
                n = VE.mark(tt(lo, src, hi.bitcast(F32), ALU.subtract))
                half_ready[j] = (m, n)
                if c != 0:
                    raw_free[i] = (m, n)
                prepared[0] += 1

        def half():
            j = taken[0]
            taken[0] += 1
            prepare(j + ahead[0])
            PE.wait(*half_ready[j])
            return j, (lambda a, n=128: SH[:, j % NS, a:a + n]), (lambda a, n=128: SL[:, j % NS, a:a + n])

        ADA1 = [range(8 * (P // 3) + 3 * (P % 3), min(8 * (P // 3) + 3 * (P % 3) + 3, 8 * (P // 3) + 8))
                for P in range(9)]
        for n in range(8):
            ada_slot(0, n)
        for P in range(4):
            cols_slot(w_qkv, 256 * P)
        cols_slot(w_qkv, 1024)
        cols_slot(w_qkv, 1280, by_rows=True)
        for P in range(4):
            ada_slot(0, 8 + 4 * P)
            ada_slot(0, 9 + 4 * P)
            rows_slot(w_o, 256 * P)
            ada_slot(0, 10 + 4 * P)
            ada_slot(0, 11 + 4 * P)
        first_of_ffn0, at_load = len(loads), {}
        for layer in range(2):
            if layer == 1:
                for P in range(4):
                    for g in range(3):
                        cols_slot(sc_in, 1024 * g + 256 * P)
                    if P:
                        rows_slot(sc_out, 256 * (P - 1))
                rows_slot(sc_out, 768)
            for P in range(11):
                cols_slot(w_up[layer], 256 * P)
                cols_slot(w_up[layer], 2816 + 256 * P)
                if P:
                    rows_slot(w_down[layer], 256 * (P - 1))
                if layer == 0 and P < 9:
                    for n in ADA1[P]:
                        ada_slot(1, n)
            rows_slot(w_down[layer], 2560)
        cols_slot(w_in, 512)
        w1_at = [load((lambda s: s.rearrange("p (i n) -> p i n", i=16), w_cmp1[i].rearrange("(i p) n -> p i n", p=128)))
                 for i in range(2)]
        cols_slot(w_in, 768, 1024)
        cols_slot(w_in, 896, 1152, by_rows=True)
        v = w_in.rearrange("(k p) n -> p k n", p=128)
        halves.append((load((lambda s: s[:, 0:256].rearrange("p (k n) -> p k n", k=8)[:, :, 0:24], v[:, :, 1280:1304]),
                            (lambda s: s[:, 0:256].rearrange("p (k n) -> p k n", k=8)[:, :, 24:32], v[:, :, 2840:2848])),
                       "gf", False))
        cols_slot(w_in, 0)
        cols_slot(w_in, 256)
        for c in (1816, 2072):
            cols_slot(w_in, c)
        for c in (2328, 2584):
            cols_slot(w_in, c, by_rows=True)
        for c in (1304, 1560):
            cols_slot(w_in, c)
        for P in range(4):
            rows_slot(w_out, 256 * P)

        NE = 32
        order[0] = order[0] + list(range(NR, len(BUF)))
        bias_at = load(*[(lambda s, r=r: s[r:r + 32, :], b_up) for r in (0, 64, 96)])
        up_at, down_at = {}, {}
        two = lambda s: s.rearrange("p (k n) -> p k n", k=2)
        for e in range(NE):
            for k in range(8):
                if e == NE - 1 and k == 5:
                    wple_at = load((two, w_ple.rearrange("(k p) n -> p k n", p=128)))
                    pt_at = load((lambda s: s[:, 0:512].rearrange("p (k n) -> p k n", k=2), pT))
                up_at[e, k] = load((lambda s: s, moe_up[e, 128 * k:128 * k + 128, :]))
            for k in range(4):
                down_at[e, k] = load((two, moe_down[e, 256 * k:256 * k + 256, :].rearrange("(k p) n -> p k n", p=128)))
        gate_at = [load((two, w_gate[256 * k:256 * k + 256, :].rearrange("(k p) n -> p k n", p=128))) for k in range(4)]

        tmp, tmc = [at(n, [128, 8, 256], F32, B2 + i * 8 * KB) for i, n in enumerate(("tmp", "tmc"))]
        AH = at("AH", [128, 8, 512], F32R, B2 + 16 * KB)
        AL = at("AL", [128, 8, 512], F32R, B2 + 32 * KB)
        sq = at("sq", [128, 8, 512], F32, B2 + 48 * KB)
        part, vp, yy, zz, rr, adaS = [at(n, [128, 512], F32, B2 + (64 + 2 * i) * KB)
                                      for i, n in enumerate(("part", "vp", "yy", "zz", "rr", "adaS"))]

        s_in = [sem(f"s_in{i}") for i in range(4)]
        in_v, in_x, in_ctx, in_c = [(s, 16) for s in s_in]
        in_c = (s_in[3], 32)
        SP.do(lambda e: e.dma_start(V[:, :], vec).then_inc(s_in[0], 16))
        SP.do(lambda e: e.dma_start(hT[:, :, :], xT).then_inc(s_in[1], 16))
        SP.do(lambda e: e.dma_start(tmc[:, :, :], ctxT).then_inc(s_in[2], 16))
        SP.do(lambda e: e.dma_start(C[:, 0:N1], cst1).then_inc(s_in[3], 16))
        SP.do(lambda e: e.dma_start(ID[:, :], cid).then_inc(s_in[3], 16))

        m_ones = VE.mark(fill(ones[:, :], 1.0))
        VE.do(fill(cols[:, 0:1], EPS))
        m_half = VE.mark(fill(cols[:, 1:2], -0.5))
        m_sums = VE.mark(fill(sums[:, :], 1.0 / 32768.0))
        SC.wait(in_v, m_sums)
        m_cc = SC.mark(act(vec_("cc"), vec_("cc"), ACT.Silu))
        LN_EXP = "natural_log_exp_and_others"
        SC.do(lambda e: e.preload_act_table_set(LN_EXP))
        VE.wait(in_c, in_v)
        VE.do(ts(nsink[:, :], vec_("sink"), -1.0, ALU.mult))
        VE.do(cp(identb[:, :], ident))
        VE.do(cp(maskb[:, 0, :], cst_("m01")))
        m_maskb = VE.mark(cp(maskb[:, 1, :], cst_("m10")))

        def ada_burst(layer, slots, b):
            PE.wait(*free[b])
            for n in slots:
                i = ada_at[layer, n]
                PE.wait(loaded(i), m_cc)
                for j in range(4):
                    f = mm(BK[b][32 * j:32 * j + 32, :], V[:, 32 * (n % 8):32 * (n % 8) + 32],
                           slot(i)[:, 512 * j:512 * j + 512], n == slots[0], n == slots[-1])
                    if j < 3:
                        PE.do(f)
                    else:
                        raw_free[i] = (PE.mark(f),)
            VE.wait(*raw_free[i])
            if slots[0] % 8 == 0:
                m = VE.mark(cp(adaS[:, :], BK[b][:, :]))
            else:
                VE.wait((VE.sem, VE.count))
                m = VE.mark(tt(adaS[:, :], BK[b][:, :], adaS[:, :], ALU.add))
            free[b] = (m,)
            return m

        def ada_end(layer, g, m, b):
            PE.wait(m, in_c, *free[b])
            for q in range(4):
                f = tp(BK[b][:, 128 * q:128 * q + 128], adaS[:, 128 * q:128 * q + 128], ident)
                if q < 3:
                    PE.do(f)
                else:
                    m = PE.mark(f)
            VE.wait(m, in_v)
            dst = adaT[:, layer, 16 * g:16 * g + 16].rearrange("p (j b) -> p j b", b=4)
            bias = vec_(f"ada_b{layer}", 16 * g, 16).rearrange("p (j b) -> p j b", b=4)
            src = BK[b][:, :].rearrange("p (b j r) -> p r j b", b=4, r=32)
            m = VE.mark(tt(dst, src[:, 0], bias, ALU.add))
            if layer == 0 and g == 0:
                m = VE.mark(tt(adaC[:, :].rearrange("p (j b) -> p j b", b=4), src[:, 1], bias, ALU.add))
            free[b] = (m,)
            return m

        def ada_col(layer, i, k):
            return adaT[:, layer, 8 * i + k:8 * i + k + 1]

        def newton(ms, m, n, b, scale=1.0):
            SC.wait(m)
            a = SC.mark(act(yy[:, 0:n], ms, ACT.Ln, bias=eps))
            VE.wait(a)
            v = VE.mark(ts(vp[:, 0:n], ms, EPS, ALU.add))
            free[b] = (v,)
            SC.wait(a)
            a = SC.mark(act(yy[:, 0:n], yy[:, 0:n], ACT.Exp, scale=-0.5))
            VE.wait(a)
            z = VE.mark(tt(zz[:, 0:n], yy[:, 0:n], yy[:, 0:n], ALU.mult))
            VE.wait(z)
            z = VE.mark(tt(zz[:, 0:n], zz[:, 0:n], vp[:, 0:n], ALU.mult))
            VE.wait(z)
            z = VE.mark(ts(zz[:, 0:n], zz[:, 0:n], -0.5 * scale, ALU.mult, 1.5 * scale, ALU.add))
            VE.wait(z)
            return VE.mark(tt(rr[:, 0:n], yy[:, 0:n], zz[:, 0:n], ALU.mult))

        def rstd(src, ready, n, b0, b1):
            A, B = BK[b0], BK[b1]
            PE.wait(m_ones, m_sums, *free[b0])
            for k in range(8):
                SC.wait(*ready[k])
                for i, x in enumerate(src(k)):
                    m = SC.mark(act(sq[:, k, 256 * i:256 * i + 256], x, ACT.Square))
                PE.wait(m)
                f = mm(A[32 * (k % 4):32 * (k % 4) + 32, 0:n], ones[:, :], sq[:, k, 0:n], k < 4, k >= 4)
                if k < 7:
                    PE.do(f)
                else:
                    m = PE.mark(f)
            VE.wait(m)
            m = VE.mark(cp(part[:, 0:n], A[:, 0:n]))
            free[b0] = (m,)
            PE.wait(m, *free[b1])
            m = PE.mark(mm(B[:, 0:n], sums[:, :], part[:, 0:n], True, True))
            return newton(B[:, 0:n], m, n, b1)

        a_ready = [[()] * 8, [()] * 8]
        a_free = [()]

        def scaled(src, t, k, n, o, *marks):
            VE.wait(*marks)
            return VE.mark(tt(t(k), src(k), rr[:, o:o + n], ALU.mult))

        def modulate(t, u, mt, n, o, A, Bv, *marks):
            m = [mt(0), mt(1)]
            SC.wait(*marks, *a_free[0])
            VE.wait(*marks, *a_free[0])
            for k in range(8):
                SC.wait(m[k])
                if Bv is None:
                    h = SC.mark(act(AH[:, k, o:o + n], t(k), ACT.Copy, scale=A(k)))
                else:
                    h = SC.mark(act(AH[:, k, o:o + n], t(k), ACT.Identity, scale=A(k), bias=Bv(k)))
                if k < 6:
                    m.append(mt(k + 2))
                VE.wait(m[k])
                if Bv is None:
                    x = VE.mark(ts(u(k), t(k), A(k), ALU.mult))
                else:
                    x = VE.mark(ts(u(k), t(k), A(k), ALU.mult, Bv(k), ALU.add))
                VE.wait(h, x)
                l = VE.mark(tt(AL[:, k, o:o + n], u(k), AH[:, k, o:o + n].bitcast(F32), ALU.subtract))
                a_ready[o // 256][k] = (h, l)

        def mm3(out, wh, wl, xh, xl, start, stop, skip=False):
            PE.do(mm(out, wh, xh, start, False, skip))
            PE.do(mm(out, wh, xl, False, False, skip))
            return mm(out, wl, xh, False, stop, skip)

        def project(out, moving=((0, 0),)):
            j, wh, wl = half()
            for a, o in moving:
                for k in range(8):
                    PE.wait(*a_ready[o // 256][k])
                    f = mm3(out[:, a:a + 256], wh(128 * k), wl(128 * k), AH[:, k, o:o + 256], AL[:, k, o:o + 256],
                            k == 0, k == 7)
                    if k < 7:
                        PE.do(f)
                    else:
                        m = PE.mark(f)
            half_free[j] = (m,)
            return m

        y_marks = [None] * 4

        def contract(xh, xl, ready, first, last, parts=4):
            j, wh, wl = half()
            PE.wait(*ready)
            for dc in range(8):
                if first and dc % 2 == 0:
                    PE.wait(*free[4 + dc // 2])
                f = mm3(Y(dc), wh(128 * dc), wl(128 * dc), xh, xl, first and dc % 2 == 0, last, True)
                if dc == 7 or (last and dc % 2):
                    y_marks[dc // 2] = PE.mark(f)
                else:
                    PE.do(f)
                if dc == 7:
                    half_free[j] = (y_marks[3],)
                    yield half_free[j]
                elif dc % (8 // parts) == 8 // parts - 1:
                    yield ()

        h_ready = [()] * 8

        def residual(layer, i):
            for dc in range(8):
                VE.wait(y_marks[dc // 2])
                m = VE.mark(stt(hT[:, dc, :], Y(dc), ada_col(layer, i, dc), hT[:, dc, :], ALU.mult, ALU.add))
                h_ready[dc] = (m,)
                if dc % 2:
                    free[4 + dc // 2] = (m,)

        def norm_mod(layer, i, gain):
            VE.wait((VE.sem, VE.count))
            m = VE.mark(stt(modA[:, 0, :], adaT[:, layer, 8 * i + 8:8 * i + 16], 1.0, gain, ALU.add, ALU.mult))
            m_rr = rstd(lambda k: (hT[:, k, :],), h_ready, 256, bank(), bank())
            t = lambda k: tmp[:, k, :]
            modulate(t, lambda k: sq[:, k, 0:256], lambda k: scaled(lambda q: hT[:, q, :], t, k, 256, 0, m_rr), 256, 0,
                     lambda k: modA[:, 0, k:k + 1], lambda k: ada_col(layer, i, k), m)

        m_rr = rstd(lambda k: (hT[:, k, :], tmc[:, k, :]), [(in_x, in_ctx)] * 8, 512, 4, 5)
        hk, xk, ck = [lambda k, t=t: t[:, k, :] for t in (hT, tmp, tmc)]
        mx = [scaled(hk, xk, k, 256, 0, in_x, m_rr) for k in range(8)]
        mc = [scaled(ck, ck, k, 256, 256, m_rr) for k in range(8)]
        m = ada_burst(0, range(8), 0)
        m_ada = ada_end(0, 0, m, 1)
        VE.wait(m_ada)
        VE.do(stt(modA[:, 0, :], adaT[:, 0, 8:16], 1.0, vec_("nm0"), ALU.add, ALU.mult))
        m_ab = VE.mark(stt(modA[:, 1, :], adaC[:, 8:16], 1.0, vec_("nm0"), ALU.add, ALU.mult))
        prepare(1)
        modulate(xk, lambda k: sq[:, k, 0:256], lambda k: mx[k], 256, 0,
                 lambda k: modA[:, 0, k:k + 1], lambda k: ada_col(0, 0, k), m_ab)

        KH = at("KH", [128, 4, 512], F32R, B2)
        KL = at("KL", [128, 4, 512], F32R, B2 + 8 * KB)
        QS = at("QS", [128, 16, 256], F32R, B2 + 48 * KB)
        sets = [[at(f"{n}{j}", [128, 512], F32, B2 + (76 + 2 * i + 8 * j) * KB)
                 for i, n in enumerate(("qq", "m1", "qr", "qw"))] for j in range(2)]
        VR = at("VR", [128, 4, 256], F32, B2 + 92 * KB)
        set_free, set_n = [(), ()], [0]

        def rows_of(hh):
            return slice(64 * hh, 64 * hh + 64)

        def pieces(x, n):
            return x.rearrange("p (a n) -> p a n", a=n)

        def heads(b, m, wcol, roped, then, stat=None):
            i = set_n[0] % 2
            set_n[0] += 1
            qq, m1, qr, w = sets[i]
            n = 256 * roped
            SC.wait(m, *set_free[i])
            s1 = SC.mark(act(qq[:, :], BK[b][:, :], ACT.Square))
            s2 = SC.mark(act(w[:, :], BK[b][:, :], ACT.Copy, scale=wcol))
            free[b] = (s2,)
            GP.wait(s2, in_c, *set_free[i])
            g = GP.mark(tt(pieces(m1[:, 0:n], roped), pieces(w[:, 0:n], roped),
                           cst_("cos").unsqueeze(1).to_broadcast([128, roped, 256]), ALU.mult))
            yield
            b2 = bank(4)
            PE.wait(s2, in_c, *free[b2])
            p2 = PE.mark(mm(BK[b2][:, 0:n], cst_("perm"), w[:, 0:n], True, True))
            if stat is None:
                b1 = bank(4)
                PE.wait(s1, *free[b1])
                p1 = PE.mark(mm(BK[b1][:, :], cst_("blk"), qq[:, :], True, True))
            else:
                stat(s1, qq)
            yield
            if stat is None:
                mr = newton(BK[b1][:, :], p1, 512, b1)
            VE.wait(p2, *set_free[i])
            x = VE.mark(tt(pieces(qr[:, 0:n], roped), pieces(BK[b2][:, 0:n], roped),
                           cst_("sin").unsqueeze(1).to_broadcast([128, roped, 256]), ALU.mult))
            free[b2] = (x,)
            VE.wait(x, g)
            x = VE.mark(tt(qr[:, 0:n], qr[:, 0:n], m1[:, 0:n], ALU.add))
            if stat is None:
                VE.wait(x, mr)
                x = VE.mark(tt(qr[:, 0:n], qr[:, 0:n], rr[:, 0:n], ALU.mult))
                if n < 512:
                    x = VE.mark(tt(qr[:, n:512], w[:, n:512], rr[:, n:512], ALU.mult))
            set_free[i] = then(x, qr)

        qs_ready, k_ready, sq_done = [], [], []
        sb = 4

        def q_stat(P):
            def f(m, qq):
                PE.wait(m, in_c)
                if P == 0:
                    PE.wait(*free[sb])
                for c in range(2):
                    ch = 2 * P + c
                    p = 32 * (ch % 4)
                    o = 256 * (ch // 4)
                    x = PE.mark(mm(BK[sb][p:p + 32, o:o + 256], cst_("hd"), qq[:, 256 * c:256 * c + 256], True, True))
                sq_done.append(x)
            return f

        def q_then(P):
            def f(x, qr):
                SC.wait(x)
                VE.wait(x)
                for i in range(4):
                    r0, r1 = rows_of(i % 2), rows_of(1 - i % 2)
                    src = qr[r0, 256 * (i // 2):256 * (i // 2) + 256]
                    a = SC.mark(act(QS[r0, 4 * P + i, :], src, ACT.Copy))
                    VE.wait(a)
                    v = VE.mark(tt(QS[r1, 4 * P + i, :], src, QS[r0, 4 * P + i, :].bitcast(F32), ALU.subtract))
                    qs_ready.append((a, v))
                return (a, v, sq_done[P])
            return f

        def k_then(c):
            def f(x, qr):
                SC.wait(x)
                VE.wait(x)
                for hh in range(2):
                    r0, r1 = rows_of(hh), rows_of(1 - hh)
                    g = 2 * c + hh
                    a = SC.mark(act(KH[r0, g, :], qr[r0, :], ACT.Copy))
                    a2 = SC.mark(act(KH[r1, g, :], qr[r0, :], ACT.Copy))
                    VE.wait(a)
                    VE.do(tt(KL[r0, g, :], qr[r0, :], KH[r0, g, :].bitcast(F32), ALU.subtract))
                    v = VE.mark(tt(KL[r1, g, :], qr[r0, :], KH[r0, g, :].bitcast(F32), ALU.subtract))
                k_ready.extend([(a2, v)] * 2)
                return (a2, v)
            return f

        rq, rv, rz = [at(n, [128, 32], F32, B2 + 96 * KB + 128 * i) for i, n in enumerate(("rq", "rv", "rz"))]
        m_rq = []

        def query_scales():
            VE.wait(*sq_done)
            m = VE.mark(cp(part[:, :], BK[sb][:, :]))
            free[sb] = (m,)
            yield
            PE.wait(m, *free[5])
            for i in range(4):
                m = PE.mark(tp(BK[5][:, 128 * i:128 * i + 128], part[:, 128 * i:128 * i + 128], ident))
            VE.wait(m)
            x = VE.mark(ts(rv[:, :].rearrange("p (i j r) -> p i j r", i=4, j=4),
                           BK[5][:, :].rearrange("p (i j r) -> p i j r", i=4, j=4)[:, :, :, 0:2], EPS, ALU.add))
            free[5] = (x,)
            SC.wait(x)
            a = SC.mark(act(rq[:, :], rv[:, :], ACT.Ln))
            SC.wait(a)
            a = SC.mark(act(rq[:, :], rq[:, :], ACT.Exp, scale=-0.5))
            yield
            VE.wait(a)
            x = VE.mark(tt(rz[:, :], rq[:, :], rq[:, :], ALU.mult))
            VE.wait(x)
            x = VE.mark(tt(rz[:, :], rz[:, :], rv[:, :], ALU.mult))
            VE.wait(x)
            x = VE.mark(ts(rz[:, :], rz[:, :], -0.0625, ALU.mult, 0.1875, ALU.add))
            VE.wait(x)
            x = VE.mark(tt(rq[:, :], rq[:, :], rz[:, :], ALU.mult))
            VE.wait(x)
            m_rq.append(VE.mark(ts(rv[:, :], rq[:, :], -1.0, ALU.mult)))

        for P in range(4):
            b = bank(4)
            PE.wait(*free[b])
            for c in range(2):
                m = project(BK[b][:, 256 * c:256 * c + 256])
                if P == 0 and c == 0:
                    modulate(ck, lambda k: sq[:, k, 256:512], lambda k: mc[k], 256, 256,
                             lambda k: modA[:, 1, k:k + 1], lambda k: adaC[:, k:k + 1])
                tick()
            tasks.append(heads(b, m, vec_("qn"), 2, q_then(P), q_stat(P)))
            tick()
        for c in range(2):
            b = bank(4)
            PE.wait(*free[b])
            m = project(BK[b], ((0, 0), (256, 256)))
            tick()
            tasks.append(heads(b, m, vec_("kn"), 1, k_then(c)))
            if c == 0:
                tick()
                tasks.append(query_scales())
        m_v = []

        def project_values():
            vb = (6, 7)
            for t in range(2):
                j, wh, wl = half()
                for q in range(4):
                    b = vb[q // 2]
                    if t == 0:
                        PE.wait(*free[b])
                    for kk in range(4):
                        k = 4 * t + kk
                        o = 128 * q
                        PE.wait(*a_ready[q // 2][k])
                        f = mm3(BK[b][:, 256 * (q % 2):256 * (q % 2) + 256], AH[:, k, o:o + 128], AL[:, k, o:o + 128],
                                wh(256 * kk, 256), wl(256 * kk, 256), k == 0 and q % 2 == 0, k == 7, True)
                        if kk < 3 or q < 3:
                            PE.do(f)
                        else:
                            m = PE.mark(f)
                    if q == 3:
                        half_free[j] = (m,)
                    yield
            SC.wait(m)
            for i in range(2):
                x = SC.mark(act(VR[:, 2 * i:2 * i + 2, :], BK[vb[i]][:, :].rearrange("p (a n) -> p a n", a=2), ACT.Copy))
                free[vb[i]] = (x,)
            m_v.extend([m, x])
            yield

        def rcol(t, h, qt):
            i = 16 * (h // 8) + 8 * qt + h % 8
            return t[:, i:i + 1]

        NP = 4
        PR = at("PR", [128, NP, 512], F32, B2 + 76 * KB)
        JK = at("JK", [128, 4, 512], BF16, B2 + 84 * KB)
        PT = at("PT", [128, 4, 4, 256], F32, B2 + 16 * KB)
        OH = at("OH", [128, 2, 256], F32R, B2 + 32 * KB)
        OL = at("OL", [128, 2, 256], F32R, B2 + 34 * KB)
        OT = at("OT", [128, 2, 256], F32, B2 + 36 * KB)
        RB = at("RB", [128, 2, 256], F32, B2 + 38 * KB)
        RD = at("RD", [128, 2, 16], F32, B2 + 96 * KB + 512)
        RX = at("RX", [128, 2, 2, 128], F32, B2 + 88 * KB)
        jk, rb_ready = [], {}
        pr_free, pt_free, o_free, pt_ready, rd_ready = {}, {}, {}, {}, {}
        no_sets = set_free

        def attend(h):
            g = h // 4
            nm, su, es = [small[:, h % 4, 2 * i:2 * i + 2] for i in range(3)]
            y = []
            for qt in range(2):
                b = qt
                PE.wait(*qs_ready[h], *k_ready[g], *free[b], m_maskb)
                q = QS[:, h, 128 * qt:128 * qt + 128]
                PE.do(mm(BK[b][:, :], q, KH[:, g, :], True, False, True))
                PE.do(mm(BK[b][:, :], q, KL[:, g, :], False, False, True))
                o = 128 if qt == 0 else 0
                m = PE.mark(mm(BK[b][:, o:o + 128], identb[:, :], maskb[:, qt, :], False, True, True))
                VE.wait(m, *m_rq, *jk[-4:-3])
                x = VE.mark(ts(JK[:, len(jk) % 4, :], BK[b][:, :], rcol(rv, h, qt), ALU.mult, nsink[:, h:h + 1], ALU.min,
                               accum_out=nm[:, qt:qt + 1]))
                jk.append(x)
                SC.wait(x, *no_sets[0], *no_sets[1], *pr_free.get((h - 2, qt), ()))
                y.append(SC.mark(act(PR[:, (2 * h + qt) % NP, :], BK[b][:, :], ACT.Exp, scale=rcol(rq, h, qt),
                                     bias=nm[:, qt:qt + 1], accum_out=su[:, qt:qt + 1])))
                free[b] = (y[qt],)
                yield
            s = SC.mark(act(es, nm, ACT.Exp, bias=vec_("sink", h, 1)))
            for qt in range(2):
                PE.wait(y[qt], *free[2])
                for t in range(4):
                    f = tp(BK[2][:, 128 * t:128 * t + 128], PR[:, (2 * h + qt) % NP, 128 * t:128 * t + 128], ident)
                    if t < 3:
                        PE.do(f)
                    else:
                        m = PE.mark(f)
                pr_free[h, qt] = (m,)
                L = VE if qt else SC
                L.wait(m, m_v[0], *pt_free.get(h - 4, ()))
                dst = PT[:, h % 4, :, 128 * qt:128 * qt + 128]
                src = BK[2][:, :].rearrange("p (t n) -> p t n", t=4)
                x = L.mark(cp(dst, src) if qt else act(dst, src, ACT.Copy))
                free[2] = (x,)
                pt_ready[h] = pt_ready.get(h, ()) + (x,)
                if qt == 0:
                    VE.wait(s)
                    x = VE.mark(tt(su, su, es, ALU.add))
                    VE.wait(x)
                    rd_ready[h] = VE.mark(recip(RD[:, :, h], su))
                    if h % 2:
                        GP.wait(rd_ready[h], *no_sets[0], *no_sets[1], *pt_free.get(h - 4, ()))
                        rb_ready[h] = GP.mark(cp(RX[:, h // 2 % 2, :, :].rearrange("p q (a n) -> p q a n", a=2),
                                                 RD[:, :, h - 1:h + 1].unsqueeze(3).to_broadcast([128, 2, 2, 64])))
                yield
            if h % 2:
                c = h // 2
                PE.wait(*free[3], rb_ready[h])
                for qt in range(2):
                    PE.do(tp(BK[3][:, 256 + 128 * qt:384 + 128 * qt], RX[:, c % 2, qt, :], ident))
                PE.wait(*pt_ready[h - 1], *pt_ready[h], m_v[1])
                for t in range(4):
                    for hh in range(2):
                        f = mm(BK[3][rows_of(hh), 0:256], VR[:, t, 64 * g:64 * g + 64], PT[:, (2 * c + hh) % 4, t, :],
                               t == 0, t == 3)
                        if t < 3 or hh == 0:
                            PE.do(f)
                        else:
                            m = PE.mark(f)
                pt_free[h - 1] = pt_free[h] = (m,)
                SC.wait(m, *o_free.get(c - 2, ()))
                a = SC.mark(act(RB[:, c % 2, :], BK[3][:, 256:512], ACT.Copy))
                VE.wait(a)
                x = VE.mark(tt(OT[:, c % 2, :], BK[3][:, 0:256], RB[:, c % 2, :], ALU.mult))
                free[3] = (x,)
                yield
                SC.wait(x)
                a = SC.mark(act(OH[:, c % 2, :], OT[:, c % 2, :], ACT.Copy))
                VE.wait(a)
                v = VE.mark(tt(OL[:, c % 2, :], OT[:, c % 2, :], OH[:, c % 2, :].bitcast(F32), ALU.subtract))
                yield
                for m in contract(OH[:, c % 2, :], OL[:, c % 2, :], (a, v), c == 0, c == 7):
                    o_free[c] = m
                    yield

        def adaln_rest():
            for n in range(8, 24, 2):
                yield
                yield
                yield
                m = ada_burst(0, range(n, n + 2), 3)
                if n % 8 == 6:
                    x = ada_end(0, n // 8, m, 3)
                    m_adas.append(x)
                yield

        m_adas = []
        ahead[0] = 2
        pv = project_values()
        next(pv)
        next(pv)
        for _ in range(7):
            tick()
            next(pv)
        tasks.append(adaln_rest())
        for h in range(16):
            tasks.append(attend(h))
            tick()
            tick()
        drain()
        VE.wait(*m_adas)
        ahead[0] = NS
        a_free[0] = o_free[7]
        residual(0, 2)

        AH = at("AH2", [128, 8, 256], F32R, B2 + 8 * KB)
        AL = at("AL2", [128, 8, 256], F32R, B2 + 16 * KB)
        sq = at("sq2", [128, 8, 256], F32, B2 + 24 * KB)
        part, vp, yy, zz, rr = [at(n + "2", [128, 512], F32, B2 + (32 + 2 * i) * KB)
                                for i, n in enumerate(("part", "vp", "yy", "zz", "rr"))]
        adaS = at("adaS2", [128, 512], F32, B2 + 42 * KB)
        ct = at("ct", [128, 2, 4, 256], F32, B2 + 44 * KB)
        mid = at("mid", [128, 2, 512], F32, B2 + 52 * KB)
        MH = at("MH", [128, 2, 512], F32R, B2 + 56 * KB)
        ML = at("ML", [128, 2, 512], F32R, B2 + 60 * KB)
        m_free, ct_free = [(), ()], [(), ()]
        fork = [(PE.sem, PE.count), (SC.sem, SC.count), (VE.sem, VE.count), (GP.sem, GP.count)]
        for L in (PE, SC, VE, GP):
            L.wait(*fork)
        s_c2 = sem("s_c2")
        at_load[first_of_ffn0 + 2] = [(fork, C[:, 0:N2], cst2, s_c2)]
        in_c2 = (s_c2, 16)
        onesb = at("onesb", [128, 128], BF16, B2 + 76 * KB)
        m = GP.mark(fill(onesb[:, :], 1.0))
        GP.wait(in_c2, m_maskb, m)
        for h in range(8):
            GP.do(ts(slopes[:, h, :], identb[:, :], 2.0 ** -(h + 1), ALU.mult))
            GP.do(ts(pick[:, h, :], onesb[:, :], cst_("pick", h, 1), ALU.mult))
        m_tabs = GP.mark(cp(alibi[:, :], cst_("alibi")))

        def conv_taps(dst, src, w, ready):
            VE.wait(*ready)
            x = VE.mark(stt(dst[:, 1:256], src[:, 0:255], w(0), dst[:, 1:256], ALU.mult, ALU.add))
            VE.wait(x)
            return VE.mark(stt(dst[:, 0:255], src[:, 1:256], w(2), dst[:, 0:255], ALU.mult, ALU.add))

        def split_mid(s, x):
            SC.wait(x, *m_free[s])
            a = SC.mark(act(MH[:, s, :], mid[:, s, :], ACT.Copy))
            VE.wait(a)
            v = VE.mark(tt(ML[:, s, :], mid[:, s, :], MH[:, s, :].bitcast(F32), ALU.subtract))
            return (a, v)

        def down(s, ready, first, last):
            for c in range(2):
                for m in contract(MH[:, s, 256 * c:256 * c + 256], ML[:, s, 256 * c:256 * c + 256], ready,
                                  first and c == 0, last and c == 1):
                    if m:
                        m_free[s] = m

        def ffn(layer):
            def tap(chunk):
                return lambda i: vec_(f"conv{layer}", 44 * i + chunk, 1)

            before = None
            for P in range(11):
                s = P % 2
                conv = []
                for half_u in range(2):
                    b = 2 * s + half_u
                    PE.wait(*free[b])
                    for c in range(2):
                        m = project(BK[b][:, 256 * c:256 * c + 256])
                    SC.wait(m, *ct_free[s])
                    for c in range(2):
                        w = tap(22 * half_u + 2 * P + c)
                        a = SC.mark(act(ct[:, s, 2 * half_u + c, :], BK[b][:, 256 * c:256 * c + 256], ACT.Copy,
                                        scale=w(1)))
                    for c in range(2):
                        w = tap(22 * half_u + 2 * P + c)
                        x = conv_taps(ct[:, s, 2 * half_u + c, :], BK[b][:, 256 * c:256 * c + 256], w, (a,))
                    free[b] = (x,)
                    conv.append(x)
                g = ct[:, s, 0:2, :].rearrange("p a n -> p (a n)")
                u = ct[:, s, 2:4, :].rearrange("p a n -> p (a n)")
                SC.wait(conv[0])
                a = SC.mark(act(g, g, ACT.Silu))
                VE.wait(a, conv[1], *m_free[s])
                x = VE.mark(tt(mid[:, s, :], g, u, ALU.mult))
                ct_free[s] = (x,)
                now = split_mid(s, x)
                if before:
                    down(1 - s, before, P == 1, False)
                if layer == 0 and P < 9:
                    b = 2 * (1 - s) + 1
                    m = ada_burst(1, ADA1[P], b)
                    if P % 3 == 2:
                        ada_end(1, P // 3, m, b)
                before = now
            down(0, before, False, True)

        def ffn_layer(layer):
            SC.do(lambda e: e.preload_act_table_set(LN_EXP))
            norm_mod(layer, 3, vec_(f"nf{layer}"))
            ffn(layer)
            a_free[0] = ((PE.sem, PE.count),)
            residual(layer, 5)

        ffn_layer(0)

        norm_mod(1, 0, vec_("nm1"))
        gc = at("gc", [128, 2, 512], F32, B2 + 64 * KB)
        cu = at("cu", [128, 2, 512], F32, B2 + 68 * KB)
        before = None
        for P in range(4):
            s = P % 2
            bs, ms = [], []
            for g in range(3):
                b = bank()
                bs.append(b)
                PE.wait(*free[b])
                for c in range(2):
                    m = project(BK[b][:, 256 * c:256 * c + 256])
                ms.append(m)
                if g == 1:
                    SC.wait(m, *ct_free[s])
                    a = SC.mark(act(gc[:, s, :], BK[b][:, :], ACT.Copy))
                    free[b] = (a,)
            VE.wait(a, ms[2], *ct_free[s])
            x = VE.mark(tt(cu[:, s, :], BK[bs[2]][:, :], gc[:, s, :], ALU.mult))
            free[bs[2]] = (x,)
            SC.wait(x)
            w = [lambda i, c=c: vec_("scconv", 8 * i + 2 * P + c, 1) for c in range(2)]
            for c in range(2):
                a = SC.mark(act(ct[:, s, c, :], cu[:, s, 256 * c:256 * c + 256], ACT.Copy, scale=w[c](1)))
            for c in range(2):
                x = conv_taps(ct[:, s, c, :], cu[:, s, 256 * c:256 * c + 256], w[c], (a,))
            VE.wait(x, ms[0], *m_free[s])
            x = VE.mark(tt(mid[:, s, :], BK[bs[0]][:, :], ct[:, s, 0:2, :].rearrange("p a n -> p (a n)"), ALU.mult))
            free[bs[0]] = (x,)
            ct_free[s] = (x,)
            now = split_mid(s, x)
            if before:
                down(1 - s, before, P == 1, False)
            before = now
        down(1, before, False, True)
        a_free[0] = ((PE.sem, PE.count),)
        residual(1, 2)
        ffn_layer(1)

        SC.do(lambda e: e.preload_act_table_set(LN_EXP))
        m_rr = rstd(lambda k: (hT[:, k, :],), h_ready, 256, bank(), bank())
        tk = lambda k: tmp[:, k, :]
        modulate(tk, lambda k: sq[:, k, 0:256], lambda k: scaled(lambda q: hT[:, q, :], tk, k, 256, 0, m_rr), 256, 0,
                 lambda k: vec_("ln1", k, 1), None)

        OT2 = at("OT2", [128, 8, 256], F32, B2)
        QF = at("QF", [128, 8, 256], F32R, B2 + 24 * KB)
        QN = at("QN", [128, 8, 256], F32R, B2 + 44 * KB)
        KNH = at("KNH", [128, 2, 512], F32R, B2 + 52 * KB)
        KNL = at("KNL", [128, 2, 512], F32R, B2 + 56 * KB)
        VN = at("VN", [128, 2, 256], F32, B2 + 60 * KB)
        ZT = at("ZT", [128, 2, 16, 2, 16], F32, B2 + 62 * KB)
        KFH = at("KFH", [128, 8, 256], F32R, B2 + 66 * KB)
        KFL = at("KFL", [128, 8, 256], F32R, B2 + 74 * KB)
        VF = at("VF", [128, 2, 512], F32, B2 + 82 * KB)
        PU = at("PU", [128, 4, 512], F32, B2 + 86 * KB)
        PV = at("PV", [128, 2, 768], F32, B2 + 94 * KB)
        o = B2 + 100 * KB
        PC = at("PC", [128, 16, 16], F32, o)
        PL = at("PL", [128, 16, 16], F32, o + KB)
        PCT = at("PCT", [128, 256], F32, o + 2 * KB)
        VCX = at("VCX", [128, 8, 64], F32, B2 + 41 * KB)
        CTB = at("CTB", [128, 256], BF16, B2 + 40 * KB + 512)
        C1 = at("C1", [128, 256], F32, B2 + 32 * KB)
        GG = at("GG", [128, 2, 2, 16], F32, B2 + 33 * KB)
        G2 = at("G2", [128, 2, 2, 16], F32, B2 + 33 * KB + 256)
        GV = at("GV", [128, 8, 16], F32, B2 + 33 * KB + 512)
        KC = at("KC", [128, 2, 2, 16], F32R, B2 + 34 * KB)
        GF = at("GF", [32, 256], F32, B2 + 35 * KB)
        gt = at("gt", [128, 2, 32], F32, B2 + 36 * KB)
        ga = at("ga", [128, 2, 24], F32, B2 + 36 * KB + 256)
        fa = at("fa", [128, 2, 8], F32, B2 + 36 * KB + 512)
        fb = at("fb", [128, 2, 8], F32, B2 + 36 * KB + 576)
        fc = at("fc", [128, 2, 8], F32, B2 + 36 * KB + 640)
        st = at("st", [128, 8, 8], F32, B2 + 36 * KB + 704)
        cs = at("cs", [128, 4, 16], F32, B2 + 37 * KB)
        cr = at("cr", [128, 2, 256], F32, B2 + 38 * KB)

        fork = [(PE.sem, PE.count), (SC.sem, SC.count), (VE.sem, VE.count)]

        def stack(dst_h, dst_l, src, hh, scale, both):
            r0, r1 = rows_of(hh), rows_of(1 - hh)
            a = SC.mark(act(dst_h[r0], src[r0], ACT.Copy, scale=scale))
            if both:
                SC.wait(a)
                a2 = SC.mark(act(dst_h[r1], dst_h[r0].bitcast(F32), ACT.Copy))
                a = a2
            VE.wait(a)
            hi = dst_h[r0].bitcast(F32)
            if both:
                v = VE.mark(tt(dst_l[r0], src[r0], hi, ALU.subtract))
                VE.wait(v)
                v = VE.mark(tt(dst_l[r1], src[r0], hi, ALU.subtract))
            elif scale != 1.0:
                v = VE.mark(stt(dst_l[r1], src[r0], scale, hi, ALU.mult, ALU.subtract))
            else:
                v = VE.mark(tt(dst_l[r1], src[r0], hi, ALU.subtract))
            return (a, v)

        pb = [0]

        def proj_bank():
            pb[0] += 1
            return pb[0] % 2

        z_ready, qn_ready, kn_ready, qf_ready, kf_ready = [], {}, {}, {}, {}

        b = proj_bank()
        PE.wait(*free[b])
        VE.wait(*fork)
        m_z0 = VE.mark(fill(ZT[:, :, :, :, :].rearrange("p a b c d -> p (a b c d)"), 0.0))
        for kv in range(2):
            m = project(BK[b][:, 256 * kv:256 * kv + 256])
        VE.wait(m, m_z0)
        for kv in range(2):
            for par in range(2):
                for g in range(2):
                    src = BK[b][rows_of(g), 256 * kv:256 * kv + 256]
                    lo = src[:, 0:240].rearrange("p (c i r) -> p i c r", i=8, r=2)[:, :, :, par]
                    hi = src[:, 16:256].rearrange("p (c i r) -> p i c r", i=8, r=2)[:, :, :, par]
                    for q, s_ in enumerate((lo, hi)):
                        pe = vec_(f"pe{kv}")[rows_of(g)].rearrange("p (i r) -> p i r", r=2)[:, 8 * q:8 * q + 8, par:par + 1]
                        m = VE.mark(tt(ZT[rows_of(par), kv, 8 * q:8 * q + 8, g, 0:15], s_,
                                       pe.to_broadcast([64, 8, 15]), ALU.add))
        free[b] = (m,)
        m_z = m

        def compress():
            b = 7
            PE.wait(m_z, *free[b])
            for kv in range(2):
                i = w1_at[kv]
                PE.wait(loaded(i))
                w1 = slot(i)[:, :].rearrange("p (i n) -> p i n", i=16)
                for i16 in range(16):
                    j = i16 % 4
                    f = mm(BK[b][32 * j:32 * j + 32, 128 * kv:128 * kv + 128],
                           ZT[:, kv, i16, :, :].rearrange("p a b -> p (a b)"), w1[:, i16, :], i16 < 4, i16 >= 12)
                    if i16 < 15:
                        PE.do(f)
                    else:
                        m = PE.mark(f)
                raw_free[i] = (m,)
                yield
            VE.wait(m, *fork)
            m = VE.mark(cp(C1[:, :], BK[b][:, 0:256]))
            yield
            PE.wait(m)
            for kv in range(2):
                m = PE.mark(mm(BK[b][:, 32 * kv:32 * kv + 32], C1[:, 128 * kv:128 * kv + 128], sel32, True, True))
            x = BK[b][:, 0:64]
            g2, gg = [t[:, :, :, :].rearrange("p a b c -> p (a b c)") for t in (G2, GG)]
            VE.wait(m)
            m = VE.mark(cp(gg, x))
            free[b] = (m,)
            VE.wait(m)
            m = VE.mark(tt(g2, gg, gg, ALU.mult))
            VE.wait(m)
            m = VE.mark(ts(g2, g2, 0.044715, ALU.mult, 1.0, ALU.add))
            VE.wait(m)
            m = VE.mark(tt(g2, g2, gg, ALU.mult))
            SC.wait(m)
            m = SC.mark(act(g2, g2, ACT.Exp, scale=-2.0 * 0.7978845608028654))
            yield
            VE.wait(m)
            m = VE.mark(ts(g2, g2, 1.0, ALU.add))
            VE.wait(m)
            m = VE.mark(recip(g2, g2))
            VE.wait(m)
            m = VE.mark(tt(gg, gg, g2, ALU.mult))
            VE.wait(m)
            m = VE.mark(cp(GV[:, :, :].rearrange("p (g r) c -> p g r c", g=2),
                           GG[:, 1, :, :].unsqueeze(2).to_broadcast([128, 2, 4, 16])))
            yield
            PE.wait(m, *free[b])
            PE.do(mm(BK[b][:, 0:32], vec_("w2k"), GG[:, 0, :, :].rearrange("p a b -> p (a b)"), True, True))
            m = PE.mark(mm(BK[b][:, 64:128], GV[:, :, :].rearrange("p a b -> p (a b)"), vec_("w2v"), True, True))
            src = BK[b][:, 0:32].rearrange("p (a b) -> p a b", a=2)
            SC.wait(m, *fork)
            a = SC.mark(act(KC[:, :, 0, :], src, ACT.Copy))
            VE.wait(a)
            v = VE.mark(tt(KC[:, :, 1, :], src, KC[:, :, 0, :].bitcast(F32), ALU.subtract))
            VE.wait(in_v)
            x = VE.mark(tt(VCX[:, :, :], BK[b][:, 64:128].unsqueeze(1).to_broadcast([128, 8, 64]),
                           cst_("hrow").unsqueeze(2).to_broadcast([128, 8, 64]), ALU.mult))
            free[b] = (x,)
            kc_ready.extend([a, v, x])

        kc_ready = []
        tasks.append(compress())

        for c in range(2):
            b = proj_bank()
            PE.wait(*free[b])
            m = project(BK[b][:, 0:256])
            SC.wait(m, *fork)
            VE.wait(*fork)
            for g in range(2):
                kn_ready[g] = kn_ready.get(g, ()) + stack(KNH[:, g, 256 * c:256 * c + 256],
                                                          KNL[:, g, 256 * c:256 * c + 256], BK[b][:, 0:256], g, 1.0, True)
            free[b] = kn_ready[1][-1:]
            tick()

        def by_rows(b, out_rows):
            PE.wait(*free[b])
            for t in range(2):
                j, wh, wl = half()
                for q in range(2):
                    for kk in range(4):
                        k = 4 * t + kk
                        PE.wait(*a_ready[0][k])
                        f = mm3(BK[b][:, 256 * q:256 * q + 256], AH[:, k, 128 * q:128 * q + 128],
                                AL[:, k, 128 * q:128 * q + 128], wh(256 * kk, 256), wl(256 * kk, 256),
                                k == 0 and q == 0, k == 7, True)
                        if kk < 3 or q < 1:
                            PE.do(f)
                        else:
                            m = PE.mark(f)
                half_free[j] = (m,)
                tick()
            SC.wait(m, *fork)
            x = SC.mark(act(out_rows, BK[b][:, :].rearrange("p (q n) -> p q n", q=2), ACT.Copy))
            free[b] = (x,)
            return x

        m_vn = by_rows(proj_bank(), VN[:, :, :])

        j, wh, wl = half()
        b = proj_bank()
        PE.wait(*free[b])
        for k in range(8):
            PE.wait(*a_ready[0][k])
            f = mm3(BK[b][0:32, 0:256], wh(32 * k, 32), wl(32 * k, 32), AH[:, k, :], AL[:, k, :], k == 0, k == 7)
            if k < 7:
                PE.do(f)
            else:
                m = PE.mark(f)
        half_free[j] = (m,)

        m_gate, m_ctb = [], []

        def gates(m, b):
            VE.wait(m, *fork)
            m = VE.mark(cp(GF[:, :], BK[b][0:32, 0:256]))
            free[b] = (m,)
            yield
            b = 7
            PE.wait(m, *free[b])
            for q in range(2):
                m = PE.mark(tp(BK[b][:, 32 * q:32 * q + 32], GF[:, 128 * q:128 * q + 128], ident[0:32, 0:32]))
            VE.wait(m)
            m = VE.mark(cp(gt[:, :, :], BK[b][:, 0:64].rearrange("p (q n) -> p q n", q=2)))
            free[b] = (m,)
            SC.wait(m)
            a = SC.mark(act(ga[:, :, :], gt[:, :, 0:24], ACT.Exp, scale=-1.0))
            VE.wait(m, in_v)
            x = VE.mark(tt(fa[:, :, :], gt[:, :, 24:32], vec_("bfg").unsqueeze(1).to_broadcast([128, 2, 8]), ALU.add))
            SC.wait(x)
            y = SC.mark(act(fb[:, :, :], fa[:, :, :], ACT.Abs))
            SC.wait(y)
            y = SC.mark(act(fb[:, :, :], fb[:, :, :], ACT.Exp, scale=-1.0))
            yield
            VE.wait(a)
            m = VE.mark(ts(ga[:, :, :], ga[:, :, :], 1.0, ALU.add))
            VE.wait(m)
            m_gate.append(VE.mark(recip(ga[:, :, :], ga[:, :, :])))
            SC.wait(y)
            y = SC.mark(act(fb[:, :, :], fb[:, :, :], ACT.Ln, bias=1.0))
            VE.wait(y, x)
            m = VE.mark(ts(fa[:, :, :], fa[:, :, :], 0.0, ALU.min))
            VE.wait(m)
            m = VE.mark(tt(fc[:, :, :], fb[:, :, :], fa[:, :, :], ALU.subtract))
            yield
            PE.wait(m, *free[b])
            for q in range(2):
                m = PE.mark(mm(BK[b][0:8, 0:256], fc[:, q, :], cst_("zto", 128 - 128 * q, 256), q == 0, q == 1))
            VE.wait(m, m_ctb0)
            x = VE.mark(cp(CTB[0:8, :], BK[b][0:8, 0:256]))
            VE.wait(x)
            x = VE.mark(tt(cr[0:8, 0, :], BK[b][0:8, 0:256], CTB[0:8, :], ALU.subtract))
            free[b] = (x,)
            VE.wait(x)
            x = VE.mark(cp(CTB[32:40, :], cr[0:8, 0, :]))
            VE.wait(x)
            x = VE.mark(cp(cb[0:8, :], cr[0:8, 0, :]))
            VE.wait(x)
            x = VE.mark(tt(cr[0:8, 1, :], cr[0:8, 0, :], cb[0:8, :], ALU.subtract))
            VE.wait(x)
            m_ctb.append(VE.mark(cp(CTB[64:72, :], cr[0:8, 1, :])))

        cb = at("cb", [128, 256], BF16, B2 + 40 * KB)
        VE.wait(*fork)
        m_ctb0 = VE.mark(fill(CTB[:, :], 0.0))
        tasks.append(gates(m, b))

        def queries(dst, ready, wait_for):
            for c in range(4):
                b = proj_bank()
                PE.wait(*free[b])
                m = project(BK[b][:, 0:256])
                SC.wait(m, *wait_for)
                VE.wait(*wait_for)
                for hh in range(2):
                    h = 2 * c + hh
                    ready[h] = stack(dst[:, h, :], dst[:, h, :], BK[b][:, 0:256], hh, 0.125, False)
                free[b] = ready[h][-1:]
                tick()

        queries(QN, qn_ready, fork)

        def compressed():
            b = 7
            PE.wait(*kc_ready, *free[b])
            for qt in range(2):
                for h in range(8):
                    PE.wait(*qn_ready[h])
                    m = PE.mark(mm(BK[b][:, 256 * qt + 32 * h:256 * qt + 32 * h + 32], QN[:, h, 128 * qt:128 * qt + 128],
                                   KC[:, h // 4, :, :].rearrange("p a b -> p (a b)"), True, True))
                yield
            src = BK[b][:, :].rearrange("p (u a c) -> p u a c", u=16, a=2)
            SC.wait(m)
            a = SC.mark(act(PL[:, :, :], src[:, :, 1, :], ACT.Copy))
            VE.wait(a)
            x = VE.mark(tt(PC[:, :, :], src[:, :, 0, :], PL[:, :, :], ALU.add))
            free[b] = (x,)
            tab = cst_("cbias").rearrange("p (u c) -> p u c", u=16)
            VE.wait(x)
            x = VE.mark(tt(PC[:, :, :], PC[:, :, :], tab, ALU.add))
            VE.wait(x)
            x = VE.mark(red(cs[:, 0, :], PC[:, :, :], ALU.max))
            yield

            def wide(t):
                return t.unsqueeze(2).to_broadcast([128, 16, 16])

            VE.wait(x)
            x = VE.mark(tt(PC[:, :, :], PC[:, :, :], wide(cs[:, 0, :]), ALU.subtract))
            SC.wait(x)
            a = SC.mark(act(PC[:, :, :], PC[:, :, :], ACT.Exp))
            VE.wait(a)
            x = VE.mark(tt(PC[:, :, :], PC[:, :, :], cst_("cmask").rearrange("p (u c) -> p u c", u=16), ALU.mult))
            VE.wait(x)
            x = VE.mark(red(cs[:, 1, :], PC[:, :, :], ALU.add))
            yield
            VE.wait(x)
            x = VE.mark(ts(cs[:, 1, :], cs[:, 1, :], 1e-30, ALU.max))
            VE.wait(x)
            x = VE.mark(recip(cs[:, 1, :], cs[:, 1, :]))
            VE.wait(x, *m_gate)
            x = VE.mark(tt(cs[:, 2, :].rearrange("p (q h) -> p q h", q=2), cs[:, 1, :].rearrange("p (q h) -> p q h", q=2),
                           ga[:, :, 0:24:3], ALU.mult))
            VE.wait(x)
            x = VE.mark(tt(PC[:, :, :], PC[:, :, :], wide(cs[:, 2, :]), ALU.mult))
            yield
            PE.wait(x, *free[b])
            for qt in range(2):
                m = PE.mark(tp(BK[b][:, 128 * qt:128 * qt + 128],
                               PC[:, 8 * qt:8 * qt + 8, :].rearrange("p a b -> p (a b)"), ident))
            SC.wait(m)
            x = SC.mark(act(PCT[:, :], BK[b][:, 0:256], ACT.Copy))
            free[b] = (x,)
            m_pct.append(x)

        m_pct = []

        pu_free, pv_free, pv_ready, ot_ready = {}, {}, {}, {}
        u_n = [0]

        def head_attention(kind, h):
            g = h // 4
            nb = 2 - kind
            ring = (8 * kind + h) % 2
            us = [u_n[0], u_n[0] + 1]
            u_n[0] += 2
            nm, su, sc = [[st[:, u % 8, 2 * i:2 * i + nb] for u in us] for i in range(3)]
            y = {}

            def scores(qt):
                u = us[qt]
                b = 2 + u % 2
                n = 128 * (qt + 1)
                PE.wait(*free[b])
                if kind == 0:
                    PE.wait(*qn_ready[h], *kn_ready[g], m_tabs)
                    q = QN[:, h, 128 * qt:128 * qt + 128]
                    PE.do(mm(BK[b][:, :], q, KNH[:, g, :], True, False, True))
                    PE.do(mm(BK[b][:, :], q, KNL[:, g, :], False, False, True))
                    for i in range(2):
                        m = PE.mark(mm(BK[b][:, 256 * i:256 * i + n], slopes[:, h, :], alibi[:, 0:n] if qt else
                                       alibi[:, 128:256], False, i == 1, True))
                else:
                    PE.wait(*qf_ready[h], *kf_ready[h], *m_ctb, m_tabs)
                    q = QF[:, h, 128 * qt:128 * qt + 128]
                    PE.do(mm(BK[b][:, 0:256], q, KFH[:, h, :], True, False, True))
                    PE.do(mm(BK[b][:, 0:256], q, KFL[:, h, :], False, False, True))
                    PE.do(mm(BK[b][:, 0:n], pick[:, h, :], CTB[:, 0:n], False, False, True))
                    m = PE.mark(mm(BK[b][:, n - 128:n], identb[:, :], maskb[:, 0, :], False, True, True))
                VE.wait(m, *pu_free.get(u - 8, ()))
                src = BK[b][:, 0:256 * nb].rearrange("p (i n) -> p i n", i=nb)[:, :, 0:n]
                x = VE.mark(red(nm[qt], src, ALU.max, negate=True))
                SC.wait(x, *fork2, *pu_free.get(u - 4, ()))
                for i in range(nb):
                    y[qt] = SC.mark(act(PU[:, u % 4, n * i:n * i + n], BK[b][:, 256 * i:256 * i + n], ACT.Exp,
                                        bias=nm[qt][:, i:i + 1], accum_out=su[qt][:, i:i + 1]))
                free[b] = (y[qt],)

            def scale(qt):
                VE.wait(y[qt])
                n = 128 * (qt + 1)
                x = VE.mark(recip(sc[qt], su[qt]))
                if kind == 0:
                    VE.wait(x, *m_gate)
                    x = VE.mark(tt(sc[qt], sc[qt], ga[:, qt, 3 * h + 1:3 * h + 3], ALU.mult))
                VE.wait(x)
                for i in range(nb):
                    p = PU[:, us[qt] % 4, n * i:n * i + n]
                    y[qt] = VE.mark(ts(p, p, sc[qt][:, i:i + 1], ALU.mult))

            def turn(qt):
                u = us[qt]
                b = 4 + u % 2
                PE.wait(y[qt], *free[b])
                nt = qt + 1
                for i in range(nb):
                    for t in range(nt):
                        m = PE.mark(tp(BK[b][:, 128 * (i + nb * t):128 * (i + nb * t) + 128],
                                       PU[:, u % 4, 128 * (nt * i + t):128 * (nt * i + t) + 128], ident))
                pu_free[u] = (m,)
                L = SC if qt == 0 else VE
                L.wait(m, *fork2, *pv_free.get(8 * kind + h - 2, ()))
                ev = (lambda d, s: act(d, s, ACT.Copy)) if qt == 0 else cp
                d = PV[:, ring, 0:256 * nb].rearrange("p (i n) -> p i n", i=nb)[:, :, 128 * qt:128 * qt + 128]
                x = L.mark(ev(d, BK[b][:, 0:128 * nb].rearrange("p (i n) -> p i n", i=nb)))
                if qt:
                    x = L.mark(ev(PV[:, ring, 256 * nb:384 * nb], BK[b][:, 128 * nb:256 * nb]))
                free[b] = (x,)
                pv_ready.setdefault(8 * kind + h, []).append(x)

            scores(0)
            yield
            scale(0)
            scores(1)
            yield
            turn(0)
            scale(1)
            yield
            turn(1)
            yield
            if h % 2:
                c = h // 2
                PE.wait(*pv_ready[8 * kind + h - 1], *pv_ready[8 * kind + h], *free[6])
                if kind == 0:
                    PE.wait(*m_pct, m_vn)
                    PE.do(mm(BK[6][:, 0:256], VCX[:, 2 * c:2 * c + 2, :].rearrange("p a b -> p (a b)"), PCT[:, :],
                             True, False, True))
                else:
                    PE.wait(*m_vf)
                for i in range(nb):
                    for t in range(2):
                        for hh in range(2):
                            if kind == 0:
                                v = VN[:, t, 128 * i + 64 * g:128 * i + 64 * g + 64]
                            else:
                                v = VF[:, t, 64 * (2 * c + hh):64 * (2 * c + hh) + 64]
                            p = PV[:, hh, 256 * i:256 * i + 256] if t == 0 else \
                                PV[:, hh, 256 * nb + 128 * i:256 * nb + 128 * i + 128]
                            m = PE.mark(mm(BK[6][rows_of(hh), 128 * t:256], v, p, kind == 1 and i == 0 and t == 0,
                                           i == nb - 1 and t == 1, True))
                pv_free[8 * kind + h - 1] = pv_free[8 * kind + h] = (m,)
                SC.wait(m, *fork2)
                x = SC.mark(act(OT2[:, 4 * kind + c, :], BK[6][:, 0:256], ACT.Copy))
                free[6] = (x,)
                ot_ready[4 * kind + c] = (x,)

        fork2 = [(PE.sem, PE.count), (SC.sem, SC.count), (VE.sem, VE.count)]
        tasks.append(compressed())

        def all_heads():
            for kind in range(2):
                for h in range(8):
                    while kind and (h not in kf_ready or h not in qf_ready or not m_vf):
                        yield
                    sub.append(head_attention(kind, h))
                    for _ in range(2):
                        step()
                        yield
            while sub:
                step()
                yield

        sub = []

        def step():
            for x in list(sub):
                if next(x, sub) is sub:
                    sub.remove(x)

        m_vf = []
        tasks.append(all_heads())
        for c in range(4):
            b = proj_bank()
            PE.wait(*free[b])
            m = project(BK[b][:, 0:256])
            SC.wait(m)
            for hh in range(2):
                h = 2 * c + hh
                kf_ready[h] = stack(KFH[:, h, :], KFL[:, h, :], BK[b][:, 0:256], hh, 1.0, True)
            free[b] = kf_ready[h][-1:]
            tick()
        for i in range(2):
            m_vf.append(by_rows(proj_bank(), VF[:, :, 256 * i:256 * i + 256]))
        queries(QF, qf_ready, fork2)
        a_free[0] = ((PE.sem, PE.count),)
        drain()
        heads_done = [(L.sem, L.count) for L in (PE, SC, VE)]

        A, B = BK[0], BK[1]
        PE.wait(*free[0], *free[1])
        for kind in range(2):
            for k in range(4):
                SC.wait(*ot_ready[4 * kind + k], *a_free[0])
                m = SC.mark(act(sq[:, 4 * kind + k, :], OT2[:, 4 * kind + k, :], ACT.Square))
                PE.wait(m)
                m = PE.mark(mm(A[32 * k:32 * k + 32, 256 * kind:256 * kind + 256], ones[:, :],
                               sq[:, 4 * kind + k, :], True, True))
        VE.wait(m)
        m = VE.mark(ts(part[:, :], A[:, :], 2.0, ALU.mult))
        free[0] = (m,)
        PE.wait(m)
        m = PE.mark(mm(B[:, :], sums[:, :], part[:, :], True, True))
        m = newton(B[:, :], m, 512, 1)
        src = lambda k: OT2[:, k, :]
        VE.wait(m)
        modulate(src, lambda k: sq[:, k, :],
                 lambda k: VE.mark(tt(src(k), src(k), rr[:, 256 * (k // 4):256 * (k // 4) + 256], ALU.mult)),
                 256, 0, lambda k: vec_("gn", k, 1), None, m)
        for k in range(8):
            for _ in contract(AH[:, k, :], AL[:, k, :], a_ready[0][k], k == 0, k == 7):
                pass
        a_free[0] = ((PE.sem, PE.count),)
        for dc in range(8):
            VE.wait(y_marks[dc // 2])
            m = VE.mark(tt(hT[:, dc, :], Y(dc), hT[:, dc, :], ALU.add))
            h_ready[dc] = (m,)
            if dc % 2:
                free[4 + dc // 2] = (m,)

        hr = at("hr", [128, 2, 1024], F32, B2)
        xr = at("xr", [128, 2, 1024], F32, B2 + 8 * KB)
        XS = [at(f"XS{i}", [128, 8, 64], F32, B2 + (16 + 2 * i) * KB) for i in range(3)]
        G, LI, SG, AT, YE = [at(n, [128, 512], F32, B2 + o * KB) for n, o in
                             (("G", 22), ("LI", 24), ("SG", 26), ("AT", 32), ("YE", 34))]
        AC = [at(f"AC{i}", [128, 512], F32, B2 + (28 + 2 * i) * KB) for i in range(2)]
        CT = [at(f"CT{i}", [128, 2, 2, 64], F32, B2 + (36 + i) * KB) for i in range(3)]
        CE = [at(f"CE{i}", [128, 256], F32, B2 + (39 + i) * KB) for i in range(3)]
        ST = [at(f"ST{i}", [128, 2, 64], F32, B2 + 42 * KB + 512 * i) for i in range(3)]
        SE = [at(f"SE{i}", [128, 64], BF16, B2 + 43 * KB + 512 + 128 * i) for i in range(2)]
        WR = at("WR", [128, 8, 32], F32, B2 + 44 * KB)
        BD = at("BD", [32, 1024], F32, B2 + 45 * KB)
        lnf = at("lnf", [128, 1024], F32, B2 + 45 * KB)
        BR = at("BR", [128, 32], F32, B2 + 43 * KB + 768)
        CI = at("CI", [128, 32], mybir.dt.int32, B2 + 43 * KB + 896)
        WT = at("WT", [32, 256], F32, B2 + 49 * KB)
        o = offset["slopes"]
        LG, GT, EQ, CU, EX, WW, PO = [at(n, [128, 2, 32], F32, o + 256 * i)
                                      for i, n in enumerate(("LG", "GT", "EQ", "CU", "EX", "WW", "PO"))]
        mx, ss, rt = [at(n, [128, 2, 8], F32, o + 1792 + 64 * i) for i, n in enumerate(("mx", "ss", "rt"))]
        BU = at("BU", [128, 2048], BF16, B2 + 51 * KB)

        s_moe, s_lnf = sem("s_moe"), sem("s_lnf")
        in_moe, in_lnf = (s_moe, 48), (s_lnf, 16)
        at_load[up_at[0, 0]] = [(heads_done, WR[:, :, :], w_router.rearrange("(k p) n -> p k n", p=128), s_moe),
                                (heads_done, BR[:, :], b_router, s_moe), (heads_done, BD[:, :], b_down, s_moe)]

        up_bias = slot(bias_at)
        GP.wait(loaded(bias_at), *heads_done)
        m = GP.mark(fill(BU[32:64, :], 0.0))
        GP.wait(m)
        m = GP.mark(cp(BU[0:32, :], up_bias[0:32, :]))
        GP.wait(m)
        m = GP.mark(cp(BU[64:128, :], up_bias[64:128, :]))
        for r in (slice(64, 128), slice(96, 128)):
            GP.wait(m)
            m = GP.mark(tt(up_bias[r, :], up_bias[r, :], BU[r, :], ALU.subtract))
            GP.wait(m)
            m = GP.mark(cp(BU[r, :], up_bias[r, :]))
        raw_free[bias_at] = m_bu = (m,)
        GP.wait(in_moe, m)
        m_wr = GP.mark(tt(WR[:, :, :], WR[:, :, :], vec_("ln2").unsqueeze(2).to_broadcast([128, 8, 32]), ALU.mult))

        w_out_done = fork = [(PE.sem, PE.count), (SC.sem, SC.count), (VE.sem, VE.count)]
        A, B, T, D = 0, 1, 2, 3
        for dc in range(8):
            PE.wait(*h_ready[dc])
            for q in range(2):
                b = 2 * q + dc // 4
                if dc % 4 == 0:
                    PE.wait(*free[b])
                m = PE.mark(tp(BK[b][:, 128 * (dc % 4):128 * (dc % 4) + 128], hT[:, dc, 128 * q:128 * q + 128], ident))
            if dc == 0:
                PE.wait(m_wr, *free[4])
            for q in range(2):
                m2 = PE.mark(mm(BK[4][:, 32 * q:32 * q + 32], hT[:, dc, 128 * q:128 * q + 128], WR[:, dc, :],
                                dc == 0 and q == 0, dc == 7, True))
            if dc % 4 == 3:
                half_ = dc // 4
                for q in range(2):
                    SC.wait(m, *fork)
                    a = SC.mark(act((G, LI, SG, AT)[dc // 4 + 2 * q][:, :], BK[2 * q + half_][:, :], ACT.Square,
                                    accum_out=ss[:, q, half_:half_ + 1]))
                    VE.wait(a, *fork)
                    x = VE.mark(cp(hr[:, q, 512 * half_:512 * half_ + 512], BK[2 * q + half_][:, :]))
                    free[2 * q + half_] = (x,)
        h_free = (m2,)
        VE.wait(a)
        x = VE.mark(tt(rt[:, :, 0], ss[:, :, 0], ss[:, :, 1], ALU.add))
        VE.wait(x)
        x = VE.mark(ts(rt[:, :, 0], rt[:, :, 0], 1.0 / 1024.0, ALU.mult, EPS, ALU.add))
        GP.wait(x, m_half)
        m_rt = GP.mark(tt(rt[:, :, 1], rt[:, :, 0], cols[:, 1:2].to_broadcast([128, 2]), ALU.pow))
        VE.wait(m_rt, m2)
        for q in range(2):
            x = VE.mark(stt(LG[:, q, :], BK[4][:, 32 * q:32 * q + 32], rt[:, q, 1:2], BR[:, :], ALU.mult, ALU.add))
        free[4] = (x,)
        VE.wait(x)
        for q in range(2):
            x = VE.mark(lambda e, q=q: e.max(mx[:, q, :], LG[:, q, :]))
        SC.wait(m_rt, *free[3])
        for q in range(2):
            m_xr = SC.mark(act(xr[:, q, :], hr[:, q, :], ACT.Copy, scale=rt[:, q, 1:2]))
        VE.wait(x)
        for q in range(2):
            VE.do(ts(GT[:, q, :], LG[:, q, :], mx[:, q, 3:4], ALU.is_gt, 0.0, ALU.add, accum_out=rt[:, q, 2:3]))
        g = VE.mark(tt(EQ[:, :, :], LG[:, :, :], mx[:, :, 3:4].to_broadcast([128, 2, 32]), ALU.is_equal))
        VE.wait(g)
        for q in range(2):
            x = VE.mark(lambda e, q=q: e.tensor_tensor_scan(CU[:, q, :], EQ[:, q, :], ones[:, :], rt[:, q, 2:3], ALU.add,
                                                            ALU.mult))
        VE.wait(x)
        x = VE.mark(stt(EQ[:, :, :], CU[:, :, :], 4.0, EQ[:, :, :], ALU.is_le, ALU.mult))
        VE.wait(x)
        m_sel = VE.mark(tt(GT[:, :, :], GT[:, :, :], EQ[:, :, :], ALU.add))
        PE.wait(m_sel, *free[5])
        tri, one = cst_("zto", 128, 128), cst_("zto", 256, 128)
        PE.do(mm(BK[5][:, 0:32], tri, GT[:, 0, :], True, True, True))
        PE.do(mm(BK[5][:, 32:64], one, GT[:, 0, :], False, False, True))
        PE.do(mm(BK[5][:, 32:64], tri, GT[:, 1, :], False, True, True))
        for q in range(2):
            m = PE.mark(mm(BK[5][:, 64:96], one, GT[:, q, :], False, q == 1, True))
        VE.wait(m)
        m_po = VE.mark(tt(PO[:, :, :], BK[5][:, 0:64].rearrange("p (q n) -> p q n", q=2), GT[:, :, :], ALU.mult))
        m_ci = VE.mark(cp(CI[:, :], BK[5][:, 64:96]))
        free[5] = (m_ci,)
        x = VE.mark(tt(LG[:, :, :], LG[:, :, :], mx[:, :, 0:1].to_broadcast([128, 2, 32]), ALU.subtract))
        SC.wait(x)
        a = SC.mark(act(EX[:, :, :], LG[:, :, :], ACT.Exp))
        m_ww = []

        def weights():
            VE.wait(a)
            x = VE.mark(tt(WW[:, :, :], EX[:, :, :], GT[:, :, :], ALU.mult))
            VE.wait(x)
            x = VE.mark(red(rt[:, :, 3], WW[:, :, :], ALU.add))
            VE.wait(x)
            x = VE.mark(recip(rt[:, :, 4], rt[:, :, 3]))
            VE.wait(x)
            m_ww.append(VE.mark(tt(WW[:, :, :], WW[:, :, :], rt[:, :, 4:5].to_broadcast([128, 2, 32]), ALU.mult)))

        st_free, ct_free, ce_free, xs_free, ac_free = [[()] * 3 for _ in range(5)]
        one_free = {"AT": (), "YE": (), "G": (), "LI": (), "SG": ()}
        ce_ready, xs_ready, ac_ready, st_ready, ct_ready = [[()] * 3 for _ in range(5)]

        def onehot(e, j, u):
            VE.wait(m_po, in_c2, *st_free[u])
            x = VE.mark(tt(ST[u][:, :, :], cst_("iota", 64 * j, 64).unsqueeze(1).to_broadcast([128, 2, 64]),
                           PO[:, :, e:e + 1].to_broadcast([128, 2, 64]), ALU.is_equal))
            st_ready[u] = (x,)
            if not m_ww:
                weights()
            VE.wait(x, *m_ww, *ct_free[u])
            for a_ in range(2):
                x = VE.mark(tt(CT[u][:, :, a_, :], ST[u][:, :, :], WW[:, :, e:e + 1].to_broadcast([128, 2, 64]), ALU.mult))
            ct_ready[u] = (x,)

        def gather(u):
            PE.wait(m_xr, *st_ready[u], *free[T])
            for k in range(8):
                for q in range(2):
                    m = PE.mark(mm(BK[T][:, 64 * k:64 * k + 64], xr[:, q, 128 * k:128 * k + 128], ST[u][:, q, :],
                                   k == 0 and q == 0, q == 1, True))
            st_free[u] = (m,)
            VE.wait(m, *xs_free[u])
            x = VE.mark(tt(XS[u][:, :, :], BK[T][:, :].rearrange("p (k n) -> p k n", k=8),
                           vec_("ln2").unsqueeze(2).to_broadcast([128, 8, 64]), ALU.mult))
            free[T] = (x,)
            xs_ready[u] = (x,)

        def turn_weights(u):
            PE.wait(*ct_ready[u], *free[T])
            for q in range(2):
                m = PE.mark(tp(BK[T][:, 128 * q:128 * q + 128], CT[u][:, q, :, :].rearrange("p a n -> p (a n)"), ident))
            ct_free[u] = (m,)
            SC.wait(m, *ce_free[u])
            x = SC.mark(act(CE[u][:, :], BK[T][:, 0:256], ACT.Copy))
            free[T] = (x,)
            ce_ready[u] = (x,)

        def side(r, s, b=512):
            return BK[r][64 * s:64 * s + 64, 0:b]

        def bias(e, sel_ready):
            PE.wait(*sel_ready, *m_bu, *free[A], *free[B])
            for n in range(4):
                m = PE.mark(mm(side(n // 2, n % 2), SE[e % 2][:, :], BU[:, 512 * n:512 * n + 512], True, False, True))
            return m

        def up(e, k, u):
            i = up_at[e, k]
            PE.wait(loaded(i), *xs_ready[u])
            for n in range(4):
                f = mm(side(n // 2, n % 2), XS[u][:, k, :], slot(i)[:, 512 * n:512 * n + 512], False, k == 7, True)
                if n < 3:
                    PE.do(f)
                else:
                    m = PE.mark(f)
            if k == 7:
                xs_free[u] = (m,)
            return m

        def swiglu(m, v):
            VE.wait(m, *one_free["G"])
            g = VE.mark(ts(G[:, :], BK[A][:, :], 7.0, ALU.min))
            free[A] = (g,)
            SC.wait(g, *one_free["SG"])
            s = SC.mark(act(SG[:, :], G[:, :], ACT.Sigmoid, scale=1.702))
            VE.wait(*one_free["LI"])
            x = VE.mark(ts(LI[:, :], BK[B][:, :], 7.0, ALU.min, -7.0, ALU.max))
            free[B] = (x,)
            return g, s, x

        def swiglu_end(marks, v):
            g, s, x = marks
            VE.wait(g, x)
            x = VE.mark(stt(LI[:, :], LI[:, :], 1.0, G[:, :], ALU.add, ALU.mult))
            VE.wait(x, s, *ac_free[v])
            y = VE.mark(tt(AC[v][:, :], LI[:, :], SG[:, :], ALU.mult))
            one_free["G"], one_free["LI"], one_free["SG"] = (x, s), (y,), (y,)
            ac_ready[v] = (y,)

        def turn(v):
            PE.wait(*ac_ready[v], *free[T])
            for q in range(4):
                m = PE.mark(tp(BK[T][:, 128 * q:128 * q + 128], AC[v][:, 128 * q:128 * q + 128], ident))
            ac_free[v] = (m,)
            SC.wait(m, *one_free["AT"])
            x = SC.mark(act(AT[:, :], BK[T][:, :], ACT.Copy))
            free[T] = (x,)
            return x

        def down_expert(e, ready, meanwhile=None):
            PE.wait(ready, *free[D])
            for i4 in range(4):
                i = down_at[e, i4]
                PE.wait(loaded(i))
                for c in range(2):
                    k = 2 * i4 + c
                    for n in range(2):
                        m = PE.mark(mm(side(D, n), AT[:, 128 * (k % 4) + 64 * (k // 4):128 * (k % 4) + 64 * (k // 4) + 64],
                                       slot(i)[:, 1024 * c + 512 * n:1024 * c + 512 * n + 512], k == 0, k == 7, True))
                raw_free[i] = (m,)
            one_free["AT"] = (m,)
            if meanwhile:
                meanwhile()
            SC.wait(m, *one_free["YE"])
            x = SC.mark(act(YE[:, :], BK[D][:, :], ACT.Copy))
            free[D] = (x,)
            return x

        def combine(u, ready, last=False):
            PE.wait(ready, *ce_ready[u])
            for q in range(2):
                for n in range(2):
                    r = slice(64 * n, 64 * n + 64)
                    m = PE.mark(mm(BK[4 + 2 * q + n][:, :], CE[u][r, 128 * q:128 * q + 128], YE[r, :], False, last, True))
            one_free["YE"] = ce_free[u] = (m,)
            return m

        sel_ready, se_free = {}, {}
        PQ = [slot(pt_at)[:, 512:1536], slot(wple_at)[:, 0:1024]]

        def selector(e):
            GP.wait(*se_free.get(e - 2, ()), m_ones, in_c)
            sel_ready[e] = (GP.mark(tt(SE[e % 2][:, :], sel32[:, e:e + 1].to_broadcast([128, 64]),
                                       ones[:, 0:1].to_broadcast([128, 64]), ALU.mult)),)

        def more_tokens(e, j):
            before = free[T]
            with Branch((PE, SC, VE), count, 64 * j):
                onehot(e, j, 2)
                gather(2)
                turn_weights(2)
                bias(e, sel_ready[e])
                for k in range(8):
                    m = up(e, k, 2)
                st_ = swiglu(m, 1)
                swiglu_end(st_, 1)
                x = down_expert(e, turn(1))
                combine(2, x)
                if j < 3:
                    more_tokens(e, j + 1)
            free[T] = (*before, *free[T])

        def bias_down():
            PE.wait(*m_ww, *free[T])
            for q in range(2):
                m = PE.mark(tp(BK[T][0:32, 128 * q:128 * q + 128], WW[:, q, :], ident))
            VE.wait(m)
            x = VE.mark(cp(WT[:, :], BK[T][0:32, 0:256]))
            free[T] = (x,)
            PE.wait(x, in_moe)
            for q in range(2):
                for n in range(2):
                    PE.wait(*free[4 + 2 * q + n])
                    m = PE.mark(mm(BK[4 + 2 * q + n][:, :], WT[:, 128 * q:128 * q + 128], BD[:, 512 * n:512 * n + 512],
                                   True, False, True))
            at_load[up_at[4, 0]] = [((m,), lnf[:, :], ln_f, s_lnf)]

        def ple_products():
            PE.wait(loaded(wple_at), loaded(pt_at))
            for q in range(2):
                for n, b in enumerate((T, D)):
                    PE.wait(*free[b])
                    for k in range(2):
                        m = PE.mark(mm(BK[b][:, :], slot(pt_at)[:, 256 * k + 128 * q:256 * k + 128 * q + 128],
                                       slot(wple_at)[:, 1024 * k + 512 * n:1024 * k + 512 * n + 512], k == 0, k == 1))
                    SC.wait(m)
                    x = SC.mark(act(PQ[q][:, 512 * n:512 * n + 512], BK[b][:, :], ACT.Copy))
                    free[b] = (x,)
                    pq_ready.append(x)

        pq_ready = []
        count = {}
        GH, GL = {}, {}

        def split_gate():
            for n in range(8):
                i = gate_at[n // 2]
                c = slice(1024 * (n % 2), 1024 * (n % 2) + 1024)
                GH[n], GL[n] = slot(up_at[NE - 1, 1 + n // 2], F32R)[:, c], slot(i, F32R)[:, c]
                SC.wait(loaded(i), last_up)
                a_ = SC.mark(act(GH[n], slot(i)[:, c], ACT.Copy))
                VE.wait(a_, last_up)
                x = VE.mark(tt(GL[n], slot(i)[:, c], GH[n].bitcast(F32), ALU.subtract))
                gate_ready.append((a_, x))

        gate_ready = []

        def counts(e):
            for L in (PE, SC, VE):
                L.wait(m_ci)
                L.do(lambda x, L=L: count.__setitem__(id(L), x.value_load(CI[0:1, e:e + 1], min_val=0, max_val=256)))

        selector(0)
        selector(1)
        onehot(0, 0, 0)
        gather(0)
        turn_weights(0)
        for e in range(NE + 1):
            u, w = e % 2, 1 - e % 2
            if e < NE:
                m = bias(e, sel_ready[e])
                for k in range(2):
                    m = up(e, k, u)
                if e == 0:
                    bias_down()
            if e:
                x = turn(0)
            if e < NE:
                m = up(e, 2, u)
            if e:
                x = down_expert(e - 1, x, split_gate if e == NE else None)
            if e + 1 < NE:
                onehot(e + 1, 0, w)
            if e < NE:
                up(e, 3, u)
                up(e, 4, u)
            if e:
                y_done = combine(w, x, e == NE)
            if e == NE:
                break
            if e == NE - 1:
                ple_products()
            for k in range(5, 8):
                m = up(e, k, u)
            se_free[e] = (m,)
            marks = swiglu(m, 0)
            if e + 1 < NE:
                gather(w)
            swiglu_end(marks, 0)
            counts(e)
            more_tokens(e, 1)
            last_up = (PE.sem, PE.count)
            for k in range(8):
                raw_free[up_at[e, k]] = (last_up,)
            se_free[e] = (last_up,)
            if e + 2 < NE:
                selector(e + 2)
            if e + 1 < NE:
                turn_weights(w)

        UH = at("UH", [128, 8, 256], F32R, B2 + 8 * KB)
        UL = at("UL", [128, 8, 256], F32R, B2 + 16 * KB)
        fork = [(PE.sem, PE.count), (SC.sem, SC.count), (VE.sem, VE.count)]

        def row_rstd(j, ready):
            VE.wait(*ready)
            x = VE.mark(tt(rt[:, :, j], ss[:, :, 0], ss[:, :, 1], ALU.add))
            VE.wait(x)
            x = VE.mark(ts(rt[:, :, j], rt[:, :, j], 1.0 / 1024.0, ALU.mult, EPS, ALU.add))
            GP.wait(x)
            return GP.mark(tt(rt[:, :, j + 1], rt[:, :, j], cols[:, 1:2].to_broadcast([128, 2]), ALU.pow))

        VE.wait(*fork)
        SC.wait(*fork)
        junk = [t for t in (SG, AT, AC[0], AC[1])]
        u_ready = {}
        for q in range(2):
            for n in range(2):
                VE.wait(y_done)
                x = VE.mark(tt(hr[:, q, 512 * n:512 * n + 512], BK[4 + 2 * q + n][:, :], hr[:, q, 512 * n:512 * n + 512],
                               ALU.add))
                free[4 + 2 * q + n] = (x,)
                SC.wait(x)
                a = SC.mark(act(junk[2 * q + n][:, :], hr[:, q, 512 * n:512 * n + 512], ACT.Square,
                                accum_out=ss[:, q, n:n + 1]))
                PE.wait(x, *free[0], *free[1], *free[2], *free[3])
                for c in range(4):
                    k = 4 * n + c
                    m = PE.mark(tp(BK[k // 2][:, 256 * (k % 2) + 128 * q:256 * (k % 2) + 128 * q + 128],
                                   hr[:, q, 128 * k:128 * k + 128], ident))
                    u_ready[k] = (m,)
        m_rt = row_rstd(5, (a,))
        for k in (0, 2, 4, 6, 1, 3, 5, 7):
            src = BK[k // 2][:, 256 * (k % 2):256 * (k % 2) + 256]
            g = vec_("lnp", k, 1)
            SC.wait(*u_ready[k], *(u_ready[k - 1] if k % 2 else u_ready[k + 1]))
            a = SC.mark(act(UH[:, k, :], src, ACT.Copy, scale=g))
            VE.wait(a)
            x = VE.mark(stt(UL[:, k, :], src, g, UH[:, k, :].bitcast(F32), ALU.mult, ALU.subtract))
            u_ready[k] = (a, x)
        for k in (0, 2, 4, 6, 1, 3, 5, 7):
            PE.wait(*u_ready[k], *gate_ready[k])
            for q in range(2):
                for n in range(2):
                    b = 4 + 2 * q + n
                    if k == 0:
                        PE.wait(*free[b])
                    m = PE.mark(mm3(BK[b][:, :], UH[:, k, 128 * q:128 * q + 128], UL[:, k, 128 * q:128 * q + 128],
                                    GH[k][:, 512 * n:512 * n + 512], GL[k][:, 512 * n:512 * n + 512], k == 0, k == 7))
                    if k == 7:
                        free[b] = (m,)
        VE.wait(*pq_ready)
        SC.wait(m_rt)
        for q in range(2):
            for n in range(2):
                b = 4 + 2 * q + n
                h_ = hr[:, q, 512 * n:512 * n + 512]
                t = junk[2 * q + n]
                SC.wait(*free[b])
                a = SC.mark(act(t[:, :], BK[b][:, :], ACT.Sigmoid, scale=rt[:, q, 6:7]))
                VE.wait(a)
                x = VE.mark(tt(t[:, :], t[:, :], PQ[q][:, 512 * n:512 * n + 512], ALU.mult))
                VE.wait(x)
                x = VE.mark(tt(h_, h_, t[:, :], ALU.add))
                SC.wait(x)
                a = SC.mark(act(t[:, :], h_, ACT.Square, accum_out=ss[:, q, n:n + 1]))
        m_rt = row_rstd(3, (a,))
        VE.wait(m_rt, in_lnf)
        out_ready = []
        for q in range(2):
            for n in range(2):
                h_ = hr[:, q, 512 * n:512 * n + 512]
                x = VE.mark(stt(h_, h_, rt[:, q, 4:5], lnf[:, 512 * n:512 * n + 512], ALU.mult, ALU.mult))
            out_ready.append(x)

        last_in = {r: first for rs, first in ((range(NR, NR + 6), heads_done), (range(NR + 6, NR + 10), w_out_done),
                                              ((NR + 10,), h_free)) for r in rs}
        for i, (pieces, value) in enumerate(loads):
            r = place[i]
            SP.wait(*last_in.get(r, ()))
            last_in[r] = raw_free.get(i)
            if i in at_load:
                for marks, d, src, sm in at_load[i]:
                    SP.wait(*marks)
                    SP.do(lambda e, d=d, src=src, sm=sm: e.dma_start(d, src).then_inc(sm, 16))
            for view, src in pieces:
                d = view(slots[F32][r][:, :])
                SP.do(lambda e, d=d, src=src, r=r: e.dma_start(d, src).then_inc(s_raw[r], 16))

        s_out = sem("s_out")
        for q in range(2):
            SP.wait(out_ready[q])
            SP.do(lambda e, q=q: e.dma_start(out[0, 128 * q:128 * q + 128, :], hr[:, q, :]).then_inc(s_out, 16))
        SP.wait((s_out, 32))

        block = ctx.enter_context(nc.Block())

        @block.tensor
        def _(e):
            PE.run(e)

        @block.scalar
        def _(e):
            SC.run(e)

        @block.vector
        def _(e):
            VE.run(e)

        @block.gpsimd
        def _(e):
            GP.run(e)

        @block.sync
        def _(e):
            SP.run(e)


def pack(inputs):
    f = {k: np.asarray(v) for k, v in inputs.items()}

    def chunks(v):
        return v.reshape(-1, 128).T

    def rows(v):
        return np.broadcast_to(v.reshape(1, -1), (128, v.size))

    i = np.arange(128)
    cid = np.concatenate([np.eye(128), i[:, None] % 32 == np.arange(32)[None]], 1).astype(np.float32)
    cst1, cst2 = np.zeros((128, N1), np.float32), np.zeros((128, N2), np.float32)

    def c(name):
        if name in CST1:
            return cst1[:, CST1[name][0]:CST1[name][1]]
        return cst2[:, CST2[name][0]:CST2[name][1]]

    c("blk")[:] = (i[:, None] // 64 == i[None] // 64) / 64.0
    c("perm")[:] = i[:, None] == (i[None] ^ 32)
    t = np.arange(256)
    inv = np.power(np.float32(10000.0), -np.arange(16, dtype=np.float32) / np.float32(16.0))
    ang = np.concatenate([(t // 64).astype(np.float32)[None] * inv[:, None],
                          (t % 64).astype(np.float32)[None] * inv[:, None]], 0)
    c("cos")[:] = np.tile(np.cos(ang), (4, 1))
    c("sin")[:] = np.tile(np.concatenate([-np.sin(ang), np.sin(ang)], 0), (2, 1))
    c("m01")[:] = np.where(i[None] <= i[:, None], 0.0, NEG)
    c("m10")[:] = np.where(i[None] >= i[:, None], 0.0, NEG)
    c("hd")[:] = (i[:, None] // 64 == np.arange(32)[None]) / 64.0
    c("zto")[:, 128:256] = i[:, None] <= i[None]
    c("zto")[:, 256:384] = 1.0
    end = np.arange(16) * 16 + 31
    for qt in range(2):
        seen = (end[None] <= (128 * qt + i)[:, None]) & (np.arange(16) < 15)[None]
        for h in range(8):
            u = 16 * (8 * qt + h)
            c("cmask")[:, u:u + 16] = seen
            c("cbias")[:, u:u + 16] = np.where(seen, -2.0 ** -(h + 1) * ((128 * qt + i)[:, None] - end[None]), NEG)
    c("hrow")[:] = i[:, None] // 16 == np.arange(8)[None]
    c("alibi")[:] = np.where(t[None] <= 128 + i[:, None], t[None] - 128 - i[:, None], NEG)
    c("iota")[:] = t[None] + 1.0
    c("pick")[:] = (i[:, None] % 32 == np.arange(8)[None]) & (i[:, None] < 96)

    vec = np.zeros((128, NVEC), np.float32)

    def v(name):
        a, b = VEC[name]
        return vec[:, a:b]

    cc = v("cc").reshape(128, 8, 32)
    cc[:, :, 0] = chunks(f["c"][0])
    cc[:, :, 1] = chunks(f["c_ctx"])
    for l in range(2):
        v(f"nm{l}")[:] = chunks(f["norm_mix"][l])
        v(f"nf{l}")[:] = chunks(f["norm_ffn"][l])
        v(f"ada_b{l}")[:] = chunks(f["ada_b"][l])
        v(f"conv{l}")[:] = np.concatenate([chunks(f["ffn_conv"][l, j]) for j in range(3)], 1)
    v("scconv")[:] = np.concatenate([chunks(f["sc_conv"][0, j]) for j in range(3)], 1)
    v("qn")[:, 0] = np.tile(f["win_q_norm"][0], 2)
    v("kn")[:, 0] = np.tile(f["win_k_norm"][0], 2)
    v("sink")[:] = rows(f["win_sink"][0])
    v("ln1")[:] = chunks(f["ln1_2"][0])
    v("ln2")[:] = chunks(f["ln2_2"][0])
    v("lnp")[:] = chunks(f["ln_ple_2"][0])
    v("lnf")[:] = chunks(f["ln_f_2"])
    v("gn")[:] = np.concatenate([chunks(f["gn_nsa_2"][0]), chunks(f["gn_fox_2"][0])], 1)

    for n, x in enumerate("kv"):
        v(f"pe{n}")[:] = np.tile(f[f"pe_cmp_{x}_2"][0].T, (2, 1))
    v("bfg")[:] = rows(f["b_fg_2"][0])
    v("w2k")[:] = np.tile(f["w_cmp2_k_2"][0], (1, 2))
    v("w2v")[:] = f["w_cmp2_v_2"][0]

    def T(x):
        return np.ascontiguousarray(x.T.reshape(-1, 128, x.shape[0]).transpose(1, 0, 2))

    return dict(xT=T(f["x"][0]), ctxT=T(f["ctx"][0]), cid=cid, cst1=cst1, cst2=cst2, vec=vec, ada_w=f["ada_w"],
                w_qkv=f["win_w_qkv"][0], w_o=f["win_w_o"][0], w_up=f["ffn_w_up"], w_down=f["ffn_w_down"],
                sc_in=f["sc_w_in"][0], sc_out=f["sc_w_out"][0], w_in=f["w_in_2"][0],
                w_cmp1=np.stack([f["w_cmp1_k_2"][0], f["w_cmp1_v_2"][0]]), w_out=f["w_out_2"][0],
                moe_up=f["w_up_2"][0], moe_down=f["w_down_2"][0], b_up=f["b_up_2"][0], b_down=f["b_down_2"][0],
                w_router=f["w_router_2"][0], b_router=np.ascontiguousarray(rows(f["b_router_2"][0])),
                pT=T(f["p_2"][0, 0]), w_ple=f["w_ple_2"][0], w_gate=f["w_ple_gate_2"][0],
                ln_f=np.ascontiguousarray(rows(f["ln_f_2"])))


def kernel(**inputs):
    import concourse.bacc as bacc
    from concourse.bass_utils import run_bass_kernel_spmd

    nc = bacc.Bacc("TRN2", target_bir_lowering=False, num_devices=1)
    arrays = {n: np.ascontiguousarray(a) for n, a in pack(inputs).items()}
    args = {n: nc.dram_tensor(n, a.shape, mybir.dt.from_np(a.dtype), kind="ExternalInput").ap()
            for n, a in arrays.items()}
    out = nc.dram_tensor("out", (1, 256, 1024), F32, kind="ExternalOutput").ap()
    program(nc, out=out, **args)
    return run_bass_kernel_spmd(nc, [arrays], core_ids=[0]).results[0]["out"]
```

```python
import concourse.bass as bass
from concourse import mybir
from concourse.alu_op_type import AluOpType as ALU
from contextlib import ExitStack
import numpy as np

F32 = mybir.dt.float32
F32R = mybir.dt.float32r
BF16 = mybir.dt.bfloat16
ACT = mybir.ActivationFunctionType
AX = mybir.AxisListType

KB = 1024
BASE = 16 * KB + 128
EPS = 1e-6
NEG = -1e30


class Line:

    def __init__(self, sem):
        self.sem = sem
        self.count = 0
        self.ops = []
        self.seen = {}

    def do(self, f):
        self.ops.append(f)

    def mark(self, f):
        self.count += 1
        self.ops.append(lambda e: f(e).then_inc(self.sem, 1))
        return (self.sem, self.count)

    def wait(self, *marks):
        for sem, value in marks:
            if self.seen.get(id(sem), 0) < value:
                self.seen[id(sem)] = value
                self.ops.append(lambda e, s=sem, v=value: e.wait_ge(s, v))

    def run(self, e):
        for f in self.ops:
            f(e)


class Branch:

    def __init__(self, lines, count, limit):
        self.lines, self.count, self.limit = lines, count, limit

    def __enter__(self):
        self.before = [(L.ops, L.count, dict(L.seen)) for L in self.lines]
        for L in self.lines:
            L.ops = []

    def __exit__(self, *_):
        for L, (ops, before, seen) in zip(self.lines, self.before):
            body, L.ops, L.seen = L.ops, ops, seen
            L.ops.append(self.both(L, body, before, L.count - before))

    def both(self, L, body, before, added):
        def f(e):
            with e.If(self.count[id(L)] > self.limit):
                for g in body:
                    g(e)
            with e.Else():
                e.wait_ge(L.sem, before)
                e.sem_inc(L.sem, added)
        return f


def act(out, in_, func, **kw):
    return lambda e: e.activation(out, in_, func, **kw)


def tt(out, a, b, op):
    return lambda e: e.tensor_tensor(out, a, b, op)


def ts(out, a, s1, op0, s2=None, op1=None, **kw):
    if op1 is None:
        return lambda e: e.tensor_scalar(out, a, s1, None, op0, **kw)
    return lambda e: e.tensor_scalar(out, a, s1, s2, op0, op1, **kw)


def stt(out, a, s, b, op0, op1, **kw):
    return lambda e: e.scalar_tensor_tensor(out, a, s, b, op0, op1, **kw)


def cp(out, a):
    return lambda e: e.tensor_copy(out, a)


def fill(out, v):
    return lambda e: e.memset(out, v)


def red(out, a, op, **kw):
    return lambda e: e.tensor_reduce(out, a, AX.X, op, **kw)


def recip(out, a):
    return lambda e: e.reciprocal(out, a)


def mm(out, w, x, start, stop, skip=False):
    return lambda e: e.matmul(out, w, x, start=start, stop=stop, skip_group_check=skip)


def tp(out, a, ident):
    return lambda e: e.transpose(out, a, ident)


def dma(out, in_):
    return lambda e: e.dma_start(out, in_)


def layout(parts):
    at, out = 0, {}
    for name, n in parts:
        out[name] = (at, at + n)
        at += n
    return out, at


CST1, N1 = layout([("blk", 128), ("perm", 128), ("cos", 256), ("sin", 256), ("m01", 128), ("m10", 128), ("hd", 32)])
CST2, N2 = layout([("zto", 384), ("cbias", 256), ("cmask", 256), ("hrow", 8), ("alibi", 256), ("pick", 8), ("iota", 256)])
NC = max(N1, N2)
VEC, NVEC = layout([("cc", 256), ("nm0", 8), ("nm1", 8), ("nf0", 8), ("nf1", 8), ("ada_b0", 48), ("ada_b1", 48),
                    ("qn", 1), ("kn", 1), ("sink", 16), ("conv0", 132), ("conv1", 132), ("scconv", 24),
                    ("ln1", 8), ("ln2", 8), ("lnp", 8), ("lnf", 8), ("gn", 8), ("pe0", 32), ("pe1", 32), ("bfg", 8),
                    ("w2k", 128), ("w2v", 64)])


def program(nc, xT, ctxT, cid, cst1, cst2, vec, ada_w, w_qkv, w_o, w_up, w_down, sc_in, sc_out, w_in, w_cmp1, w_out, moe_up, moe_down,
            b_up, b_down, w_router, b_router, pT, w_ple, w_gate, ln_f, out):
    ctx = ExitStack()
    with ctx:
        def at(name, shape, dt, off):
            return nc.alloc_sbuf_tensor_at(name, shape, dt, offset=BASE + off)

        def sem(name):
            return ctx.enter_context(nc.semaphore(name))

        PE, SC, VE, GP, SP = [Line(sem("s_" + n)) for n in ("pe", "act", "dve", "pool", "sp")]

        BK = [ctx.enter_context(nc.psum_tensor(f"B{i}", [128, 512], F32)) for i in range(8)]
        free = [()] * 8
        rot = [0]

        def bank(n=4, first=0):
            rot[0] += 1
            return first + rot[0] % n

        def Y(dc):
            return BK[4 + dc // 2][:, 256 * (dc % 2):256 * (dc % 2) + 256]

        used, offset = [0], {}

        def put(name, shape, dt):
            size = 2 if dt == BF16 else 4
            for s in shape[1:]:
                size *= s
            t = at(name, shape, dt, used[0])
            offset[name] = used[0]
            used[0] += (size + 31) // 32 * 32
            return t

        ID = put("ID", [128, 160], F32)
        C = put("C", [128, NC], F32)
        V = put("V", [128, NVEC], F32)
        hT = put("hT", [128, 8, 256], F32)
        identb = put("identb", [128, 128], BF16)
        alibi = put("alibi", [128, 256], BF16)
        slopes = put("slopes", [128, 8, 128], BF16)
        pick = put("pick", [128, 8, 128], BF16)
        maskb = put("maskb", [128, 2, 128], BF16)
        sums = put("sums", [128, 128], F32)
        ones = put("ones", [128, 32], F32)
        cols = put("cols", [128, 2], F32)
        adaT = put("adaT", [128, 2, 48], F32)
        adaC = put("adaC", [128, 16], F32)
        modA = put("modA", [128, 2, 8], F32)
        small = put("small", [128, 4, 8], F32)
        nsink = put("nsink", [128, 16], F32)
        NR, NS = 6, 4
        RAW = put("RAW", [128, NR, 2048], F32)
        SH = put("SH", [128, NS, 1024], F32R)
        SL = put("SL", [128, NS, 1024], F32R)
        B2 = used[0]

        def cst_(n, i=0, w=None):
            a, b = CST1[n] if n in CST1 else CST2[n]
            return C[:, a + i:(b if w is None else a + i + w)]

        def vec_(n, i=0, w=None):
            a, b = VEC[n]
            return V[:, a + i:(b if w is None else a + i + w)]

        ident = ID[:, 0:128]
        sel32 = ID[:, 128:160]
        eps = cols[:, 0:1]

        tasks = []

        def tick():
            for g in list(tasks):
                if next(g, tasks) is tasks:
                    tasks.remove(g)

        def begin(g):
            next(g)
            tasks.append(g)

        def drain():
            while tasks:
                tick()

        loads, place, raw_count, raw_free = [], [], {}, {}
        halves, half_ready, half_free, split_marks = [], {}, {}, {}
        BUF = [offset["RAW"] + 8 * KB * i for i in range(NR)]
        BUF += [B2 + (47 + 8 * i) * KB for i in range(7)]
        BUF += [offset["SH"], offset["SH"] + 8 * KB, offset["SL"], offset["SL"] + 8 * KB, offset["hT"]]
        slots = {dt: [at(f"{n}{i}", [128, 2048], dt, o) for i, o in enumerate(BUF)] for n, dt in (("R", F32), ("RR", F32R))}
        s_raw = [sem(f"s_raw{i}") for i in range(len(BUF))]
        order = [list(range(NR))]

        first_of_moe = None

        def load(*pieces):
            i = len(loads)
            if not order[0]:
                order[0].append(place[next(used_up)])
            r = order[0].pop(0)
            if first_of_moe is None:
                order[0].append(r)
            place.append(r)
            raw_count[r] = raw_count.get(r, 0) + 16 * len(pieces)
            loads.append((pieces, raw_count[r]))
            return i

        def loaded(i):
            return (s_raw[place[i]], loads[i][1])

        def slot(i, dt=F32):
            return slots[dt][place[i]]

        def cols_slot(w, c0, c1=None, by_rows=False):
            c1 = c0 + 128 if c1 is None else c1
            src = w.rearrange("(k p) n -> p k n", p=128)
            view = lambda s: s.rearrange("p (k n) -> p k n", k=8)
            if c1 == c0 + 128:
                i = load((view, src[:, :, c0:c0 + 256]))
            else:
                i = load((lambda s: view(s)[:, :, 0:128], src[:, :, c0:c0 + 128]),
                         (lambda s: view(s)[:, :, 128:256], src[:, :, c1:c1 + 128]))
            for c in range(2):
                halves.append((i, c, not by_rows))

        def rows_slot(w, r0):
            i = load((lambda s: s.rearrange("p (k n) -> p k n", k=2),
                      w[r0:r0 + 256, :].rearrange("(k p) n -> p k n", p=128)))
            for c in range(2):
                halves.append((i, c, False))

        ada_at = {}

        def ada_slot(layer, n):
            ada_at[layer, n] = load((lambda s: s, ada_w[layer, 128 * (n % 8):128 * (n % 8) + 128,
                                                        2048 * (n // 8):2048 * (n // 8) + 2048]))

        prepared, taken, ahead = [0], [0], [NS]
        lower = [(VE,)]

        def prepare(upto):
            while prepared[0] < min(upto, len(halves)):
                j = prepared[0]
                i, c, strided = halves[j]
                hi, lo = SH[:, j % NS, :], SL[:, j % NS, :]
                if c == "gf":
                    src = slot(i)[:, 0:256]
                    hi, lo = hi[:, 0:256], lo[:, 0:256]
                elif strided:
                    src = slot(i)[:, :].rearrange("p (k n) -> p k n", k=8)[:, :, 128 * c:128 * c + 128]
                    hi, lo = [x.rearrange("p (k n) -> p k n", k=8) for x in (hi, lo)]
                else:
                    src = slot(i)[:, 1024 * c:1024 * c + 1024]
                SC.wait(loaded(i), *half_free.get(j - NS, ()))
                m = SC.mark(act(hi, src, ACT.Copy))
                L = lower[0][j % len(lower[0])]
                L.wait(loaded(i), m, *half_free.get(j - NS, ()))
                n = L.mark(tt(lo, src, hi.bitcast(F32), ALU.subtract))
                half_ready[j] = (m, n)
                split_marks[i] = split_marks.get(i, ()) + (m, n)
                if c != 0:
                    raw_free[i] = split_marks[i]
                prepared[0] += 1

        def half():
            j = taken[0]
            taken[0] += 1
            prepare(j + ahead[0])
            PE.wait(*half_ready[j])
            return j, (lambda a, n=128: SH[:, j % NS, a:a + n]), (lambda a, n=128: SL[:, j % NS, a:a + n])

        ADA1 = [range(8 * (P // 3) + 3 * (P % 3), min(8 * (P // 3) + 3 * (P % 3) + 3, 8 * (P // 3) + 8))
                for P in range(9)]
        for n in range(8):
            ada_slot(0, n)
        for P in range(4):
            cols_slot(w_qkv, 256 * P)
        cols_slot(w_qkv, 1024)
        cols_slot(w_qkv, 1280, by_rows=True)
        for P in range(4):
            ada_slot(0, 8 + 4 * P)
            ada_slot(0, 9 + 4 * P)
            rows_slot(w_o, 256 * P)
            ada_slot(0, 10 + 4 * P)
            ada_slot(0, 11 + 4 * P)
        first_of_ffn0 = len(loads)
        for layer in range(2):
            if layer == 1:
                for P in range(4):
                    for g in range(3):
                        cols_slot(sc_in, 1024 * g + 256 * P)
                    if P:
                        rows_slot(sc_out, 256 * (P - 1))
                rows_slot(sc_out, 768)
            for P in range(11):
                cols_slot(w_up[layer], 256 * P)
                if P > 2:
                    rows_slot(w_down[layer], 256 * (P - 2))
                cols_slot(w_up[layer], 2816 + 256 * P)
                if P == 2:
                    rows_slot(w_down[layer], 0)
                if layer == 0 and 0 < P < 10:
                    for n in ADA1[P - 1]:
                        ada_slot(1, n)
            rows_slot(w_down[layer], 2304)
            rows_slot(w_down[layer], 2560)
        cols_slot(w_in, 512)
        cols_slot(w_in, 768, 1024)
        cols_slot(w_in, 896, 1152, by_rows=True)
        v = w_in.rearrange("(k p) n -> p k n", p=128)
        halves.append((load((lambda s: s[:, 0:256].rearrange("p (k n) -> p k n", k=8)[:, :, 0:24], v[:, :, 1280:1304]),
                            (lambda s: s[:, 0:256].rearrange("p (k n) -> p k n", k=8)[:, :, 24:32], v[:, :, 2840:2848])),
                       "gf", False))
        w1_at = [load((lambda s: s.rearrange("p (i n) -> p i n", i=16), w_cmp1[i].rearrange("(i p) n -> p i n", p=128)))
                 for i in range(2)]
        cols_slot(w_in, 0)
        cols_slot(w_in, 256)
        for c in (1816, 2072):
            cols_slot(w_in, c)
        for c in (2328, 2584):
            cols_slot(w_in, c, by_rows=True)
        for c in (1304, 1560):
            cols_slot(w_in, c)
        for P in range(4):
            rows_slot(w_out, 256 * P)

        NE = 32
        order[0] = order[0][:2] + list(range(NR, NR + 7)) + order[0][2:] + list(range(NR + 7, len(BUF)))
        up_at, down_at = {}, {}
        first_of_moe = len(loads)

        def in_order_of_use():
            for e in range(NE):
                for k in range(8):
                    yield up_at[e, k]
                    if k == 2 and e == 0:
                        yield bias_at
                    elif k == 2:
                        for n in range(4):
                            yield down_at[e - 1, n]

        used_up = in_order_of_use()
        two = lambda s: s.rearrange("p (k n) -> p k n", k=2)
        for e in range(NE):
            for k in range(8):
                if e == 0 and k == 2:
                    bias_at = load(*[(lambda s, r=r: s[r:r + 32, :], b_up) for r in (0, 64, 96)],
                                   (lambda s: s[32:64, 0:1024], b_down))
                if e == NE - 2 and k == 5:
                    wple_at = load((two, w_ple.rearrange("(k p) n -> p k n", p=128)))
                    pt_at = load((lambda s: s[:, 0:512].rearrange("p (k n) -> p k n", k=2), pT))
                up_at[e, k] = load((lambda s: s, moe_up[e, 128 * k:128 * k + 128, :]))
            for k in range(4):
                down_at[e, k] = load((two, moe_down[e, 256 * k:256 * k + 256, :].rearrange("(k p) n -> p k n", p=128)))
        gate_at = [load((two, w_gate[256 * k:256 * k + 256, :].rearrange("(k p) n -> p k n", p=128))) for k in range(4)]
        lnf_at = load((lambda s: s[:, 0:1024], ln_f))

        tmp, tmc = [at(n, [128, 8, 256], F32, B2 + i * 8 * KB) for i, n in enumerate(("tmp", "tmc"))]
        AH = at("AH", [128, 8, 512], F32R, B2 + 16 * KB)
        AL = at("AL", [128, 8, 512], F32R, B2 + 32 * KB)
        sq = at("sq", [128, 8, 512], F32, B2 + 48 * KB)
        part, vp, yy, zz, rr, adaS = [at(n, [128, 512], F32, B2 + (64 + 2 * i) * KB)
                                      for i, n in enumerate(("part", "vp", "yy", "zz", "rr", "adaS"))]

        s_in = [sem(f"s_in{i}") for i in range(5)]
        in_v, in_x, in_ctx, in_c, in_id = [(s, 16) for s in s_in]
        SP.do(lambda e: e.dma_start(V[:, :], vec).then_inc(s_in[0], 16))
        SP.do(lambda e: e.dma_start(ID[:, :], cid).then_inc(s_in[4], 16))
        at_load = {ada_at[0, 2]: [((), hT[:, :, :], xT, s_in[1])],
                   ada_at[0, 7] + 3: [((), tmc[:, :, :], ctxT, s_in[2]), ((), C[:, 0:N1], cst1, s_in[3])]}

        m_ones = VE.mark(fill(ones[:, :], 1.0))
        VE.do(fill(cols[:, 0:1], EPS))
        m_half = VE.mark(fill(cols[:, 1:2], -0.5))
        m_sums = VE.mark(fill(sums[:, :], 1.0 / 32768.0))
        SC.wait(in_v, m_sums)
        m_cc = SC.mark(act(vec_("cc"), vec_("cc"), ACT.Silu))
        LN_EXP = "natural_log_exp_and_others"
        SC.do(lambda e: e.preload_act_table_set(LN_EXP))
        VE.wait(in_id, in_v)
        VE.do(ts(nsink[:, :], vec_("sink"), -1.0, ALU.mult))
        VE.do(cp(identb[:, :], ident))

        def ada_burst(layer, slots, b):
            PE.wait(*free[b])
            for n in slots:
                i = ada_at[layer, n]
                PE.wait(loaded(i), m_cc)
                for j in range(4):
                    f = mm(BK[b][32 * j:32 * j + 32, :], V[:, 32 * (n % 8):32 * (n % 8) + 32],
                           slot(i)[:, 512 * j:512 * j + 512], n == slots[0], n == slots[-1])
                    if j < 3:
                        PE.do(f)
                    else:
                        raw_free[i] = (PE.mark(f),)
            VE.wait(*raw_free[i])
            if slots[0] % 8 == 0:
                m = VE.mark(cp(adaS[:, :], BK[b][:, :]))
            else:
                VE.wait((VE.sem, VE.count))
                m = VE.mark(tt(adaS[:, :], BK[b][:, :], adaS[:, :], ALU.add))
            free[b] = (m,)
            return m

        def ada_end(layer, g, m, b):
            PE.wait(m, in_id, *free[b])
            for q in range(4):
                f = tp(BK[b][:, 128 * q:128 * q + 128], adaS[:, 128 * q:128 * q + 128], ident)
                if q < 3:
                    PE.do(f)
                else:
                    m = PE.mark(f)
            VE.wait(m, in_v)
            dst = adaT[:, layer, 16 * g:16 * g + 16].rearrange("p (j b) -> p j b", b=4)
            bias = vec_(f"ada_b{layer}", 16 * g, 16).rearrange("p (j b) -> p j b", b=4)
            src = BK[b][:, :].rearrange("p (b j r) -> p r j b", b=4, r=32)
            m = VE.mark(tt(dst, src[:, 0], bias, ALU.add))
            if layer == 0 and g == 0:
                m = VE.mark(tt(adaC[:, :].rearrange("p (j b) -> p j b", b=4), src[:, 1], bias, ALU.add))
            free[b] = (m,)
            return m

        def ada_col(layer, i, k):
            return adaT[:, layer, 8 * i + k:8 * i + k + 1]

        def newton(ms, m, n, b, scale=1.0):
            SC.wait(m)
            a = SC.mark(act(yy[:, 0:n], ms, ACT.Ln, bias=eps))
            VE.wait(a)
            v = VE.mark(ts(vp[:, 0:n], ms, EPS, ALU.add))
            free[b] = (v,)
            SC.wait(a)
            a = SC.mark(act(yy[:, 0:n], yy[:, 0:n], ACT.Exp, scale=-0.5))
            VE.wait(a)
            z = VE.mark(tt(zz[:, 0:n], yy[:, 0:n], yy[:, 0:n], ALU.mult))
            VE.wait(z)
            z = VE.mark(tt(zz[:, 0:n], zz[:, 0:n], vp[:, 0:n], ALU.mult))
            VE.wait(z)
            z = VE.mark(ts(zz[:, 0:n], zz[:, 0:n], -0.5 * scale, ALU.mult, 1.5 * scale, ALU.add))
            VE.wait(z)
            return VE.mark(tt(rr[:, 0:n], yy[:, 0:n], zz[:, 0:n], ALU.mult))

        def rstd(src, ready, b0, b1, o):
            A, B, n = BK[b0], BK[b1], 256
            PE.wait(m_ones, m_sums, *free[b0])
            for k in range(8):
                SC.wait(*ready[k])
                m = SC.mark(act(sq[:, k, o:o + n], src(k), ACT.Square))
                PE.wait(m)
                f = mm(A[32 * (k % 4):32 * (k % 4) + 32, 0:n], ones[:, :], sq[:, k, o:o + n], k < 4, k >= 4)
                if k < 7:
                    PE.do(f)
                else:
                    m = PE.mark(f)
            VE.wait(m)
            m = VE.mark(cp(part[:, 0:n], A[:, 0:n]))
            free[b0] = (m,)
            PE.wait(m, *free[b1])
            m = PE.mark(mm(B[:, 0:n], sums[:, :], part[:, 0:n], True, True))
            return newton(B[:, 0:n], m, n, b1)

        a_ready = [[()] * 8, [()] * 8]
        a_free = [()]

        def scaled(src, dst):
            return [VE.mark(tt(dst(k), src(k), rr[:, 0:256], ALU.mult)) for k in range(8)]

        def modulate(t, u, m, o, A, Bv, ks=range(8)):
            h, x = {}, {}

            def low(k):
                L = GP if k % 2 else VE
                L.wait(h[k], x[k], *a_free[0])
                l = L.mark(tt(AL[:, k, o:o + 256], u(k), AH[:, k, o:o + 256].bitcast(F32), ALU.subtract))
                a_ready[o // 256][k] = (h[k], l)

            for k in ks:
                SC.wait(m[k], m_ab, *a_free[0])
                VE.wait(m[k], m_ab, *a_free[0])
                if Bv is None:
                    h[k] = SC.mark(act(AH[:, k, o:o + 256], t(k), ACT.Copy, scale=A(k)))
                    x[k] = VE.mark(ts(u(k), t(k), A(k), ALU.mult))
                else:
                    h[k] = SC.mark(act(AH[:, k, o:o + 256], t(k), ACT.Identity, scale=A(k), bias=Bv(k)))
                    x[k] = VE.mark(ts(u(k), t(k), A(k), ALU.mult, Bv(k), ALU.add))
                if k > ks[0]:
                    low(k - 1)
            low(ks[-1])

        def mm3(out, wh, wl, xh, xl, start, stop, skip=False):
            PE.do(mm(out, wh, xh, start, False, skip))
            PE.do(mm(out, wh, xl, False, False, skip))
            return mm(out, wl, xh, False, stop, skip)

        def project(out, moving=((0, 0),)):
            j, wh, wl = half()
            for a, o in moving:
                for k in range(8):
                    PE.wait(*a_ready[o // 256][k])
                    f = mm3(out[:, a:a + 256], wh(128 * k), wl(128 * k), AH[:, k, o:o + 256], AL[:, k, o:o + 256],
                            k == 0, k == 7)
                    if k < 7:
                        PE.do(f)
                    else:
                        m = PE.mark(f)
            half_free[j] = (m,)
            return m

        def pair(b, together=False):
            if not together:
                return [project(BK[b][:, 256 * c:256 * c + 256]) for c in range(2)][-1]
            prepare(taken[0] + NS)
            ahead[0] = 0
            js = [half() for _ in range(2)]
            ahead[0] = NS
            for k in range(8):
                PE.wait(*a_ready[0][k])
                for c, (j, wh, wl) in enumerate(js):
                    f = mm3(BK[b][:, 256 * c:256 * c + 256], wh(128 * k), wl(128 * k), AH[:, k, 0:256], AL[:, k, 0:256],
                            k == 0 and c == 0, k == 7, True)
                    if k < 7:
                        PE.do(f)
                    else:
                        m = PE.mark(f)
                        half_free[j] = (m,)
            return m

        y_marks = [None] * 4

        def contract(xh, xl, ready, first, last, parts=4):
            j, wh, wl = half()
            PE.wait(*ready)
            for dc in range(8):
                if first and dc % 2 == 0:
                    PE.wait(*free[4 + dc // 2])
                f = mm3(Y(dc), wh(128 * dc), wl(128 * dc), xh, xl, first and dc % 2 == 0, last, True)
                if dc == 7 or (last and dc % 2):
                    y_marks[dc // 2] = PE.mark(f)
                else:
                    PE.do(f)
                if dc == 7:
                    half_free[j] = (y_marks[3],)
                    yield half_free[j]
                elif dc % (8 // parts) == 8 // parts - 1:
                    yield ()

        h_ready = [()] * 8

        def residual(layer, i, chunks=range(8)):
            for dc in chunks:
                VE.wait(y_marks[dc // 2])
                m = VE.mark(stt(hT[:, dc, :], Y(dc), ada_col(layer, i, dc), hT[:, dc, :], ALU.mult, ALU.add))
                h_ready[dc] = (m,)
                if dc % 2:
                    free[4 + dc // 2] = (m,)

        UH = at("UH", [128, 8, 258], F32R, B2 + 78 * KB)
        UL = at("UL", [128, 8, 258], F32R, B2 + 78 * KB + 8256)
        EG = at("EG", [128, 4, 256], F32, B2 + 95 * KB)
        DG = at("DG", [128, 2, 128], F32, B2 + 99 * KB)
        r2 = at("r2", [128, 2], F32, B2 + 100 * KB)
        wb = at("wb", [128, 4], F32, B2 + 100 * KB + 32)
        early_at = (0, 1, 4, 5)
        early_done = []

        def norm_scales(gain, mod=None):
            if not mod:
                return gain, None, ()
            layer, i = mod
            VE.wait((VE.sem, VE.count))
            m = VE.mark(stt(modA[:, 0, :], adaT[:, layer, 8 * i + 8:8 * i + 16], 1.0, gain, ALU.add, ALU.mult))
            return modA[:, 0, :], adaT[:, layer, 8 * i:8 * i + 8], (m,)

        def times_rr(t, k, *marks):
            L = GP if k % 2 else VE
            L.wait(*marks)
            return L.mark(tt(t[:, k, :], t[:, k, :], rr[:, 0:256], ALU.mult))

        def finish(t, product, shift, o, ks):
            def normed(k):
                m = product(k)
                SC.wait(m)
                if shift is None:
                    return m, SC.mark(act(AH[:, k, o:o + 256], t[:, k, :], ACT.Copy))
                return m, SC.mark(act(AH[:, k, o:o + 256], t[:, k, :], ACT.Identity, bias=shift[:, k:k + 1]))

            pending = [normed(k) for k in ks[:2]]
            for i, k in enumerate(ks):
                if i + 2 < len(ks):
                    pending.append(normed(ks[i + 2]))
                VE.wait(*pending[i])
                hi = AH[:, k, o:o + 256].bitcast(F32)
                if shift is None:
                    l = VE.mark(tt(AL[:, k, o:o + 256], t[:, k, :], hi, ALU.subtract))
                else:
                    l = VE.mark(stt(AL[:, k, o:o + 256], t[:, k, :], shift[:, k:k + 1], hi, ALU.add, ALU.subtract))
                a_ready[o // 256][k] = (pending[i][1], l)

        def next_norm(res, gain, shift, ready, fork=()):
            A = lambda k: gain[:, k:k + 1]
            n = 256 if shift is None else 258
            hi, lo, sqr = [], [], []

            def low(k):
                VE.wait(hi[k])
                lo.append(VE.mark(stt(UL[:, k, 0:256], hT[:, k, :], A(k), UH[:, k, 0:256].bitcast(F32),
                                      ALU.mult, ALU.subtract)))

            SC.wait(*ready, *fork)
            for k in range(8):
                residual(*res, (k,))
                SC.wait(*h_ready[k])
                hi.append(SC.mark(act(UH[:, k, 0:256], hT[:, k, :], ACT.Copy, scale=A(k))))
                sqr.append(SC.mark(act(sq[:, k, 0:256], hT[:, k, :], ACT.Square)))
                if k == 1:
                    VE.wait(*fork)
                    if n > 256:
                        wide = shift.unsqueeze(2).to_broadcast([128, 8, 2])
                        a = SC.mark(act(UH[:, :, 256:258], wide, ACT.Copy))
                if k > 1:
                    low(k - 2)
                if k == 2 and n > 256:
                    VE.wait(a)
                    x = VE.mark(tt(UL[:, :, 256:258], wide, UH[:, :, 256:258].bitcast(F32), ALU.subtract))
                    ready = (a, x)
            low(6)
            low(7)
            prepare(taken[0] + 4)
            t = [SC.mark(act(tmp[:, k, :], hT[:, k, :], ACT.Copy, scale=A(k))) for k in range(8)]

            def early(cs, also={}):
                js = [half() for _ in cs]
                PE.wait(*ready)
                for c in cs:
                    PE.wait(*free[early_at[c]])
                for k in range(8):
                    PE.wait(hi[k], lo[k])
                    for c, (j, wh, wl) in zip(cs, js):
                        f = mm3(BK[early_at[c]][:, 0:n], wh(128 * k), wl(128 * k), UH[:, k, 0:n], UL[:, k, 0:n],
                                k == 0, k == 7)
                        if k < 7:
                            PE.do(f)
                        else:
                            m = PE.mark(f)
                            early_done[c:] = [m]
                            half_free[j] = (m,)
                    if k in also:
                        also[k]()

            marks = {}

            def token_sums():
                PE.wait(marks["part"])
                for q in range(2):
                    m = PE.mark(mm(BK[7][:, q:q + 1], part[:, 128 * q:128 * q + 128], sums[:, 0:1], True, True))
                VE.wait(m)
                v = VE.mark(ts(r2[:, :], BK[7][:, 0:2], EPS, ALU.add, 2.0 ** -30, ALU.mult))
                GP.wait(v, m_half)
                g = GP.mark(tt(r2[:, :], r2[:, :], cols[:, 1:2].to_broadcast([128, 2]), ALU.pow))
                GP.wait(g, in_id)
                marks["diag"] = GP.mark(tt(DG[:, :, :], ident.unsqueeze(1).to_broadcast([128, 2, 128]),
                                           r2[:, :].unsqueeze(2).to_broadcast([128, 2, 128]), ALU.mult))

            def spread():
                PE.wait(marks["diag"])
                m = PE.mark(mm(BK[7][:, 0:256], sums[:, :], DG[:, :, :].rearrange("p a b -> p (a b)"), True, True))
                SC.wait(m)
                marks["rr"] = SC.mark(act(rr[:, 0:256], BK[7][:, 0:256], ACT.Copy))
                free[7] = (marks["rr"],)

            ahead[0] = 0
            early((0, 1))
            PE.wait(*free[7])
            for k in range(8):
                PE.wait(sqr[k])
                f = mm(BK[7][32 * (k % 4):32 * (k % 4) + 32, 0:256], ones[:, :], sq[:, k, 0:256], k < 4, k >= 4)
                if k < 7:
                    PE.do(f)
                else:
                    m = PE.mark(f)
            VE.wait(m)
            marks["part"] = VE.mark(cp(part[:, 0:256], BK[7][:, 0:256]))
            early((2,), {2: token_sums})
            lower[0] = (VE,)
            prepare(taken[0] + 3)
            early((3,), {1: spread})
            lower[0] = (VE, GP)
            ahead[0] = NS

            finish(tmp, lambda k: times_rr(tmp, k, marks["rr"], t[k]), shift, 0, range(8))
            prepare(taken[0] + NS)
            for c in range(4):
                b = early_at[c]
                VE.wait(early_done[c])
                m = VE.mark(tt(EG[:, c, :], BK[b][:, 0:256], rr[:, 0:256], ALU.mult))
                if n > 256:
                    m = VE.mark(cp(wb[:, c:c + 1], BK[b][:, 256:257]))
                    SC.wait(m)
                    a = SC.mark(act(EG[:, c, :], EG[:, c, :], ACT.Identity, bias=wb[:, c:c + 1]))
                    early_done[c] = a
                else:
                    early_done[c] = m
                free[b] = (m,)

        hk, xk, ck = [lambda k, t=t: t[:, k, :] for t in (hT, tmp, tmc)]
        VE.wait(rstd(hk, [(in_x,)] * 8, 4, 5, 0))
        mx = scaled(hk, xk)
        m = ada_burst(0, range(8), 0)
        m_ada = ada_end(0, 0, m, 1)
        VE.wait(m_ada)
        VE.do(stt(modA[:, 0, :], adaT[:, 0, 8:16], 1.0, vec_("nm0"), ALU.add, ALU.mult))
        m_ab = VE.mark(stt(modA[:, 1, :], adaC[:, 8:16], 1.0, vec_("nm0"), ALU.add, ALU.mult))
        lower[0] = (VE, GP)
        for ks in (range(2), range(2, 8)):
            modulate(xk, lambda k: sq[:, k, 0:256], mx, 0, lambda k: modA[:, 0, k:k + 1], lambda k: ada_col(0, 0, k), ks)
            prepare(2)

        KH = at("KH", [128, 4, 512], F32R, B2)
        KL = at("KL", [128, 4, 512], F32R, B2 + 8 * KB)
        QS = at("QS", [128, 16, 256], F32R, B2 + 48 * KB)
        sets = [[at(f"{n}{j}", [128, 512], F32, B2 + (76 + 2 * i + 8 * j) * KB)
                 for i, n in enumerate(("qq", "m1", "qr", "qw"))] for j in range(2)]
        VR = at("VR", [128, 4, 256], F32, B2 + 92 * KB)
        set_free, set_n = [(), ()], [0]

        def rows_of(hh):
            return slice(64 * hh, 64 * hh + 64)

        def pieces(x, n):
            return x.rearrange("p (a n) -> p a n", a=n)

        def heads(b, m, wcol, roped, then, stat=None):
            i = set_n[0] % 2
            set_n[0] += 1
            qq, m1, qr, w = sets[i]
            n = 256 * roped
            SC.wait(m, *set_free[i])
            s1 = SC.mark(act(qq[:, :], BK[b][:, :], ACT.Square))
            s2 = SC.mark(act(w[:, :], BK[b][:, :], ACT.Copy, scale=wcol))
            free[b] = (s2,)
            GP.wait(s2, in_c, *set_free[i])
            g = GP.mark(tt(pieces(m1[:, 0:n], roped), pieces(w[:, 0:n], roped),
                           cst_("cos").unsqueeze(1).to_broadcast([128, roped, 256]), ALU.mult))
            yield
            b2 = bank(4)
            PE.wait(s2, in_c, *free[b2])
            p2 = PE.mark(mm(BK[b2][:, 0:n], cst_("perm"), w[:, 0:n], True, True))
            if stat is None:
                b1 = bank(4)
                PE.wait(s1, *free[b1])
                p1 = PE.mark(mm(BK[b1][:, :], cst_("blk"), qq[:, :], True, True))
            else:
                stat(s1, qq)
            yield
            if stat is None:
                mr = newton(BK[b1][:, :], p1, 512, b1)
            VE.wait(p2, *set_free[i])
            x = VE.mark(tt(pieces(qr[:, 0:n], roped), pieces(BK[b2][:, 0:n], roped),
                           cst_("sin").unsqueeze(1).to_broadcast([128, roped, 256]), ALU.mult))
            free[b2] = (x,)
            VE.wait(x, g)
            x = VE.mark(tt(qr[:, 0:n], qr[:, 0:n], m1[:, 0:n], ALU.add))
            if stat is None:
                VE.wait(x, mr)
                x = VE.mark(tt(qr[:, 0:n], qr[:, 0:n], rr[:, 0:n], ALU.mult))
                if n < 512:
                    x = VE.mark(tt(qr[:, n:512], w[:, n:512], rr[:, n:512], ALU.mult))
            set_free[i] = then(x, qr)

        qs_ready, k_ready, sq_done = [], [], []
        sb = 4

        def q_stat(P):
            def f(m, qq):
                PE.wait(m, in_c)
                if P == 0:
                    PE.wait(*free[sb])
                for c in range(2):
                    ch = 2 * P + c
                    p = 32 * (ch % 4)
                    o = 256 * (ch // 4)
                    x = PE.mark(mm(BK[sb][p:p + 32, o:o + 256], cst_("hd"), qq[:, 256 * c:256 * c + 256], True, True))
                sq_done.append(x)
            return f

        def q_then(P):
            def f(x, qr):
                SC.wait(x, m_x)
                VE.wait(x, m_x)
                for i in range(4):
                    r0, r1 = rows_of(i % 2), rows_of(1 - i % 2)
                    src = qr[r0, 256 * (i // 2):256 * (i // 2) + 256]
                    a = SC.mark(act(QS[r0, 4 * P + i, :], src, ACT.Copy))
                    VE.wait(a)
                    v = VE.mark(tt(QS[r1, 4 * P + i, :], src, QS[r0, 4 * P + i, :].bitcast(F32), ALU.subtract))
                    qs_ready.append((a, v))
                return (a, v, sq_done[P])
            return f

        def k_then(c):
            def f(x, qr):
                SC.wait(x)
                VE.wait(x)
                for hh in range(2):
                    r0, r1 = rows_of(hh), rows_of(1 - hh)
                    g = 2 * c + hh
                    a = SC.mark(act(KH[r0, g, :], qr[r0, :], ACT.Copy))
                    a2 = SC.mark(act(KH[r1, g, :], qr[r0, :], ACT.Copy))
                    VE.wait(a)
                    VE.do(tt(KL[r0, g, :], qr[r0, :], KH[r0, g, :].bitcast(F32), ALU.subtract))
                    v = VE.mark(tt(KL[r1, g, :], qr[r0, :], KH[r0, g, :].bitcast(F32), ALU.subtract))
                k_ready.extend([(a2, v)] * 2)
                return (a2, v)
            return f

        rq, rv, rz = [at(n, [128, 32], F32, B2 + 96 * KB + 128 * i) for i, n in enumerate(("rq", "rv", "rz"))]
        m_rq = []

        def query_scales():
            VE.wait(*sq_done)
            m = VE.mark(cp(part[:, :], BK[sb][:, :]))
            free[sb] = (m,)
            yield
            PE.wait(m, *free[5])
            for i in range(4):
                m = PE.mark(tp(BK[5][:, 128 * i:128 * i + 128], part[:, 128 * i:128 * i + 128], ident))
            VE.wait(m)
            x = VE.mark(ts(rv[:, :].rearrange("p (i j r) -> p i j r", i=4, j=4),
                           BK[5][:, :].rearrange("p (i j r) -> p i j r", i=4, j=4)[:, :, :, 0:2], EPS, ALU.add))
            free[5] = (x,)
            SC.wait(x)
            a = SC.mark(act(rq[:, :], rv[:, :], ACT.Ln))
            SC.wait(a)
            a = SC.mark(act(rq[:, :], rq[:, :], ACT.Exp, scale=-0.5))
            yield
            VE.wait(a)
            x = VE.mark(tt(rz[:, :], rq[:, :], rq[:, :], ALU.mult))
            VE.wait(x)
            x = VE.mark(tt(rz[:, :], rz[:, :], rv[:, :], ALU.mult))
            VE.wait(x)
            x = VE.mark(ts(rz[:, :], rz[:, :], -0.0625, ALU.mult, 0.1875, ALU.add))
            VE.wait(x)
            x = VE.mark(tt(rq[:, :], rq[:, :], rz[:, :], ALU.mult))
            VE.wait(x)
            m_rq.append(VE.mark(ts(rv[:, :], rq[:, :], -1.0, ALU.mult)))

        for P in range(4):
            b = bank(4)
            PE.wait(*free[b])
            if P == 0:
                m = pair(b)
                m_x = (GP.sem, GP.count)
            for c in range(2):
                if P:
                    m = project(BK[b][:, 256 * c:256 * c + 256])
                if (P, c) == (1, 0):
                    m_rr = rstd(ck, [(in_ctx,)] * 8, 4, 5, 256)
                if (P, c) == (1, 1):
                    mc = [SC.mark(act(ck(k), ck(k), ACT.Copy, scale=modA[:, 1, k:k + 1])) for k in range(8)]
                    mc = [times_rr(tmc, k, mc[k], m_rr) for k in range(8)]
                if P > 1:
                    finish(tmc, lambda k: mc[k], adaC[:, 0:8], 256, range(4 * P - 8 + 2 * c, 4 * P - 6 + 2 * c))
                tick()
            begin(heads(b, m, vec_("qn"), 2, q_then(P), q_stat(P)))
        for c in range(2):
            b = bank(4)
            PE.wait(*free[b])
            m = project(BK[b], ((0, 0), (256, 256)))
            tick()
            begin(heads(b, m, vec_("kn"), 1, k_then(c)))
            if c == 0:
                tick()
                tasks.append(query_scales())
        m_v = []
        VE.wait(in_c)
        VE.do(cp(maskb[:, 0, :], cst_("m01")))
        m_maskb = VE.mark(cp(maskb[:, 1, :], cst_("m10")))

        def project_values():
            vb = (6, 7)
            for t in range(2):
                j, wh, wl = half()
                for q in range(4):
                    b = vb[q // 2]
                    if t == 0:
                        PE.wait(*free[b])
                    for kk in range(4):
                        k = 4 * t + kk
                        o = 128 * q
                        PE.wait(*a_ready[q // 2][k])
                        f = mm3(BK[b][:, 256 * (q % 2):256 * (q % 2) + 256], AH[:, k, o:o + 128], AL[:, k, o:o + 128],
                                wh(256 * kk, 256), wl(256 * kk, 256), k == 0 and q % 2 == 0, k == 7, True)
                        if kk < 3 or q < 3:
                            PE.do(f)
                        else:
                            m = PE.mark(f)
                    if q == 3:
                        half_free[j] = (m,)
                    yield
            SC.wait(m)
            for i in range(2):
                x = SC.mark(act(VR[:, 2 * i:2 * i + 2, :], BK[vb[i]][:, :].rearrange("p (a n) -> p a n", a=2), ACT.Copy))
                free[vb[i]] = (x,)
            m_v.extend([m, x])
            yield

        def rcol(t, h, qt):
            i = 16 * (h // 8) + 8 * qt + h % 8
            return t[:, i:i + 1]

        NP = 4
        PR = at("PR", [128, NP, 512], F32, B2 + 76 * KB)
        JK = at("JK", [128, 4, 512], BF16, B2 + 84 * KB)
        PT = at("PT", [128, 4, 4, 256], F32, B2 + 16 * KB)
        OH = at("OH", [128, 2, 256], F32R, B2 + 32 * KB)
        OL = at("OL", [128, 2, 256], F32R, B2 + 34 * KB)
        OT = at("OT", [128, 2, 256], F32, B2 + 36 * KB)
        RB = at("RB", [128, 2, 256], F32, B2 + 38 * KB)
        RD = at("RD", [128, 2, 16], F32, B2 + 96 * KB + 512)
        RX = at("RX", [128, 2, 2, 128], F32, B2 + 88 * KB)
        jk, rb_ready = [], {}
        pr_free, pt_free, o_free, pt_ready, rd_ready = {}, {}, {}, {}, {}
        no_sets = set_free

        def attend(h):
            g = h // 4
            nm, su, es = [small[:, h % 4, 2 * i:2 * i + 2] for i in range(3)]
            y = []
            for qt in range(2):
                b = (2 * h + qt) % 3
                PE.wait(*qs_ready[h], *k_ready[g], *free[b], m_maskb)
                q = QS[:, h, 128 * qt:128 * qt + 128]
                PE.do(mm(BK[b][:, :], q, KH[:, g, :], True, False, True))
                PE.do(mm(BK[b][:, :], q, KL[:, g, :], False, False, True))
                o = 128 if qt == 0 else 0
                m = PE.mark(mm(BK[b][:, o:o + 128], identb[:, :], maskb[:, qt, :], False, True, True))
                VE.wait(m, *m_rq, *jk[-4:-3])
                x = VE.mark(ts(JK[:, len(jk) % 4, :], BK[b][:, :], rcol(rv, h, qt), ALU.mult, nsink[:, h:h + 1], ALU.min,
                               accum_out=nm[:, qt:qt + 1]))
                jk.append(x)
                SC.wait(x, *no_sets[0], *no_sets[1], *pr_free.get((h - 2, qt), ()))
                y.append(SC.mark(act(PR[:, (2 * h + qt) % NP, :], BK[b][:, :], ACT.Exp, scale=rcol(rq, h, qt),
                                     bias=nm[:, qt:qt + 1], accum_out=su[:, qt:qt + 1])))
                yield
            s = SC.mark(act(es, nm, ACT.Exp, bias=vec_("sink", h, 1)))
            for qt in range(2):
                b = (2 * h + qt) % 3
                PE.wait(y[qt])
                for t in range(4):
                    f = tp(BK[b][:, 128 * t:128 * t + 128], PR[:, (2 * h + qt) % NP, 128 * t:128 * t + 128], ident)
                    if t < 3:
                        PE.do(f)
                    else:
                        m = PE.mark(f)
                pr_free[h, qt] = (m,)
                L = VE if qt else SC
                L.wait(m, m_v[0], *pt_free.get(h - 4, ()))
                dst = PT[:, h % 4, :, 128 * qt:128 * qt + 128]
                src = BK[b][:, :].rearrange("p (t n) -> p t n", t=4)
                x = L.mark(cp(dst, src) if qt else act(dst, src, ACT.Copy))
                free[b] = (x,)
                pt_ready[h] = pt_ready.get(h, ()) + (x,)
                if qt == 0:
                    VE.wait(s)
                    x = VE.mark(tt(su, su, es, ALU.add))
                    VE.wait(x)
                    rd_ready[h] = VE.mark(recip(RD[:, :, h], su))
                    if h % 2:
                        VE.wait(rd_ready[h], *no_sets[0], *no_sets[1], *pt_free.get(h - 4, ()))
                        rb_ready[h] = VE.mark(cp(RX[:, h // 2 % 2, :, :].rearrange("p q (a n) -> p q a n", a=2),
                                                 RD[:, :, h - 1:h + 1].unsqueeze(3).to_broadcast([128, 2, 2, 64])))
                yield
            if h % 2:
                c = h // 2
                PE.wait(*free[3], rb_ready[h])
                for qt in range(2):
                    PE.do(tp(BK[3][:, 256 + 128 * qt:384 + 128 * qt], RX[:, c % 2, qt, :], ident))
                PE.wait(*pt_ready[h - 1], *pt_ready[h], m_v[1])
                for t in range(4):
                    for hh in range(2):
                        f = mm(BK[3][rows_of(hh), 0:256], VR[:, t, 64 * g:64 * g + 64], PT[:, (2 * c + hh) % 4, t, :],
                               t == 0, t == 3)
                        if t < 3 or hh == 0:
                            PE.do(f)
                        else:
                            m = PE.mark(f)
                pt_free[h - 1] = pt_free[h] = (m,)
                SC.wait(m, *o_free.get(c - 2, ()))
                a = SC.mark(act(RB[:, c % 2, :], BK[3][:, 256:512], ACT.Copy))
                VE.wait(a)
                x = VE.mark(tt(OT[:, c % 2, :], BK[3][:, 0:256], RB[:, c % 2, :], ALU.mult))
                free[3] = (x,)
                yield
                SC.wait(x)
                a = SC.mark(act(OH[:, c % 2, :], OT[:, c % 2, :], ACT.Copy))
                VE.wait(a)
                v = VE.mark(tt(OL[:, c % 2, :], OT[:, c % 2, :], OH[:, c % 2, :].bitcast(F32), ALU.subtract))
                yield
                if h == 15:
                    lower[0], ahead[0] = (GP, VE), NS
                for m in contract(OH[:, c % 2, :], OL[:, c % 2, :], (a, v), c == 0, c == 7):
                    o_free[c] = m
                    yield

        def adaln_rest():
            for n in range(8, 24, 2):
                yield
                yield
                yield
                m = ada_burst(0, range(n, n + 2), 3)
                if n % 8 == 6:
                    x = ada_end(0, n // 8, m, 3)
                    m_adas.append(x)
                yield

        m_adas = []
        lower[0], ahead[0] = (GP,), 2
        pv = project_values()
        next(pv)
        next(pv)
        for _ in range(7):
            tick()
            next(pv)
        tasks.append(adaln_rest())
        for h in range(16):
            tasks.append(attend(h))
            tick()
            tick()
        while len(m_adas) < 2:
            tick()
        VE.wait(*m_adas)
        after = norm_scales(vec_("nf0"), (0, 3))
        drain()

        AH = at("AH2", [128, 8, 256], F32R, B2 + 8 * KB)
        AL = at("AL2", [128, 8, 256], F32R, B2 + 16 * KB)
        sq = at("sq2", [128, 8, 256], F32, B2 + 24 * KB)
        part, vp, yy, zz, rr = [at(n + "2", [128, 512], F32, B2 + (32 + 2 * i) * KB)
                                for i, n in enumerate(("part", "vp", "yy", "zz", "rr"))]
        adaS = at("adaS2", [128, 512], F32, B2 + 42 * KB)
        ct = at("ct", [128, 2, 4, 256], F32, B2 + 44 * KB)
        mid = at("mid", [128, 2, 512], F32, B2 + 52 * KB)
        MH = at("MH", [128, 2, 512], F32R, B2 + 56 * KB)
        ML = at("ML", [128, 2, 512], F32R, B2 + 60 * KB)
        m_free, ct_free = [(), ()], [(), ()]
        fork = [(PE.sem, PE.count), (SC.sem, SC.count), (VE.sem, VE.count), (GP.sem, GP.count)]
        GP.wait(*fork)
        s_c2 = sem("s_c2")
        at_load[first_of_ffn0 + 2] = [(fork, C[:, 0:N2], cst2, s_c2)]
        in_c2 = (s_c2, 16)
        onesb = at("onesb", [128, 128], BF16, B2 + 76 * KB)

        def tables():
            GP.wait((GP.sem, GP.count))
            m = GP.mark(fill(onesb[:, :], 1.0))
            GP.wait(in_c2, m_maskb, m)
            for h in range(8):
                GP.do(ts(slopes[:, h, :], identb[:, :], 2.0 ** -(h + 1), ALU.mult))
                m_tabs[0] = GP.mark(ts(pick[:, h, :], onesb[:, :], cst_("pick", h, 1), ALU.mult))
                yield
            m_tabs[0] = GP.mark(cp(alibi[:, :], cst_("alibi")))

        m_tabs, in_turn = [None], tables()

        def conv_taps(tiles, ready):
            VE.wait(*ready)
            m = [VE.mark(stt(dst[:, 1:256], src[:, 0:255], w(0), dst[:, 1:256], ALU.mult, ALU.add))
                 for dst, src, w in tiles]
            for x, (dst, src, w) in zip(m, tiles):
                VE.wait(x)
                y = VE.mark(stt(dst[:, 0:255], src[:, 1:256], w(2), dst[:, 0:255], ALU.mult, ALU.add))
            return y

        def split_mid(s, x):
            SC.wait(x, *m_free[s])
            a = SC.mark(act(MH[:, s, :], mid[:, s, :], ACT.Copy))
            VE.wait(a)
            v = VE.mark(tt(ML[:, s, :], mid[:, s, :], MH[:, s, :].bitcast(F32), ALU.subtract))
            return (a, v)

        def down(s, ready, first, last):
            for c in range(2):
                for m in contract(MH[:, s, 256 * c:256 * c + 256], ML[:, s, 256 * c:256 * c + 256], ready,
                                  first and c == 0, last and c == 1):
                    if m:
                        m_free[s] = m

        def ffn(layer, scales):
            def tap(chunk):
                return lambda i: vec_(f"conv{layer}", 44 * i + chunk, 1)

            ready, made, conv, gated, product = [None, None], {}, {}, {}, {}
            made[0, 0], made[0, 1] = early_done[1], early_done[3]

            def taps(P, half_u):
                s = P % 2
                SC.wait(made[P, half_u], *ct_free[s])
                if P:
                    src = [BK[2 * s + half_u][:, 256 * c:256 * c + 256] for c in range(2)]
                else:
                    src = [EG[:, 2 * half_u + c, :] for c in range(2)]
                for c in range(2):
                    w = tap(22 * half_u + 2 * P + c)
                    a = SC.mark(act(ct[:, s, 2 * half_u + c, :], src[c], ACT.Copy, scale=w(1)))
                x = conv_taps([(ct[:, s, 2 * half_u + c, :], src[c], tap(22 * half_u + 2 * P + c)) for c in range(2)], (a,))
                if P:
                    free[2 * s + half_u] = (x,)
                conv[P, half_u] = x

            def silu(P):
                g = ct[:, P % 2, 0:2, :].rearrange("p a n -> p (a n)")
                SC.wait(conv[P, 0])
                gated[P] = SC.mark(act(g, g, ACT.Silu))

            def multiply(P):
                s = P % 2
                g, u = [ct[:, s, i:i + 2, :].rearrange("p a n -> p (a n)") for i in (0, 2)]
                VE.wait(gated[P], conv[P, 1], *m_free[s])
                product[P] = VE.mark(tt(mid[:, s, :], g, u, ALU.mult))
                ct_free[s] = (product[P],)

            def split(P):
                ready[P % 2] = split_mid(P % 2, product[P])

            turns = {(1, 0): ((taps, 0, 0), (taps, 0, 1)),
                     (1, 2): ((silu, 0), (multiply, 0), (taps, 1, 0)),
                     (2, 0): ((split, 0), (silu, 1), (taps, 1, 1)),
                     (2, 2): ((multiply, 1), (split, 1), (taps, 2, 0)),
                     (2, 1): ((silu, 2), (taps, 2, 1), (multiply, 2)),
                     (3, 0): ((taps, 3, 0),), (3, 1): ((split, 2), (silu, 3))}

            def turn(P, i):
                rest = (((split, P - 1), (taps, P, 0)), ((silu, P),), ((taps, P, 1), (multiply, P)))[i]
                for f, *x in turns.get((P, i), rest if P > 1 else ()):
                    f(*x)

            for P in range(1, 11):
                s = P % 2
                PE.wait(*free[2 * s])
                made[P, 0] = pair(2 * s, P == 1)
                if layer == 0 and P in (4, 7, 10):
                    ada_end(1, P // 3 - 1, m_ada1, 2 * (1 - s) + 1)
                if P == 1:
                    prepare(taken[0] + NS)
                turn(P, 0)
                if P > 2:
                    down(s, ready[s], False, False)
                    turn(P, 1)
                PE.wait(*free[2 * s + 1])
                made[P, 1] = pair(2 * s + 1)
                prepare(taken[0] + NS)
                if layer == 0 and P < 10:
                    m_ada1 = ada_burst(1, ADA1[P - 1], 2 * (1 - s) + 1)
                turn(P, 2)
                if P == 2:
                    down(0, ready[0], True, False)
                    turn(2, 1)
                if layer == 0:
                    next(in_turn, None)
            split(10)
            down(1, ready[1], False, False)
            lower[0] = (GP,)
            after = scales()
            down(0, ready[0], False, True)
            return after

        next_norm((0, 2), *after, fork)
        after = ffn(0, lambda: norm_scales(vec_("nm1"), (1, 0)))

        next_norm((0, 5), *after)
        gc = at("gc", [128, 2, 512], F32, B2 + 64 * KB)
        cu = at("cu", [128, 2, 512], F32, B2 + 68 * KB)
        before = None
        rot[0] = 1
        for P in range(4):
            s = P % 2
            bs, ms = [], []
            for g in range(3):
                if P == 0 and g < 2:
                    ms.append(early_done[2 * g + 1])
                    bs.append(None)
                    continue
                b = bank()
                bs.append(b)
                PE.wait(*free[b])
                m = pair(b, P == 0)
                ms.append(m)
                if g == 1:
                    SC.wait(m, *ct_free[s])
                    a = SC.mark(act(gc[:, s, :], BK[b][:, :], ACT.Copy))
                    free[b] = (a,)
            g1 = gc[:, s, :]
            if P == 0:
                a, g1 = ms[1], EG[:, 2:4, :].rearrange("p a n -> p (a n)")
            prepare(taken[0] + NS)
            VE.wait(a, ms[2], *ct_free[s])
            x = VE.mark(tt(cu[:, s, :], BK[bs[2]][:, :], g1, ALU.mult))
            free[bs[2]] = (x,)
            SC.wait(x)
            w = [lambda i, c=c: vec_("scconv", 8 * i + 2 * P + c, 1) for c in range(2)]
            for c in range(2):
                a = SC.mark(act(ct[:, s, c, :], cu[:, s, 256 * c:256 * c + 256], ACT.Copy, scale=w[c](1)))
            x = conv_taps([(ct[:, s, c, :], cu[:, s, 256 * c:256 * c + 256], w[c]) for c in range(2)], (a,))
            VE.wait(x, ms[0], *m_free[s])
            g0 = BK[bs[0]][:, :] if P else EG[:, 0:2, :].rearrange("p a n -> p (a n)")
            x = VE.mark(tt(mid[:, s, :], g0, ct[:, s, 0:2, :].rearrange("p a n -> p (a n)"), ALU.mult))
            if P:
                free[bs[0]] = (x,)
            ct_free[s] = (x,)
            now = split_mid(s, x)
            if before:
                down(1 - s, before, P == 1, False)
            before = now
        lower[0] = (GP,)
        after = norm_scales(vec_("nf1"), (1, 3))
        down(1, before, False, True)
        next_norm((1, 2), *after)
        after = ffn(1, lambda: norm_scales(vec_("ln1")))

        next_norm((1, 5), *after)
        SC.do(lambda e: e.preload_act_table_set(LN_EXP))

        OT2 = at("OT2", [128, 8, 256], F32, B2)
        QF = at("QF", [128, 8, 256], F32R, B2 + 24 * KB)
        QN = at("QN", [128, 8, 256], F32R, B2 + 44 * KB)
        KNH = at("KNH", [128, 2, 512], F32R, B2 + 52 * KB)
        KNL = at("KNL", [128, 2, 512], F32R, B2 + 56 * KB)
        VN = at("VN", [128, 2, 256], F32, B2 + 60 * KB)
        ZT = at("ZT", [128, 2, 16, 2, 16], F32, B2 + 62 * KB)
        KFH = at("KFH", [128, 8, 256], F32R, B2 + 66 * KB)
        KFL = at("KFL", [128, 8, 256], F32R, B2 + 74 * KB)
        VF = at("VF", [128, 2, 512], F32, B2 + 82 * KB)
        PU = at("PU", [128, 4, 512], F32, B2 + 86 * KB)
        PV = at("PV", [128, 2, 768], F32, B2 + 94 * KB)
        o = B2 + 100 * KB
        PC = at("PC", [128, 16, 16], F32, o)
        PL = at("PL", [128, 16, 16], F32, o + KB)
        PCT = at("PCT", [128, 256], F32, o + 2 * KB)
        VCX = at("VCX", [128, 8, 64], F32, B2 + 41 * KB)
        CTB = at("CTB", [128, 256], BF16, B2 + 40 * KB + 512)
        C1 = at("C1", [128, 256], F32, B2 + 32 * KB)
        GG = at("GG", [128, 2, 2, 16], F32, B2 + 33 * KB)
        G2 = at("G2", [128, 2, 2, 16], F32, B2 + 33 * KB + 256)
        GV = at("GV", [128, 8, 16], F32, B2 + 33 * KB + 512)
        KC = at("KC", [128, 2, 2, 16], F32R, B2 + 34 * KB)
        GF = at("GF", [32, 256], F32, B2 + 35 * KB)
        gt = at("gt", [128, 2, 32], F32, B2 + 36 * KB)
        ga = at("ga", [128, 2, 24], F32, B2 + 36 * KB + 256)
        fa = at("fa", [128, 2, 8], F32, B2 + 36 * KB + 512)
        fb = at("fb", [128, 2, 8], F32, B2 + 36 * KB + 576)
        fc = at("fc", [128, 2, 8], F32, B2 + 36 * KB + 640)
        st = at("st", [128, 8, 8], F32, B2 + 36 * KB + 704)
        cs = at("cs", [128, 4, 16], F32, B2 + 37 * KB)
        cr = at("cr", [128, 2, 256], F32, B2 + 38 * KB)

        fork = [(PE.sem, PE.count), (SC.sem, SC.count), (VE.sem, VE.count)]

        def stack(dst_h, dst_l, src, hh, scale, both):
            r0, r1 = rows_of(hh), rows_of(1 - hh)
            a = SC.mark(act(dst_h[r0], src[r0], ACT.Copy, scale=scale))
            if both:
                SC.wait(a)
                a2 = SC.mark(act(dst_h[r1], dst_h[r0].bitcast(F32), ACT.Copy))
                a = a2
            VE.wait(a)
            hi = dst_h[r0].bitcast(F32)
            if both:
                v = VE.mark(tt(dst_l[r0], src[r0], hi, ALU.subtract))
                VE.wait(v)
                v = VE.mark(tt(dst_l[r1], src[r0], hi, ALU.subtract))
            elif scale != 1.0:
                v = VE.mark(stt(dst_l[r1], src[r0], scale, hi, ALU.mult, ALU.subtract))
            else:
                v = VE.mark(tt(dst_l[r1], src[r0], hi, ALU.subtract))
            return (a, v)

        pb = [0]

        def proj_bank():
            pb[0] += 1
            return pb[0] % 2 if pb[0] > 2 else pb[0] + 1

        z_ready, qn_ready, kn_ready, qf_ready, kf_ready = [], {}, {}, {}, {}

        VE.wait(*fork)
        m_z0 = VE.mark(fill(ZT[:, :, :, :, :].rearrange("p a b c d -> p (a b c d)"), 0.0))
        VE.wait(*early_done, m_z0)
        for kv in range(2):
            for par in range(2):
                for g in range(2):
                    src = EG[rows_of(g), kv, :]
                    lo = src[:, 0:240].rearrange("p (c i r) -> p i c r", i=8, r=2)[:, :, :, par]
                    hi = src[:, 16:256].rearrange("p (c i r) -> p i c r", i=8, r=2)[:, :, :, par]
                    for q, s_ in enumerate((lo, hi)):
                        pe = vec_(f"pe{kv}")[rows_of(g)].rearrange("p (i r) -> p i r", r=2)[:, 8 * q:8 * q + 8, par:par + 1]
                        m = VE.mark(tt(ZT[rows_of(par), kv, 8 * q:8 * q + 8, g, 0:15], s_,
                                       pe.to_broadcast([64, 8, 15]), ALU.add))
        m_z = m

        def compress():
            b = 7
            PE.wait(m_z, *free[b])
            for kv in range(2):
                i = w1_at[kv]
                PE.wait(loaded(i))
                w1 = slot(i)[:, :].rearrange("p (i n) -> p i n", i=16)
                for i16 in range(16):
                    j = i16 % 4
                    f = mm(BK[b][32 * j:32 * j + 32, 128 * kv:128 * kv + 128],
                           ZT[:, kv, i16, :, :].rearrange("p a b -> p (a b)"), w1[:, i16, :], i16 < 4, i16 >= 12)
                    if i16 < 15:
                        PE.do(f)
                    else:
                        m = PE.mark(f)
                raw_free[i] = (m,)
                yield
            VE.wait(m, *fork)
            m = VE.mark(cp(C1[:, :], BK[b][:, 0:256]))
            yield
            PE.wait(m)
            for kv in range(2):
                m = PE.mark(mm(BK[b][:, 32 * kv:32 * kv + 32], C1[:, 128 * kv:128 * kv + 128], sel32, True, True))
            x = BK[b][:, 0:64]
            g2, gg = [t[:, :, :, :].rearrange("p a b c -> p (a b c)") for t in (G2, GG)]
            VE.wait(m)
            m = VE.mark(cp(gg, x))
            free[b] = (m,)
            VE.wait(m)
            m = VE.mark(tt(g2, gg, gg, ALU.mult))
            VE.wait(m)
            m = VE.mark(ts(g2, g2, 0.044715, ALU.mult, 1.0, ALU.add))
            VE.wait(m)
            m = VE.mark(tt(g2, g2, gg, ALU.mult))
            SC.wait(m)
            m = SC.mark(act(g2, g2, ACT.Exp, scale=-2.0 * 0.7978845608028654))
            yield
            VE.wait(m)
            m = VE.mark(ts(g2, g2, 1.0, ALU.add))
            VE.wait(m)
            m = VE.mark(recip(g2, g2))
            VE.wait(m)
            m = VE.mark(tt(gg, gg, g2, ALU.mult))
            VE.wait(m)
            m = VE.mark(cp(GV[:, :, :].rearrange("p (g r) c -> p g r c", g=2),
                           GG[:, 1, :, :].unsqueeze(2).to_broadcast([128, 2, 4, 16])))
            yield
            PE.wait(m, *free[b])
            PE.do(mm(BK[b][:, 0:32], vec_("w2k"), GG[:, 0, :, :].rearrange("p a b -> p (a b)"), True, True))
            m = PE.mark(mm(BK[b][:, 64:128], GV[:, :, :].rearrange("p a b -> p (a b)"), vec_("w2v"), True, True))
            src = BK[b][:, 0:32].rearrange("p (a b) -> p a b", a=2)
            SC.wait(m, *fork)
            a = SC.mark(act(KC[:, :, 0, :], src, ACT.Copy))
            VE.wait(a)
            v = VE.mark(tt(KC[:, :, 1, :], src, KC[:, :, 0, :].bitcast(F32), ALU.subtract))
            VE.wait(in_v)
            x = VE.mark(tt(VCX[:, :, :], BK[b][:, 64:128].unsqueeze(1).to_broadcast([128, 8, 64]),
                           cst_("hrow").unsqueeze(2).to_broadcast([128, 8, 64]), ALU.mult))
            free[b] = (x,)
            kc_ready.extend([a, v, x])

        kc_ready = []

        for c in range(2):
            SC.wait(early_done[2 + c], *fork)
            VE.wait(early_done[2 + c], *fork)
            for g in range(2):
                kn_ready[g] = kn_ready.get(g, ()) + stack(KNH[:, g, 256 * c:256 * c + 256],
                                                          KNL[:, g, 256 * c:256 * c + 256], EG[:, 2 + c, :], g, 1.0, True)
            tick()

        def by_rows(b, out_rows):
            PE.wait(*free[b])
            for t in range(2):
                j, wh, wl = half()
                for q in range(2):
                    for kk in range(4):
                        k = 4 * t + kk
                        PE.wait(*a_ready[0][k])
                        f = mm3(BK[b][:, 256 * q:256 * q + 256], AH[:, k, 128 * q:128 * q + 128],
                                AL[:, k, 128 * q:128 * q + 128], wh(256 * kk, 256), wl(256 * kk, 256),
                                k == 0 and q == 0, k == 7, True)
                        if kk < 3 or q < 1:
                            PE.do(f)
                        else:
                            m = PE.mark(f)
                half_free[j] = (m,)
                tick()
            SC.wait(m, *fork)
            x = SC.mark(act(out_rows, BK[b][:, :].rearrange("p (q n) -> p q n", q=2), ACT.Copy))
            free[b] = (x,)
            return x

        m_vn = by_rows(proj_bank(), VN[:, :, :])

        j, wh, wl = half()
        b = proj_bank()
        PE.wait(*free[b])
        for k in range(8):
            PE.wait(*a_ready[0][k])
            f = mm3(BK[b][0:32, 0:256], wh(32 * k, 32), wl(32 * k, 32), AH[:, k, :], AL[:, k, :], k == 0, k == 7)
            if k < 7:
                PE.do(f)
            else:
                m = PE.mark(f)
        half_free[j] = (m,)

        m_gate, m_ctb = [], []

        def gates(m, b):
            VE.wait(m, *fork)
            m = VE.mark(cp(GF[:, :], BK[b][0:32, 0:256]))
            free[b] = (m,)
            yield
            b = 6
            PE.wait(m, *free[b])
            for q in range(2):
                m = PE.mark(tp(BK[b][:, 32 * q:32 * q + 32], GF[:, 128 * q:128 * q + 128], ident[0:32, 0:32]))
            VE.wait(m)
            m = VE.mark(cp(gt[:, :, :], BK[b][:, 0:64].rearrange("p (q n) -> p q n", q=2)))
            free[b] = (m,)
            SC.wait(m)
            a = SC.mark(act(ga[:, :, :], gt[:, :, 0:24], ACT.Exp, scale=-1.0))
            VE.wait(m, in_v)
            x = VE.mark(tt(fa[:, :, :], gt[:, :, 24:32], vec_("bfg").unsqueeze(1).to_broadcast([128, 2, 8]), ALU.add))
            SC.wait(x)
            y = SC.mark(act(fb[:, :, :], fa[:, :, :], ACT.Abs))
            SC.wait(y)
            y = SC.mark(act(fb[:, :, :], fb[:, :, :], ACT.Exp, scale=-1.0))
            yield
            VE.wait(a)
            m = VE.mark(ts(ga[:, :, :], ga[:, :, :], 1.0, ALU.add))
            VE.wait(m)
            m_gate.append(VE.mark(recip(ga[:, :, :], ga[:, :, :])))
            SC.wait(y)
            y = SC.mark(act(fb[:, :, :], fb[:, :, :], ACT.Ln, bias=1.0))
            VE.wait(y, x)
            m = VE.mark(ts(fa[:, :, :], fa[:, :, :], 0.0, ALU.min))
            VE.wait(m)
            m = VE.mark(tt(fc[:, :, :], fb[:, :, :], fa[:, :, :], ALU.subtract))
            yield
            PE.wait(m, *free[b])
            for q in range(2):
                m = PE.mark(mm(BK[b][0:8, 0:256], fc[:, q, :], cst_("zto", 128 - 128 * q, 256), q == 0, q == 1))
            VE.wait(m, m_ctb0)
            x = VE.mark(cp(CTB[0:8, :], BK[b][0:8, 0:256]))
            VE.wait(x)
            x = VE.mark(tt(cr[0:8, 0, :], BK[b][0:8, 0:256], CTB[0:8, :], ALU.subtract))
            free[b] = (x,)
            VE.wait(x)
            x = VE.mark(cp(CTB[32:40, :], cr[0:8, 0, :]))
            VE.wait(x)
            x = VE.mark(cp(cb[0:8, :], cr[0:8, 0, :]))
            VE.wait(x)
            x = VE.mark(tt(cr[0:8, 1, :], cr[0:8, 0, :], cb[0:8, :], ALU.subtract))
            VE.wait(x)
            m_ctb.append(VE.mark(cp(CTB[64:72, :], cr[0:8, 1, :])))

        cb = at("cb", [128, 256], BF16, B2 + 40 * KB)
        VE.wait(*fork)
        m_ctb0 = VE.mark(fill(CTB[:, :], 0.0))
        tasks.append(compress())
        tasks.append(gates(m, b))

        def queries(dst, ready, wait_for):
            for c in range(4):
                b = proj_bank()
                PE.wait(*free[b])
                m = project(BK[b][:, 0:256])
                SC.wait(m, *wait_for)
                VE.wait(*wait_for)
                for hh in range(2):
                    h = 2 * c + hh
                    ready[h] = stack(dst[:, h, :], dst[:, h, :], BK[b][:, 0:256], hh, 0.125, False)
                free[b] = ready[h][-1:]
                tick()

        queries(QN, qn_ready, fork)

        def compressed():
            b = 7
            PE.wait(*kc_ready, *free[b])
            for qt in range(2):
                for h in range(8):
                    PE.wait(*qn_ready[h])
                    m = PE.mark(mm(BK[b][:, 256 * qt + 32 * h:256 * qt + 32 * h + 32], QN[:, h, 128 * qt:128 * qt + 128],
                                   KC[:, h // 4, :, :].rearrange("p a b -> p (a b)"), True, True))
                yield
            src = BK[b][:, :].rearrange("p (u a c) -> p u a c", u=16, a=2)
            SC.wait(m)
            a = SC.mark(act(PL[:, :, :], src[:, :, 1, :], ACT.Copy))
            VE.wait(a)
            x = VE.mark(tt(PC[:, :, :], src[:, :, 0, :], PL[:, :, :], ALU.add))
            free[b] = (x,)
            tab = cst_("cbias").rearrange("p (u c) -> p u c", u=16)
            VE.wait(x)
            x = VE.mark(tt(PC[:, :, :], PC[:, :, :], tab, ALU.add))
            VE.wait(x)
            x = VE.mark(red(cs[:, 0, :], PC[:, :, :], ALU.max))
            yield

            def wide(t):
                return t.unsqueeze(2).to_broadcast([128, 16, 16])

            VE.wait(x)
            x = VE.mark(tt(PC[:, :, :], PC[:, :, :], wide(cs[:, 0, :]), ALU.subtract))
            SC.wait(x)
            a = SC.mark(act(PC[:, :, :], PC[:, :, :], ACT.Exp))
            VE.wait(a)
            x = VE.mark(tt(PC[:, :, :], PC[:, :, :], cst_("cmask").rearrange("p (u c) -> p u c", u=16), ALU.mult))
            VE.wait(x)
            x = VE.mark(red(cs[:, 1, :], PC[:, :, :], ALU.add))
            yield
            VE.wait(x)
            x = VE.mark(ts(cs[:, 1, :], cs[:, 1, :], 1e-30, ALU.max))
            VE.wait(x)
            x = VE.mark(recip(cs[:, 1, :], cs[:, 1, :]))
            VE.wait(x, *m_gate)
            x = VE.mark(tt(cs[:, 2, :].rearrange("p (q h) -> p q h", q=2), cs[:, 1, :].rearrange("p (q h) -> p q h", q=2),
                           ga[:, :, 0:24:3], ALU.mult))
            VE.wait(x)
            x = VE.mark(tt(PC[:, :, :], PC[:, :, :], wide(cs[:, 2, :]), ALU.mult))
            yield
            PE.wait(x, *free[b])
            for qt in range(2):
                m = PE.mark(tp(BK[b][:, 128 * qt:128 * qt + 128],
                               PC[:, 8 * qt:8 * qt + 8, :].rearrange("p a b -> p (a b)"), ident))
            SC.wait(m)
            x = SC.mark(act(PCT[:, :], BK[b][:, 0:256], ACT.Copy))
            free[b] = (x,)
            m_pct.append(x)

        m_pct = []

        pu_free, pv_free, pv_ready, ot_ready = {}, {}, {}, {}
        u_n = [0]

        def head_attention(kind, h):
            g = h // 4
            nb = 2 - kind
            ring = (8 * kind + h) % 2
            us = [u_n[0], u_n[0] + 1]
            u_n[0] += 2
            nm, su, sc = [[st[:, u % 8, 2 * i:2 * i + nb] for u in us] for i in range(3)]
            y = {}

            def scores(qt):
                u = us[qt]
                b = 2 + u % 2
                n = 128 * (qt + 1)
                PE.wait(*free[b])
                if kind == 0:
                    PE.wait(*qn_ready[h], *kn_ready[g], m_tabs[0])
                    q = QN[:, h, 128 * qt:128 * qt + 128]
                    PE.do(mm(BK[b][:, :], q, KNH[:, g, :], True, False, True))
                    PE.do(mm(BK[b][:, :], q, KNL[:, g, :], False, False, True))
                    for i in range(2):
                        m = PE.mark(mm(BK[b][:, 256 * i:256 * i + n], slopes[:, h, :], alibi[:, 0:n] if qt else
                                       alibi[:, 128:256], False, i == 1, True))
                else:
                    PE.wait(*qf_ready[h], *kf_ready[h], *m_ctb, m_tabs[0])
                    q = QF[:, h, 128 * qt:128 * qt + 128]
                    PE.do(mm(BK[b][:, 0:256], q, KFH[:, h, :], True, False, True))
                    PE.do(mm(BK[b][:, 0:256], q, KFL[:, h, :], False, False, True))
                    PE.do(mm(BK[b][:, 0:n], pick[:, h, :], CTB[:, 0:n], False, False, True))
                    m = PE.mark(mm(BK[b][:, n - 128:n], identb[:, :], maskb[:, 0, :], False, True, True))
                VE.wait(m, *pu_free.get(u - 8, ()))
                src = BK[b][:, 0:256 * nb].rearrange("p (i n) -> p i n", i=nb)[:, :, 0:n]
                x = VE.mark(red(nm[qt], src, ALU.max, negate=True))
                SC.wait(x, *fork2, *pu_free.get(u - 4, ()))
                for i in range(nb):
                    y[qt] = SC.mark(act(PU[:, u % 4, n * i:n * i + n], BK[b][:, 256 * i:256 * i + n], ACT.Exp,
                                        bias=nm[qt][:, i:i + 1], accum_out=su[qt][:, i:i + 1]))
                free[b] = (y[qt],)

            def scale(qt):
                VE.wait(y[qt])
                n = 128 * (qt + 1)
                x = VE.mark(recip(sc[qt], su[qt]))
                if kind == 0:
                    VE.wait(x, *m_gate)
                    x = VE.mark(tt(sc[qt], sc[qt], ga[:, qt, 3 * h + 1:3 * h + 3], ALU.mult))
                VE.wait(x)
                for i in range(nb):
                    p = PU[:, us[qt] % 4, n * i:n * i + n]
                    y[qt] = VE.mark(ts(p, p, sc[qt][:, i:i + 1], ALU.mult))

            def turn(qt):
                u = us[qt]
                b = 4 + u % 2
                PE.wait(y[qt], *free[b])
                nt = qt + 1
                for i in range(nb):
                    for t in range(nt):
                        m = PE.mark(tp(BK[b][:, 128 * (i + nb * t):128 * (i + nb * t) + 128],
                                       PU[:, u % 4, 128 * (nt * i + t):128 * (nt * i + t) + 128], ident))
                pu_free[u] = (m,)
                L = SC if qt == 0 else VE
                L.wait(m, *fork2, *pv_free.get(8 * kind + h - 2, ()))
                ev = (lambda d, s: act(d, s, ACT.Copy)) if qt == 0 else cp
                d = PV[:, ring, 0:256 * nb].rearrange("p (i n) -> p i n", i=nb)[:, :, 128 * qt:128 * qt + 128]
                x = L.mark(ev(d, BK[b][:, 0:128 * nb].rearrange("p (i n) -> p i n", i=nb)))
                if qt:
                    x = L.mark(ev(PV[:, ring, 256 * nb:384 * nb], BK[b][:, 128 * nb:256 * nb]))
                free[b] = (x,)
                pv_ready.setdefault(8 * kind + h, []).append(x)

            scores(0)
            yield
            scale(0)
            scores(1)
            yield
            turn(0)
            scale(1)
            yield
            turn(1)
            yield
            if h % 2:
                c = h // 2
                PE.wait(*pv_ready[8 * kind + h - 1], *pv_ready[8 * kind + h], *free[6])
                if kind == 0:
                    PE.wait(*m_pct, m_vn)
                    PE.do(mm(BK[6][:, 0:256], VCX[:, 2 * c:2 * c + 2, :].rearrange("p a b -> p (a b)"), PCT[:, :],
                             True, False, True))
                else:
                    PE.wait(*m_vf)
                for i in range(nb):
                    for t in range(2):
                        for hh in range(2):
                            if kind == 0:
                                v = VN[:, t, 128 * i + 64 * g:128 * i + 64 * g + 64]
                            else:
                                v = VF[:, t, 64 * (2 * c + hh):64 * (2 * c + hh) + 64]
                            p = PV[:, hh, 256 * i:256 * i + 256] if t == 0 else \
                                PV[:, hh, 256 * nb + 128 * i:256 * nb + 128 * i + 128]
                            m = PE.mark(mm(BK[6][rows_of(hh), 128 * t:256], v, p, kind == 1 and i == 0 and t == 0,
                                           i == nb - 1 and t == 1, True))
                pv_free[8 * kind + h - 1] = pv_free[8 * kind + h] = (m,)
                SC.wait(m, *fork2)
                x = SC.mark(act(OT2[:, 4 * kind + c, :], BK[6][:, 0:256], ACT.Copy))
                free[6] = (x,)
                ot_ready[4 * kind + c] = (x,)

        fork2 = [(PE.sem, PE.count), (SC.sem, SC.count), (VE.sem, VE.count)]
        while not kc_ready:
            tick()
        tasks.append(compressed())

        def all_heads():
            for kind in range(2):
                for h in range(8):
                    while kind and (h not in kf_ready or h not in qf_ready or not m_vf):
                        yield
                    sub.append(head_attention(kind, h))
                    for _ in range(2):
                        step()
                        yield
            while sub:
                step()
                yield

        sub = []

        def step():
            for x in list(sub):
                if next(x, sub) is sub:
                    sub.remove(x)

        m_vf = []
        tasks.append(all_heads())
        for c in range(4):
            b = proj_bank()
            PE.wait(*free[b])
            m = project(BK[b][:, 0:256])
            SC.wait(m)
            for hh in range(2):
                h = 2 * c + hh
                kf_ready[h] = stack(KFH[:, h, :], KFL[:, h, :], BK[b][:, 0:256], hh, 1.0, True)
            free[b] = kf_ready[h][-1:]
            tick()
        for i in range(2):
            m_vf.append(by_rows(proj_bank(), VF[:, :, 256 * i:256 * i + 256]))
        queries(QF, qf_ready, fork2)
        a_free[0] = ((PE.sem, PE.count),)
        drain()
        heads_done = [(L.sem, L.count) for L in (PE, SC, VE)]

        A, B = BK[0], BK[1]
        PE.wait(*free[0], *free[1])
        for kind in range(2):
            for k in range(4):
                SC.wait(*ot_ready[4 * kind + k], *a_free[0])
                m = SC.mark(act(sq[:, 4 * kind + k, :], OT2[:, 4 * kind + k, :], ACT.Square))
                PE.wait(m)
                m = PE.mark(mm(A[32 * k:32 * k + 32, 256 * kind:256 * kind + 256], ones[:, :],
                               sq[:, 4 * kind + k, :], True, True))
        VE.wait(m)
        m = VE.mark(ts(part[:, :], A[:, :], 2.0, ALU.mult))
        free[0] = (m,)
        PE.wait(m)
        m = PE.mark(mm(B[:, :], sums[:, :], part[:, :], True, True))
        m = newton(B[:, :], m, 512, 1)
        src = lambda k: OT2[:, k, :]
        VE.wait(m)
        mg = [VE.mark(tt(src(k), src(k), rr[:, 256 * (k // 4):256 * (k // 4) + 256], ALU.mult)) for k in range(8)]
        modulate(src, lambda k: sq[:, k, :], mg, 0, lambda k: vec_("gn", k, 1), None)

        hr = at("hr", [128, 2, 1024], F32, B2)
        X3 = at("X3", [128, 3, 2, 1024], BF16, B2 + 8 * KB)
        XS = [at(f"XS{i}", [128, 8, 64], F32, o) for i, o in enumerate((B2 + 20 * KB, B2 + 22 * KB, offset["C"]))]
        G, LI, SG, AC0, AT, YF = [at(n, [128, 512], F32, B2 + (24 + 2 * i) * KB)
                                  for i, n in enumerate(("G", "LI", "SG", "AC0", "AT", "YF"))]
        AC1 = at("AC1", [128, 512], F32, offset["C"] + 2 * KB)
        YH, YL = [at(n, [128, 512], F32R, B2 + (34 + 2 * i) * KB) for i, n in enumerate(("YH", "YL"))]
        X_ = [at(f"X_{i}", [128, 1024], F32, B2 + (24 + 4 * i) * KB) for i in range(2)]
        ST = [at(f"ST{i}", [128, 256], BF16, B2 + 42 * KB + 512 * i) for i in range(3)]
        SE = [at(f"SE{i}", [128, 64], BF16, B2 + 43 * KB + 512 + 128 * i) for i in range(2)]
        BR = at("BR", [128, 32], F32, B2 + 43 * KB + 768)
        CI = at("CI", [128, 32], mybir.dt.int32, B2 + 43 * KB + 896)
        WR = at("WR", [128, 8, 32], F32, B2 + 46 * KB)
        CE = [at(f"CE{i}", [128, 256], F32R, o) for i, o in enumerate((B2 + 44 * KB, B2 + 45 * KB, offset["pick"]))]
        BU = at("BU", [128, 2048], BF16, B2 + 38 * KB)
        WT = at("WT", [128, 256], F32, offset["pick"] + KB)
        o = offset["slopes"]
        LG, GT, EQ, CU, EX, WW, PO = [at(n, [128, 2, 32], F32, o + 256 * i)
                                      for i, n in enumerate(("LG", "GT", "EQ", "CU", "EX", "WW", "PO"))]
        mx, ss, rt = [at(n, [128, 2, 8], F32, o + 1792 + 64 * i) for i, n in enumerate(("mx", "ss", "rt"))]
        W3 = at("W3", [128, 3, 2, 32], BF16, offset["alibi"])
        MK = at("MK", [128, 2, 32], BF16, offset["alibi"] + 384)
        WS = at("WS", [128, 4], F32, offset["small"])
        ZT16 = at("ZT16", [128, 256], BF16, offset["maskb"])

        s_moe = sem("s_moe")
        in_moe = (s_moe, 32)
        at_load[up_at[0, 0]] = [(heads_done, WR[:, :, :], w_router.rearrange("(k p) n -> p k n", p=128), s_moe),
                                (heads_done, BR[:, :], b_router, s_moe)]

        sel_ready, se_free = {}, {}

        def selector(e):
            GP.wait(*se_free.get(e - 2, ()), m_ones, in_c)
            sel_ready[e] = (GP.mark(tt(SE[e % 2][:, :], sel32[:, e:e + 1].to_broadcast([128, 64]),
                                       ones[:, 0:1].to_broadcast([128, 64]), ALU.mult)),)

        GP.wait(in_moe, *heads_done)
        m_wr = GP.mark(tt(WR[:, :, :], WR[:, :, :], vec_("ln2").unsqueeze(2).to_broadcast([128, 8, 32]), ALU.mult))
        m_zt = GP.mark(cp(ZT16[:, :], cst_("zto", 128, 256)))
        selector(0)
        selector(1)

        def bias_parts():
            src = slot(bias_at)
            x = VE.mark(fill(BU[32:64, :], 0.0))
            SC.wait(loaded(bias_at), (VE.sem, VE.count))
            SC.do(act(BU[0:32, :], src[0:32, :], ACT.Copy))
            a = SC.mark(act(BU[64:128, :], src[64:128, :], ACT.Copy))
            for r in (slice(64, 128), slice(96, 128)):
                yield
                VE.wait(a)
                x = VE.mark(tt(src[r, :], src[r, :], BU[r, :], ALU.subtract))
                yield
                SC.wait(x)
                a = SC.mark(act(BU[r, :], src[r, :], ACT.Copy))
            m_bu.extend((a, x))

        m_bu = []
        tasks.append(bias_parts())
        for k in range(8):
            for _ in contract(AH[:, k, :], AL[:, k, :], a_ready[0][k], k == 0, k == 7):
                pass
            tick()
        drain()
        a_free[0] = ((PE.sem, PE.count),)
        for dc in range(8):
            VE.wait(y_marks[dc // 2])
            m = VE.mark(tt(hT[:, dc, :], Y(dc), hT[:, dc, :], ALU.add))
            h_ready[dc] = (m,)
            if dc % 2:
                free[4 + dc // 2] = (m,)

        w_out_done = fork = [(PE.sem, PE.count), (SC.sem, SC.count), (VE.sem, VE.count)]
        A, B, T, D = 0, 1, 2, 3
        for dc in range(8):
            PE.wait(*h_ready[dc])
            for q in range(2):
                b = 2 * q + dc // 4
                if dc % 4 == 0:
                    PE.wait(*free[b])
                m = PE.mark(tp(BK[b][:, 128 * (dc % 4):128 * (dc % 4) + 128], hT[:, dc, 128 * q:128 * q + 128], ident))
            if dc % 4 == 3:
                half_ = dc // 4
                for q in range(2):
                    SC.wait(m, *fork)
                    a = SC.mark(act((G, LI, SG, AT)[dc // 4 + 2 * q][:, :], BK[2 * q + half_][:, :], ACT.Square,
                                    accum_out=ss[:, q, half_:half_ + 1]))
                    VE.wait(a, *fork)
                    x = VE.mark(cp(hr[:, q, 512 * half_:512 * half_ + 512], BK[2 * q + half_][:, :]))
                    free[2 * q + half_] = (x,)
        PE.wait(m_wr, *free[4])
        for dc in range(8):
            for q in range(2):
                m2 = PE.mark(mm(BK[4][:, 32 * q:32 * q + 32], hT[:, dc, 128 * q:128 * q + 128], WR[:, dc, :],
                                dc == 0 and q == 0, dc == 7, True))
        h_free = (m2,)
        VE.wait(a)
        x = VE.mark(tt(rt[:, :, 0], ss[:, :, 0], ss[:, :, 1], ALU.add))
        VE.wait(x)
        x = VE.mark(ts(rt[:, :, 0], rt[:, :, 0], 1.0 / 1024.0, ALU.mult, EPS, ALU.add))
        GP.wait(x, m_half, (GP.sem, GP.count))
        m_rt = GP.mark(tt(rt[:, :, 1], rt[:, :, 0], cols[:, 1:2].to_broadcast([128, 2]), ALU.pow))
        VE.wait(m_rt, m2)
        for q in range(2):
            x = VE.mark(stt(LG[:, q, :], BK[4][:, 32 * q:32 * q + 32], rt[:, q, 1:2], BR[:, :], ALU.mult, ALU.add))
        free[4] = (x,)
        VE.wait(x)
        for q in range(2):
            x = VE.mark(lambda e, q=q: e.max(mx[:, q, :], LG[:, q, :]))
        SC.wait(m_rt, *free[3])
        x3 = {}
        for q in range(2):
            x3[0, q] = (SC.mark(act(X3[:, 0, q, :], hr[:, q, :], ACT.Copy, scale=rt[:, q, 1:2])),)
        VE.wait(x)
        for q in range(2):
            VE.do(ts(GT[:, q, :], LG[:, q, :], mx[:, q, 3:4], ALU.is_gt, 0.0, ALU.add, accum_out=rt[:, q, 2:3]))
        g = VE.mark(tt(EQ[:, :, :], LG[:, :, :], mx[:, :, 3:4].to_broadcast([128, 2, 32]), ALU.is_equal))
        VE.wait(g)
        for q in range(2):
            x = VE.mark(lambda e, q=q: e.tensor_tensor_scan(CU[:, q, :], EQ[:, q, :], ones[:, :], rt[:, q, 2:3], ALU.add,
                                                            ALU.mult))
        VE.wait(x)
        x = VE.mark(stt(EQ[:, :, :], CU[:, :, :], 4.0, EQ[:, :, :], ALU.is_le, ALU.mult))
        VE.wait(x)
        VE.wait(*fork)
        m_sel = VE.mark(tt(MK[:, :, :], GT[:, :, :], EQ[:, :, :], ALU.add))
        PE.wait(m_sel, m_zt, *free[5])
        tri, one = ZT16[:, 0:128], ZT16[:, 128:256]
        PE.do(mm(BK[5][:, 0:32], tri, MK[:, 0, :], True, True, True))
        PE.do(mm(BK[5][:, 32:64], one, MK[:, 0, :], False, False, True))
        PE.do(mm(BK[5][:, 32:64], tri, MK[:, 1, :], False, True, True))
        for q in range(2):
            m = PE.mark(mm(BK[5][:, 64:96], one, MK[:, q, :], False, q == 1, True))

        def x3_rest(q, p):
            L = GP if (q, p) == (0, 2) else VE
            L.wait(*x3[p - 1, q])
            hi = X3[:, p - 1, q, :]
            if p == 1:
                x = VE.mark(stt(X_[q][:, :], hr[:, q, :], rt[:, q, 1:2], hi, ALU.mult, ALU.subtract))
            else:
                x = L.mark(tt(X_[q][:, :], X_[q][:, :], hi, ALU.subtract))
            SC.wait(x)
            x3[p, q] = (SC.mark(act(X3[:, p, q, :], X_[q][:, :], ACT.Copy)),)

        x3_rest(0, 1)
        VE.wait(m)
        m_po = VE.mark(tt(PO[:, :, :], BK[5][:, 0:64].rearrange("p (q n) -> p q n", q=2), MK[:, :, :], ALU.mult))
        m_ci = VE.mark(cp(CI[:, :], BK[5][:, 64:96]))
        free[5] = (m_ci,)
        x = VE.mark(tt(LG[:, :, :], LG[:, :, :], mx[:, :, 0:1].to_broadcast([128, 2, 32]), ALU.subtract))
        SC.wait(x)
        a = SC.mark(act(EX[:, :, :], LG[:, :, :], ACT.Exp))
        m_ww, m_w3 = [], []

        def weights():
            VE.wait(a)
            x = VE.mark(tt(WW[:, :, :], EX[:, :, :], MK[:, :, :], ALU.mult))
            VE.wait(x)
            x = VE.mark(red(rt[:, :, 3], WW[:, :, :], ALU.add))
            VE.wait(x)
            x = VE.mark(recip(rt[:, :, 4], rt[:, :, 3]))
            VE.wait(x)
            x = VE.mark(tt(WW[:, :, :], WW[:, :, :], rt[:, :, 4:5].to_broadcast([128, 2, 32]), ALU.mult))
            m_ww.append(x)
            for p in range(3):
                VE.wait(x)
                x = VE.mark(cp(W3[:, p, :, :], WW[:, :, :] if p == 0 else LG[:, :, :]))
                if p < 2:
                    VE.wait(x)
                    x = VE.mark(tt(LG[:, :, :], LG[:, :, :] if p else WW[:, :, :], W3[:, p, :, :], ALU.subtract))
            m_w3.append(x)

        st_free, ce_free, xs_free, ac_free = [[()] * 3 for _ in range(4)]
        one_free = {"AT": (), "Y": (), "G": (), "LI": (), "SG": ()}
        ce_ready, xs_ready, ac_ready, st_ready, ws_ready = [[()] * 3 for _ in range(5)]

        def onehot(e, first, n, u):
            VE.wait(m_po, in_c2, *st_free[u])
            shape = [128, 2, 128 // n, n]
            x = VE.mark(tt(ST[u][:, :].rearrange("p (q a s) -> p q a s", q=2, s=n),
                           cst_("iota", first, n).unsqueeze(1).unsqueeze(1).to_broadcast(shape),
                           PO[:, :, e:e + 1].unsqueeze(3).to_broadcast(shape), ALU.is_equal))
            st_ready[u] = (x,)

        def gather(u, n=64):
            PE.wait(*st_ready[u], *free[T])
            for p in range(3):
                for k in range(8):
                    for q in range(2):
                        PE.wait(*x3[p, q])
                        m = PE.mark(mm(BK[T][:, n * k:n * k + n], X3[:, p, q, 128 * k:128 * k + 128],
                                       ST[u][:, 128 * q:128 * q + n],
                                       p == 0 and k == 0 and q == 0, p == 2 and q == 1, True))
            VE.wait(m, *xs_free[u])
            x = VE.mark(tt(XS[u][:, :, 0:n], BK[T][:, 0:8 * n].rearrange("p (k n) -> p k n", k=8),
                           vec_("ln2").unsqueeze(2).to_broadcast([128, 8, n]), ALU.mult))
            free[T] = (x,)
            xs_ready[u] = (x,)

        def turn_onehot(e, u):
            PE.wait(*st_ready[u], *free[T])
            s = [ST[u][:, 128 * q:128 * q + 128] for q in range(2)]
            for q in range(2):
                PE.do(mm(BK[T][:, 128 * q:128 * q + 128], s[q], identb[:, :], q == 0, True, True))
            PE.wait(*m_w3)
            for i in range(6):
                m = PE.mark(mm(BK[T][:, 256:257], s[i % 2], W3[:, i // 2, i % 2, e:e + 1], False, i == 5, True))
            st_free[u] = (m,)
            SC.wait(m, *ce_free[u])
            SC.do(act(CE[u][:, :], BK[T][:, 0:256], ACT.Copy))
            x = SC.mark(act(WS[:, u:u + 1], BK[T][:, 256:257], ACT.Copy))
            free[T] = (x,)
            ce_ready[u] = (x,)

        def side(r, s, n):
            return BK[r][n * s:n * s + n, 0:8 * n]

        def bias(e, n=64):
            PE.wait(*sel_ready[e], *m_bu, *free[A], *free[B])
            a = 128 // n
            for i in range(2 * a):
                m = PE.mark(mm(side(A + i // a, i % a, n), SE[e % 2][:, 0:n], BU[:, 8 * n * i:8 * n * i + 8 * n],
                               True, False, True))

        def up(e, k, u, n=64):
            i = up_at[e, k]
            PE.wait(loaded(i), *xs_ready[u])
            a = 128 // n
            for c in range(2 * a):
                m = PE.mark(mm(side(A + c // a, c % a, n), XS[u][:, k, 0:n], slot(i)[:, 8 * n * c:8 * n * c + 8 * n],
                               False, k == 7, True))
            raw_free[i] = (m,)
            if k == 7:
                xs_free[u] = (m,)
            return m

        def swiglu(m, g_, li, sg, w=512):
            VE.wait(m, *one_free["G"])
            g = VE.mark(ts(g_[:, 0:w], BK[A][:, 0:w], 7.0, ALU.min))
            free[A] = (g,)
            SC.wait(g, *one_free["SG"])
            s = SC.mark(act(sg[:, 0:w], g_[:, 0:w], ACT.Sigmoid, scale=1.702))
            VE.wait(*one_free["LI"])
            x = VE.mark(ts(li[:, 0:w], BK[B][:, 0:w], 7.0, ALU.min, -7.0, ALU.max))
            free[B] = (x,)
            return g, s, x

        def swiglu_end(marks, u, ac, g_, li, sg, w=512):
            g, s, x = marks
            VE.wait(g, x)
            x = VE.mark(stt(li[:, 0:w], li[:, 0:w], 1.0, g_[:, 0:w], ALU.add, ALU.mult))
            VE.wait(x, s, *ce_ready[u], *ac_free[u // 2])
            y = VE.mark(stt(ac[:, 0:w], li[:, 0:w], WS[:, u:u + 1], sg[:, 0:w], ALU.mult, ALU.mult))
            one_free["G"], one_free["LI"], one_free["SG"] = (x, s), (y,), (y,)
            ac_ready[u // 2] = (y,)

        def turn(v, w=512):
            PE.wait(*ac_ready[v], *free[T])
            for q in range(w // 128):
                m = PE.mark(tp(BK[T][:, 128 * q:128 * q + 128], (AC0, AC1)[v][:, 128 * q:128 * q + 128], ident))
            ac_free[v] = (m,)
            SC.wait(m, *one_free["AT"])
            x = SC.mark(act(AT[:, 0:w], BK[T][:, 0:w], ACT.Copy))
            free[T] = (x,)
            return x

        def down_expert(e, ready, meanwhile=None, n=64):
            PE.wait(ready, *free[D])
            a, w = 128 // n, 8 * n
            for k in range(8):
                i = down_at[e, k // 2]
                PE.wait(loaded(i))
                o = 128 * (k % (w // 128)) + n * (k // (w // 128))
                for c in range(a):
                    s = 1024 * (k % 2) + w * c
                    m = PE.mark(mm(side(D, c, n), AT[:, o:o + n], slot(i)[:, s:s + w], k == 0, k == 7, True))
                raw_free[i] = (m,)
            one_free["AT"] = (m,)
            if meanwhile:
                next(meanwhile)
            SC.wait(m, *one_free["Y"])
            x = SC.mark(act(YH[:, 0:w], BK[D][:, 0:w], ACT.Copy))
            VE.wait(x, *one_free["Y"])
            y = VE.mark(tt(YL[:, 0:w], BK[D][:, 0:w], YH[:, 0:w].bitcast(F32), ALU.subtract))
            free[D] = (y,)
            if meanwhile:
                next(meanwhile, None)
            return (x, y)

        def combine(u, ready, last=False, n=64):
            PE.wait(*ready, *ce_ready[u])
            w = 8 * n
            for c0 in range(512 // w):
                for q in range(2):
                    for h_ in range(2):
                        c = c0 + 512 // w * h_
                        r = slice(n * c, n * c + n)
                        for y in (YH, YL):
                            m = PE.mark(mm(BK[4 + 2 * q + h_][:, w * c0:w * c0 + w], CE[u][r, 128 * q:128 * q + 128],
                                           y[r, 0:w], False, last and y is YL, True))
                PE.wait(m)
            one_free["Y"] = ce_free[u] = (m,)
            return m

        sooner = {}
        MORE = ((64, 32), (96, 64), (160, 64), (224, 32))

        def more_tokens(e, i=0):
            first, n = MORE[i]
            before = free[T]
            for k in range(8):
                if up_at[e, k] in (sooner if i else raw_free):
                    sooner.setdefault(up_at[e, k], []).append((e, first, raw_free[up_at[e, k]]))
            with Branch((PE, SC, VE), count, first):
                kept = {k: one_free[k] for k in ("G", "LI", "SG")}
                onehot(e, first, n, 2)
                gather(2, n)
                turn_onehot(e, 2)
                bias(e, n)
                for k in range(8):
                    m = up(e, k, 2, n)
                one_free["G"], one_free["LI"], one_free["SG"] = one_free["AT"], one_free["Y"], ac_free[1]
                marks = swiglu(m, AT, YF, AC1, 8 * n)
                swiglu_end(marks, 2, AC1, AT, YF, AC1, 8 * n)
                one_free["AT"], one_free["Y"] = one_free["G"], one_free["LI"]
                combine(2, down_expert(e, turn(1, 8 * n), None, n), False, n)
                if i + 1 < len(MORE):
                    more_tokens(e, i + 1)
                one_free.update(kept)
            free[T] = (*before, *free[T])

        def bias_down():
            PE.wait(*m_ww, *free[T])
            for q in range(2):
                m = PE.mark(mm(BK[T][32:64, 128 * q:128 * q + 128], WW[:, q, :], ident, q == 0, True, True))
            VE.wait(m)
            x = VE.mark(cp(WT[32:64, :], BK[T][32:64, 0:256]))
            free[T] = (x,)
            PE.wait(x)
            for q in range(2):
                for n in range(2):
                    m = PE.mark(mm(BK[4 + 2 * q + n][:, :], WT[32:64, 128 * q:128 * q + 128],
                                   slot(bias_at)[32:64, 512 * n:512 * n + 512], False, False, True))
            raw_free[bias_at] = (m,)

        PQ = [slot(pt_at)[:, 512:1536], slot(wple_at)[:, 0:1024]]

        def ple_products():
            PE.wait(loaded(wple_at), loaded(pt_at))
            for q in range(2):
                for n, b in enumerate((T, D)):
                    PE.wait(*free[b])
                    for k in range(2):
                        m = PE.mark(mm(BK[b][:, :], slot(pt_at)[:, 256 * k + 128 * q:256 * k + 128 * q + 128],
                                       slot(wple_at)[:, 1024 * k + 512 * n:1024 * k + 512 * n + 512], k == 0, k == 1))
                    SC.wait(m)
                    x = SC.mark(act(PQ[q][:, 512 * n:512 * n + 512], BK[b][:, :], ACT.Copy))
                    free[b] = (x,)
                    pq_ready.append(x)

        pq_ready = []
        count = {}
        GH, GL = {}, {}

        def split_gate():
            for n in range(8):
                if n in (2, 6):
                    yield
                i = gate_at[n // 2]
                c = slice(1024 * (n % 2), 1024 * (n % 2) + 1024)
                GH[n], GL[n] = slot(kept_ups[n // 2], F32R)[:, c], slot(i, F32R)[:, c]
                SC.wait(loaded(i), last_up)
                a_ = SC.mark(act(GH[n], slot(i)[:, c], ACT.Copy))
                L = GP if n in (4, 5, 7) else VE
                L.wait(a_, last_up)
                x = L.mark(tt(GL[n], slot(i)[:, c], GH[n].bitcast(F32), ALU.subtract))
                gate_ready.append((a_, x))

        gate_ready, gate_parts = [], split_gate()
        kept_ups = [up_at[NE - 1, k] for k in range(8)
                    if place[up_at[NE - 1, k]] not in [place[i] for i in (*gate_at, lnf_at)]]

        def counts(e, lines=(PE, SC, VE)):
            for L in lines:
                L.wait(m_ci)
                L.do(lambda x, L=L: count.__setitem__(id(L), x.value_load(CI[0:1, e:e + 1], min_val=0, max_val=256)))

        m_0 = GP.mark(fill(ST[2][:, 0:128], 0.0))
        onehot(0, 0, 64, 0)
        st_free[2] = (m_0,)
        PE.wait(m_0, *m_bu)
        for b in range(4, 8):
            PE.wait(*free[b])
            m = PE.mark(mm(BK[b][:, :], ST[2][:, 0:128], BU[:, 0:512], True, False, True))
        st_free[2] = (m,)
        x3_rest(1, 1)
        x3_rest(0, 2)
        x3_rest(1, 2)
        weights()
        gather(0)
        turn_onehot(0, 0)
        for e in range(NE + 1):
            u, w = e % 2, 1 - e % 2
            if e == 0:
                counts(e)
                more_tokens(e)
            if e < NE:
                bias(e)
                up(e, 0, u)
                up(e, 1, u)
            if e:
                swiglu_end(marks, w, AC0, G, LI, SG)
                x = turn(0)
            if e < NE:
                up(e, 2, u)
            if e:
                y = down_expert(e - 1, x, gate_parts if e == NE else None)
            if e == NE:
                y_done = combine(w, y, True)
                break
            if e == 0:
                bias_down()
            up(e, 3, u)
            if 0 < e < NE - 1:
                onehot(e + 1, 0, 64, w)
                gather(w)
            up(e, 4, u)
            if e == NE - 2:
                ple_products()
            for k in range(5, 8):
                m = up(e, k, u)
            marks = swiglu(m, G, LI, SG)
            if e:
                combine(w, y)
            if e == 0:
                onehot(e + 1, 0, 64, w)
                gather(w)
            if e + 1 < NE:
                turn_onehot(e + 1, w)
            if e:
                counts(e)
                more_tokens(e)
            last_up = (PE.sem, PE.count)
            se_free[e] = (last_up,)
            if e + 2 < NE:
                selector(e + 2)

        UH = at("UH", [128, 8, 256], F32R, B2 + 8 * KB)
        UL = at("UL", [128, 8, 256], F32R, B2 + 16 * KB)
        fork = [(PE.sem, PE.count), (SC.sem, SC.count), (VE.sem, VE.count)]

        def row_rstd(j, q, ready):
            VE.wait(*ready)
            x = VE.mark(tt(rt[:, q, j:j + 1], ss[:, q, 0:1], ss[:, q, 1:2], ALU.add))
            VE.wait(x)
            x = VE.mark(ts(rt[:, q, j:j + 1], rt[:, q, j:j + 1], 1.0 / 1024.0, ALU.mult, EPS, ALU.add))
            GP.wait(x, (GP.sem, GP.count))
            return GP.mark(tt(rt[:, q, j + 1:j + 2], rt[:, q, j:j + 1], cols[:, 1:2], ALU.pow))

        VE.wait(*fork)
        SC.wait(*fork)
        junk = (G, LI, AC0, AC1)
        u_ready = {}
        for q in range(2):
            for n in range(2):
                VE.wait(y_done)
                x = VE.mark(tt(hr[:, q, 512 * n:512 * n + 512], BK[4 + 2 * q + n][:, :], hr[:, q, 512 * n:512 * n + 512],
                               ALU.add))
                free[4 + 2 * q + n] = (x,)
                SC.wait(x)
                a = SC.mark(act(junk[2 * q + n][:, :], hr[:, q, 512 * n:512 * n + 512], ACT.Square,
                                accum_out=ss[:, q, n:n + 1]))
                PE.wait(x, *free[0], *free[1], *free[2], *free[3])
                for c in range(4):
                    k = 4 * n + c
                    m = PE.mark(tp(BK[k // 2][:, 256 * (k % 2) + 128 * q:256 * (k % 2) + 128 * q + 128],
                                   hr[:, q, 128 * k:128 * k + 128], ident))
                    u_ready[k] = (m,)
        m_rt = [row_rstd(5, q, (a,)) for q in range(2)]
        k_order = (0, 2, 1, 3, 4, 6, 5, 7)
        for k in k_order:
            src = BK[k // 2][:, 256 * (k % 2):256 * (k % 2) + 256]
            g = vec_("lnp", k, 1)
            SC.wait(*u_ready[k], *(u_ready[k - 1] if k % 2 else u_ready[k + 1]))
            a = SC.mark(act(UH[:, k, :], src, ACT.Copy, scale=g))
            VE.wait(a)
            x = VE.mark(stt(UL[:, k, :], src, g, UH[:, k, :].bitcast(F32), ALU.mult, ALU.subtract))
            u_ready[k] = (a, x)
        next(gate_parts, None)
        out_ready = []

        def res(q, c):
            return slot(kept_ups[4])[:, 1024 * q + c.start:1024 * q + c.stop]

        VE.wait(*pq_ready, loaded(lnf_at))
        SC.wait(*m_rt)
        for q in range(2):
            for n in range(2):
                b = 4 + 2 * q + n
                c = slice(512 * n, 512 * n + 512)
                h_, l_, t = hr[:, q, c], slot(lnf_at)[:, c], junk[2 * q + n][:, :]
                PE.wait(*free[b])
                for k in k_order:
                    PE.wait(*u_ready[k], *gate_ready[k])
                    m = PE.mark(mm3(BK[b][:, :], UH[:, k, 128 * q:128 * q + 128], UL[:, k, 128 * q:128 * q + 128],
                                    GH[k][:, c], GL[k][:, c], k == 0, k == 7))
                SC.wait(m)
                a = SC.mark(act(t, BK[b][:, :], ACT.Sigmoid, scale=rt[:, q, 6:7]))
                VE.wait(a)
                x = VE.mark(tt(t, t, PQ[q][:, c], ALU.mult))
                VE.wait(x)
                x = VE.mark(tt(h_, h_, t, ALU.add))
                SC.wait(x)
                a = SC.mark(act(t, h_, ACT.Square, accum_out=ss[:, q, n:n + 1]))
                VE.wait(x)
                x = VE.mark(tt(res(q, c), h_, l_, ALU.mult))
            m_rt = row_rstd(3, q, (a,))
            VE.wait(m_rt, x)
            SC.wait(m_rt, x)
            r0, r1 = res(q, slice(0, 512)), res(q, slice(512, 1024))
            out_ready.append((SC.mark(act(r1, r1, ACT.Copy, scale=rt[:, q, 4:5])),
                              VE.mark(ts(r0, r0, rt[:, q, 4:5], ALU.mult))))

        last_in = {r: first for rs, first in ((range(NR, NR + 7), heads_done), (range(NR + 7, NR + 11), w_out_done),
                                              ((NR + 11,), h_free)) for r in rs}
        read, last_of = set(), {}

        def wait_free(i):
            def later(x, levels):
                if levels:
                    (e, limit, marks), *rest = levels
                    for s, v in marks:
                        x.wait_ge(s, v)
                    with x.If(count[id(SP)] > limit):
                        later(x, rest)
                else:
                    for s, v in raw_free[i]:
                        x.wait_ge(s, v)

            if i in sooner:
                e = sooner[i][0][0]
                if e not in read:
                    counts(e, (SP,))
                    read.add(e)
                SP.do(lambda x: later(x, sooner[i]))
            else:
                SP.wait(*raw_free[i])

        for i, (pieces, value) in enumerate(loads):
            r = place[i]
            if r in last_of:
                wait_free(last_of[r])
            else:
                SP.wait(*last_in.get(r, ()))
            last_of[r] = i
            if i in at_load:
                for marks, d, src, sm in at_load[i]:
                    SP.wait(*marks)
                    SP.do(lambda e, d=d, src=src, sm=sm: e.dma_start(d, src).then_inc(sm, 16))
            for view, src in pieces:
                d = view(slots[F32][r][:, :])
                SP.do(lambda e, d=d, src=src, r=r: e.dma_start(d, src).then_inc(s_raw[r], 16))

        s_out = sem("s_out")
        for q in range(2):
            SP.wait(*out_ready[q])
            SP.do(lambda e, q=q: e.dma_start(out[0, 128 * q:128 * q + 128, :], res(q, slice(0, 1024))).then_inc(s_out, 16))
        SP.wait((s_out, 32))

        block = ctx.enter_context(nc.Block())

        @block.tensor
        def _(e):
            PE.run(e)

        @block.scalar
        def _(e):
            SC.run(e)

        @block.vector
        def _(e):
            VE.run(e)

        @block.gpsimd
        def _(e):
            GP.run(e)

        @block.sync
        def _(e):
            SP.run(e)


def pack(inputs):
    f = {k: np.asarray(v) for k, v in inputs.items()}

    def chunks(v):
        return v.reshape(-1, 128).T

    def rows(v):
        return np.broadcast_to(v.reshape(1, -1), (128, v.size))

    i = np.arange(128)
    cid = np.concatenate([np.eye(128), i[:, None] % 32 == np.arange(32)[None]], 1).astype(np.float32)
    cst1, cst2 = np.zeros((128, N1), np.float32), np.zeros((128, N2), np.float32)

    def c(name):
        if name in CST1:
            return cst1[:, CST1[name][0]:CST1[name][1]]
        return cst2[:, CST2[name][0]:CST2[name][1]]

    c("blk")[:] = (i[:, None] // 64 == i[None] // 64) / 64.0
    c("perm")[:] = i[:, None] == (i[None] ^ 32)
    t = np.arange(256)
    inv = np.power(np.float32(10000.0), -np.arange(16, dtype=np.float32) / np.float32(16.0))
    ang = np.concatenate([(t // 64).astype(np.float32)[None] * inv[:, None],
                          (t % 64).astype(np.float32)[None] * inv[:, None]], 0)
    c("cos")[:] = np.tile(np.cos(ang), (4, 1))
    c("sin")[:] = np.tile(np.concatenate([-np.sin(ang), np.sin(ang)], 0), (2, 1))
    c("m01")[:] = np.where(i[None] <= i[:, None], 0.0, NEG)
    c("m10")[:] = np.where(i[None] >= i[:, None], 0.0, NEG)
    c("hd")[:] = (i[:, None] // 64 == np.arange(32)[None]) / 64.0
    c("zto")[:, 128:256] = i[:, None] <= i[None]
    c("zto")[:, 256:384] = 1.0
    end = np.arange(16) * 16 + 31
    for qt in range(2):
        seen = (end[None] <= (128 * qt + i)[:, None]) & (np.arange(16) < 15)[None]
        for h in range(8):
            u = 16 * (8 * qt + h)
            c("cmask")[:, u:u + 16] = seen
            c("cbias")[:, u:u + 16] = np.where(seen, -2.0 ** -(h + 1) * ((128 * qt + i)[:, None] - end[None]), NEG)
    c("hrow")[:] = i[:, None] // 16 == np.arange(8)[None]
    c("alibi")[:] = np.where(t[None] <= 128 + i[:, None], t[None] - 128 - i[:, None], NEG)
    c("iota")[:] = t[None] + 1.0
    c("pick")[:] = (i[:, None] % 32 == np.arange(8)[None]) & (i[:, None] < 96)

    vec = np.zeros((128, NVEC), np.float32)

    def v(name):
        a, b = VEC[name]
        return vec[:, a:b]

    cc = v("cc").reshape(128, 8, 32)
    cc[:, :, 0] = chunks(f["c"][0])
    cc[:, :, 1] = chunks(f["c_ctx"])
    for l in range(2):
        v(f"nm{l}")[:] = chunks(f["norm_mix"][l])
        v(f"nf{l}")[:] = chunks(f["norm_ffn"][l])
        v(f"ada_b{l}")[:] = chunks(f["ada_b"][l])
        v(f"conv{l}")[:] = np.concatenate([chunks(f["ffn_conv"][l, j]) for j in range(3)], 1)
    v("scconv")[:] = np.concatenate([chunks(f["sc_conv"][0, j]) for j in range(3)], 1)
    v("qn")[:, 0] = np.tile(f["win_q_norm"][0], 2)
    v("kn")[:, 0] = np.tile(f["win_k_norm"][0], 2)
    v("sink")[:] = rows(f["win_sink"][0])
    v("ln1")[:] = chunks(f["ln1_2"][0])
    v("ln2")[:] = chunks(f["ln2_2"][0])
    v("lnp")[:] = chunks(f["ln_ple_2"][0])
    v("lnf")[:] = chunks(f["ln_f_2"])
    v("gn")[:] = np.concatenate([chunks(f["gn_nsa_2"][0]), chunks(f["gn_fox_2"][0])], 1)

    for n, x in enumerate("kv"):
        v(f"pe{n}")[:] = np.tile(f[f"pe_cmp_{x}_2"][0].T, (2, 1))
    v("bfg")[:] = rows(f["b_fg_2"][0])
    v("w2k")[:] = np.tile(f["w_cmp2_k_2"][0], (1, 2))
    v("w2v")[:] = f["w_cmp2_v_2"][0]

    def T(x):
        return np.ascontiguousarray(x.T.reshape(-1, 128, x.shape[0]).transpose(1, 0, 2))

    return dict(xT=T(f["x"][0]), ctxT=T(f["ctx"][0]), cid=cid, cst1=cst1, cst2=cst2, vec=vec, ada_w=f["ada_w"],
                w_qkv=f["win_w_qkv"][0], w_o=f["win_w_o"][0], w_up=f["ffn_w_up"], w_down=f["ffn_w_down"],
                sc_in=f["sc_w_in"][0], sc_out=f["sc_w_out"][0], w_in=f["w_in_2"][0],
                w_cmp1=np.stack([f["w_cmp1_k_2"][0], f["w_cmp1_v_2"][0]]), w_out=f["w_out_2"][0],
                moe_up=f["w_up_2"][0], moe_down=f["w_down_2"][0], b_up=f["b_up_2"][0], b_down=f["b_down_2"][0],
                w_router=f["w_router_2"][0], b_router=np.ascontiguousarray(rows(f["b_router_2"][0])),
                pT=T(f["p_2"][0, 0]), w_ple=f["w_ple_2"][0], w_gate=f["w_ple_gate_2"][0],
                ln_f=np.ascontiguousarray(rows(f["ln_f_2"])))


def kernel(**inputs):
    import concourse.bacc as bacc
    from concourse.bass_utils import run_bass_kernel_spmd

    nc = bacc.Bacc("TRN2", target_bir_lowering=False, num_devices=1)
    arrays = {n: np.ascontiguousarray(a) for n, a in pack(inputs).items()}
    args = {n: nc.dram_tensor(n, a.shape, mybir.dt.from_np(a.dtype), kind="ExternalInput").ap()
            for n, a in arrays.items()}
    out = nc.dram_tensor("out", (1, 256, 1024), F32, kind="ExternalOutput").ap()
    program(nc, out=out, **args)
    return run_bass_kernel_spmd(nc, [arrays], core_ids=[0]).results[0]["out"]
```

```python
import concourse.bass as bass
from concourse import mybir
from concourse.alu_op_type import AluOpType as ALU
from contextlib import ExitStack
import numpy as np

F32 = mybir.dt.float32
F32R = mybir.dt.float32r
BF16 = mybir.dt.bfloat16
ACT = mybir.ActivationFunctionType
AX = mybir.AxisListType

KB = 1024
BASE = 16 * KB + 128
EPS = 1e-6
NEG = -1e30


class Line:

    def __init__(self, sem):
        self.sem = sem
        self.count = 0
        self.ops = []
        self.seen = {}

    def do(self, f):
        self.ops.append(f)

    def mark(self, f):
        self.count += 1
        self.ops.append(lambda e: f(e).then_inc(self.sem, 1))
        return (self.sem, self.count)

    def wait(self, *marks):
        for sem, value in marks:
            if self.seen.get(id(sem), 0) < value:
                self.seen[id(sem)] = value
                self.ops.append(lambda e, s=sem, v=value: e.wait_ge(s, v))

    def run(self, e):
        for f in self.ops:
            f(e)


class Branch:

    def __init__(self, lines, count, limit):
        self.lines, self.count, self.limit = lines, count, limit

    def __enter__(self):
        self.before = [(L.ops, L.count, dict(L.seen)) for L in self.lines]
        for L in self.lines:
            L.ops = []

    def __exit__(self, *_):
        for L, (ops, before, seen) in zip(self.lines, self.before):
            body, L.ops, L.seen = L.ops, ops, seen
            L.ops.append(self.both(L, body, before, L.count - before))

    def both(self, L, body, before, added):
        def f(e):
            with e.If(self.count[id(L)] > self.limit):
                for g in body:
                    g(e)
            with e.Else():
                e.wait_ge(L.sem, before)
                e.sem_inc(L.sem, added)
        return f


def act(out, in_, func, **kw):
    return lambda e: e.activation(out, in_, func, **kw)


def tt(out, a, b, op):
    return lambda e: e.tensor_tensor(out, a, b, op)


def ts(out, a, s1, op0, s2=None, op1=None, **kw):
    if op1 is None:
        return lambda e: e.tensor_scalar(out, a, s1, None, op0, **kw)
    return lambda e: e.tensor_scalar(out, a, s1, s2, op0, op1, **kw)


def stt(out, a, s, b, op0, op1, **kw):
    return lambda e: e.scalar_tensor_tensor(out, a, s, b, op0, op1, **kw)


def cp(out, a):
    return lambda e: e.tensor_copy(out, a)


def fill(out, v):
    return lambda e: e.memset(out, v)


def red(out, a, op, **kw):
    return lambda e: e.tensor_reduce(out, a, AX.X, op, **kw)


def recip(out, a):
    return lambda e: e.reciprocal(out, a)


def mm(out, w, x, start, stop, skip=False):
    return lambda e: e.matmul(out, w, x, start=start, stop=stop, skip_group_check=skip)


def tp(out, a, ident):
    return lambda e: e.transpose(out, a, ident)


def dma(out, in_):
    return lambda e: e.dma_start(out, in_)


def layout(parts):
    at, out = 0, {}
    for name, n in parts:
        out[name] = (at, at + n)
        at += n
    return out, at


CST1, N1 = layout([("blk", 128), ("perm", 128), ("cos", 256), ("sin", 256), ("m01", 128), ("m10", 128), ("hd", 32)])
CST2, N2 = layout([("zto", 384), ("cbias", 256), ("cmask", 256), ("hrow", 8), ("alibi", 256), ("pick", 8), ("iota", 256)])
NC = max(N1, N2)
VEC, NVEC = layout([("cc", 256), ("nm0", 8), ("nm1", 8), ("nf0", 8), ("nf1", 8), ("ada_b0", 48), ("ada_b1", 48),
                    ("qn", 1), ("kn", 1), ("sink", 16), ("conv0", 132), ("conv1", 132), ("scconv", 24),
                    ("ln1", 8), ("ln2", 8), ("lnp", 8), ("lnf", 8), ("gn", 8), ("pe0", 32), ("pe1", 32), ("bfg", 8),
                    ("w2k", 128), ("w2v", 64)])


def program(nc, xT, ctxT, cid, cst1, cst2, vec, ada_w, w_qkv, w_o, w_up, w_down, sc_in, sc_out, w_in, w_cmp1, w_out, moe_up, moe_down,
            b_up, b_down, w_router, b_router, pT, w_ple, w_gate, ln_f, out):
    ctx = ExitStack()
    with ctx:
        def at(name, shape, dt, off):
            return nc.alloc_sbuf_tensor_at(name, shape, dt, offset=BASE + off)

        def sem(name):
            return ctx.enter_context(nc.semaphore(name))

        PE, SC, VE, GP, SP = [Line(sem("s_" + n)) for n in ("pe", "act", "dve", "pool", "sp")]

        BK = [ctx.enter_context(nc.psum_tensor(f"B{i}", [128, 512], F32)) for i in range(8)]
        free = [()] * 8
        rot = [0]

        def bank(n=4, first=0):
            rot[0] += 1
            return first + rot[0] % n

        def Y(dc):
            return BK[4 + dc // 2][:, 256 * (dc % 2):256 * (dc % 2) + 256]

        used, offset = [0], {}

        def put(name, shape, dt):
            size = 2 if dt == BF16 else 4
            for s in shape[1:]:
                size *= s
            t = at(name, shape, dt, used[0])
            offset[name] = used[0]
            used[0] += (size + 31) // 32 * 32
            return t

        ID = put("ID", [128, 160], F32)
        C = put("C", [128, NC], F32)
        V = put("V", [128, NVEC], F32)
        hT = put("hT", [128, 8, 256], F32)
        identb = put("identb", [128, 128], BF16)
        alibi = put("alibi", [128, 256], BF16)
        slopes = put("slopes", [128, 8, 128], BF16)
        pick = put("pick", [128, 8, 128], BF16)
        maskb = put("maskb", [128, 2, 128], BF16)
        sums = put("sums", [128, 128], F32)
        ones = put("ones", [128, 32], F32)
        cols = put("cols", [128, 2], F32)
        adaT = put("adaT", [128, 2, 48], F32)
        adaC = put("adaC", [128, 16], F32)
        modA = put("modA", [128, 2, 8], F32)
        small = put("small", [128, 4, 8], F32)
        nsink = put("nsink", [128, 16], F32)
        NR, NS = 6, 4
        RAW = put("RAW", [128, NR, 2048], F32)
        SH = put("SH", [128, NS, 1024], F32R)
        SL = put("SL", [128, NS, 1024], F32R)
        B2 = used[0]

        def cst_(n, i=0, w=None):
            a, b = CST1[n] if n in CST1 else CST2[n]
            return C[:, a + i:(b if w is None else a + i + w)]

        def vec_(n, i=0, w=None):
            a, b = VEC[n]
            return V[:, a + i:(b if w is None else a + i + w)]

        ident = ID[:, 0:128]
        sel32 = ID[:, 128:160]
        eps = cols[:, 0:1]

        tasks = []

        def tick():
            for g in list(tasks):
                if next(g, tasks) is tasks:
                    tasks.remove(g)

        def begin(g):
            next(g)
            tasks.append(g)

        def drain():
            while tasks:
                tick()

        loads, place, raw_count, raw_free = [], [], {}, {}
        halves, half_ready, half_free, split_marks = [], {}, {}, {}
        BUF = [offset["RAW"] + 8 * KB * i for i in range(NR)]
        BUF += [B2 + (47 + 8 * i) * KB for i in range(7)]
        BUF += [offset["SH"], offset["SH"] + 8 * KB, offset["SL"], offset["SL"] + 8 * KB, offset["hT"]]
        slots = {dt: [at(f"{n}{i}", [128, 2048], dt, o) for i, o in enumerate(BUF)] for n, dt in (("R", F32), ("RR", F32R))}
        s_raw = [sem(f"s_raw{i}") for i in range(len(BUF))]
        order = [list(range(NR))]

        first_of_moe = None

        def load(*pieces):
            i = len(loads)
            if not order[0]:
                order[0].append(place[next(used_up)])
            r = order[0].pop(0)
            if first_of_moe is None:
                order[0].append(r)
            place.append(r)
            raw_count[r] = raw_count.get(r, 0) + 16 * len(pieces)
            loads.append((pieces, raw_count[r]))
            return i

        def loaded(i):
            return (s_raw[place[i]], loads[i][1])

        def slot(i, dt=F32):
            return slots[dt][place[i]]

        def cols_slot(w, c0, c1=None, by_rows=False):
            c1 = c0 + 128 if c1 is None else c1
            src = w.rearrange("(k p) n -> p k n", p=128)
            view = lambda s: s.rearrange("p (k n) -> p k n", k=8)
            if c1 == c0 + 128:
                i = load((view, src[:, :, c0:c0 + 256]))
            else:
                i = load((lambda s: view(s)[:, :, 0:128], src[:, :, c0:c0 + 128]),
                         (lambda s: view(s)[:, :, 128:256], src[:, :, c1:c1 + 128]))
            for c in range(2):
                halves.append((i, c, not by_rows))

        def rows_slot(w, r0):
            i = load((lambda s: s.rearrange("p (k n) -> p k n", k=2),
                      w[r0:r0 + 256, :].rearrange("(k p) n -> p k n", p=128)))
            for c in range(2):
                halves.append((i, c, False))

        ada_at = {}

        def ada_slot(layer, n):
            ada_at[layer, n] = load((lambda s: s, ada_w[layer, 128 * (n % 8):128 * (n % 8) + 128,
                                                        2048 * (n // 8):2048 * (n // 8) + 2048]))

        prepared, taken, ahead = [0], [0], [NS]
        pattern = [(VE, GP)]
        lower = [(VE,)]

        def prepare(upto):
            while prepared[0] < min(upto, len(halves)):
                j = prepared[0]
                i, c, strided = halves[j]
                hi, lo = SH[:, j % NS, :], SL[:, j % NS, :]
                if c == "gf":
                    src = slot(i)[:, 0:256]
                    hi, lo = hi[:, 0:256], lo[:, 0:256]
                elif strided:
                    src = slot(i)[:, :].rearrange("p (k n) -> p k n", k=8)[:, :, 128 * c:128 * c + 128]
                    hi, lo = [x.rearrange("p (k n) -> p k n", k=8) for x in (hi, lo)]
                else:
                    src = slot(i)[:, 1024 * c:1024 * c + 1024]
                SC.wait(loaded(i), *half_free.get(j - NS, ()))
                m = SC.mark(act(hi, src, ACT.Copy))
                L = lower[0][j % len(lower[0])]
                L.wait(loaded(i), m, *half_free.get(j - NS, ()), *[(L.sem, L.count)] * (L is GP))
                n = L.mark(tt(lo, src, hi.bitcast(F32), ALU.subtract))
                half_ready[j] = (m, n)
                split_marks[i] = split_marks.get(i, ()) + (m, n)
                if c != 0:
                    raw_free[i] = split_marks[i]
                if j in adds:
                    ada_add(*divmod(adds[j], 2))
                prepared[0] += 1

        def half():
            j = taken[0]
            taken[0] += 1
            prepare(j + ahead[0])
            PE.wait(*half_ready[j])
            return j, (lambda a, n=128: SH[:, j % NS, a:a + n]), (lambda a, n=128: SL[:, j % NS, a:a + n])

        adds = {}

        def with_adds(first, n, offs=(0, 1)):
            for j in range(len(halves) - 2, len(halves)):
                if j % 3 in offs and first <= j and len(adds) < n:
                    if len(adds) % 2 == 0:
                        ada_slot(1, len(adds) // 2)
                    adds[j] = len(adds)

        for n in range(8):
            ada_slot(0, n)
        for P in range(4):
            cols_slot(w_qkv, 256 * P)
        cols_slot(w_qkv, 1024)
        cols_slot(w_qkv, 1280, by_rows=True)
        for P in range(4):
            ada_slot(0, 8 + 4 * P)
            ada_slot(0, 9 + 4 * P)
            rows_slot(w_o, 256 * P)
            ada_slot(0, 10 + 4 * P)
            ada_slot(0, 11 + 4 * P)
        first_of_ffn0, half0 = len(loads), len(halves)
        for layer in range(2):
            if layer == 1:
                half1 = len(halves)
                for P in range(4):
                    for g in range(3):
                        cols_slot(sc_in, 1024 * g + 256 * P)
                        with_adds(half1 + 8, 48)
                    if P:
                        rows_slot(sc_out, 256 * (P - 1))
                        with_adds(half1, 48)
                rows_slot(sc_out, 768)
            adding = lambda: with_adds(half0 + 10, 34) if layer == 0 else None
            for P in range(11):
                cols_slot(w_up[layer], 256 * P)
                adding()
                if P > 2:
                    rows_slot(w_down[layer], 256 * (P - 2))
                    adding()
                cols_slot(w_up[layer], 2816 + 256 * P)
                adding()
                if P == 2:
                    rows_slot(w_down[layer], 0)
                    adding()
            rows_slot(w_down[layer], 2304)
            rows_slot(w_down[layer], 2560)
        cols_slot(w_in, 512)
        cols_slot(w_in, 768, 1024)
        cols_slot(w_in, 896, 1152, by_rows=True)
        v = w_in.rearrange("(k p) n -> p k n", p=128)
        halves.append((load((lambda s: s[:, 0:256].rearrange("p (k n) -> p k n", k=8)[:, :, 0:24], v[:, :, 1280:1304]),
                            (lambda s: s[:, 0:256].rearrange("p (k n) -> p k n", k=8)[:, :, 24:32], v[:, :, 2840:2848])),
                       "gf", False))
        w1_at = [load((lambda s: s.rearrange("p (i n) -> p i n", i=16), w_cmp1[i].rearrange("(i p) n -> p i n", p=128)))
                 for i in range(2)]
        cols_slot(w_in, 0)
        cols_slot(w_in, 256)
        for c in (2328, 2584):
            cols_slot(w_in, c, by_rows=True)
        for c in (1816, 1304, 2072, 1560):
            cols_slot(w_in, c)
        for P in range(4):
            rows_slot(w_out, 256 * P)

        NE = 32
        order[0] = [*order[0][:2], NR, NR + 1, NR + 6, *order[0][2:4], *range(NR + 2, NR + 6), *order[0][4:],
                    *range(NR + 7, len(BUF))]
        up_at, down_at = {}, {}
        first_of_moe = len(loads)

        def in_order_of_use():
            for e in range(NE):
                for k in range(8):
                    yield up_at[e, k]
                    if k == 2 and e == 0:
                        yield bias_at
                    elif k == 2:
                        for n in range(4):
                            yield down_at[e - 1, n]

        used_up = in_order_of_use()
        two = lambda s: s.rearrange("p (k n) -> p k n", k=2)
        for e in range(NE):
            for k in range(8):
                if e == 0 and k == 2:
                    bias_at = load(*[(lambda s, r=r: s[r:r + 32, :], b_up) for r in (0, 64, 96)],
                                   (lambda s: s[32:64, 0:1024], b_down))
                if e == NE - 2 and k == 5:
                    wple_at = load((two, w_ple.rearrange("(k p) n -> p k n", p=128)))
                    pt_at = load((lambda s: s[:, 0:512].rearrange("p (k n) -> p k n", k=2), pT))
                up_at[e, k] = load((lambda s: s, moe_up[e, 128 * k:128 * k + 128, :]))
            for k in range(4):
                down_at[e, k] = load((two, moe_down[e, 256 * k:256 * k + 256, :].rearrange("(k p) n -> p k n", p=128)))
        gate_at = [load((two, w_gate[256 * k:256 * k + 256, :].rearrange("(k p) n -> p k n", p=128))) for k in range(4)]
        lnf_at = load((lambda s: s[:, 0:1024], ln_f))

        tmp, tmc = [at(n, [128, 8, 256], F32, B2 + i * 8 * KB) for i, n in enumerate(("tmp", "tmc"))]
        AH = at("AH", [128, 8, 512], F32R, B2 + 16 * KB)
        AL = at("AL", [128, 8, 512], F32R, B2 + 32 * KB)
        sq = at("sq", [128, 8, 512], F32, B2 + 48 * KB)
        part, vp, yy, zz, rr, adaS = [at(n, [128, 512], F32, B2 + (64 + 2 * i) * KB)
                                      for i, n in enumerate(("part", "vp", "yy", "zz", "rr", "adaS"))]

        s_in = [sem(f"s_in{i}") for i in range(5)]
        in_v, in_x, in_ctx, in_c, in_id = [(s, 16) for s in s_in]
        SP.do(lambda e: e.dma_start(V[:, :], vec).then_inc(s_in[0], 16))
        SP.do(lambda e: e.dma_start(ID[:, :], cid).then_inc(s_in[4], 16))
        at_load = {ada_at[0, 2]: [((), hT[:, :, :], xT, s_in[1])],
                   ada_at[0, 7] + 3: [((), tmc[:, :, :], ctxT, s_in[2]), ((), C[:, 0:N1], cst1, s_in[3])]}

        m_ones = VE.mark(fill(ones[:, :], 1.0))
        VE.do(fill(cols[:, 0:1], EPS))
        m_half = VE.mark(fill(cols[:, 1:2], -0.5))
        m_sums = VE.mark(fill(sums[:, :], 1.0 / 32768.0))
        SC.wait(in_v, m_sums)
        m_cc = SC.mark(act(vec_("cc"), vec_("cc"), ACT.Silu))
        LN_EXP = "natural_log_exp_and_others"
        SC.do(lambda e: e.preload_act_table_set(LN_EXP))
        VE.wait(in_id, in_v)
        VE.do(ts(nsink[:, :], vec_("sink"), -1.0, ALU.mult))
        VE.do(cp(identb[:, :], ident))

        def ada_burst(layer, slots, b):
            PE.wait(*free[b])
            for n in slots:
                i = ada_at[layer, n]
                PE.wait(loaded(i), m_cc)
                for j in range(4):
                    f = mm(BK[b][32 * j:32 * j + 32, :], V[:, 32 * (n % 8):32 * (n % 8) + 32],
                           slot(i)[:, 512 * j:512 * j + 512], n == slots[0], n == slots[-1])
                    if j < 3:
                        PE.do(f)
                    else:
                        raw_free[i] = (PE.mark(f),)
            VE.wait(*raw_free[i])
            if slots[0] % 8 == 0:
                m = VE.mark(cp(adaS[:, :], BK[b][:, :]))
            else:
                VE.wait((VE.sem, VE.count))
                m = VE.mark(tt(adaS[:, :], BK[b][:, :], adaS[:, :], ALU.add))
            free[b] = (m,)
            return m

        added, acc_last = [0], {}

        def ada_add(n, c):
            a = n // 8 % 2
            i = ada_at[1, n]
            col = V[:, 32 * (n % 8):32 * (n % 8) + 1]
            src, dst = [x[:, 1024 * c:1024 * c + 1024] for x in (slot(i), acc[a])]
            VE.wait(loaded(i), m_cc, *acc_last.get((a, c), ()))
            f = ts(dst, src, col, ALU.mult) if n % 8 == 0 else stt(dst, src, col, dst, ALU.mult, ALU.add)
            acc_last[a, c] = (VE.mark(f),)
            added[0] += 1
            if c:
                raw_free[i] = acc_last[a, c]

        def ada_sum(g, b):
            a = g % 2
            PE.wait(*free[b], *acc_last[a, 0], *acc_last[a, 1], m_ones)
            for j in range(4):
                m = PE.mark(mm(BK[b][32 * j:32 * j + 32, :], ones[:, :], acc[a][:, 512 * j:512 * j + 512], True, True))
            acc_last[a, 0] = acc_last[a, 1] = (m,)
            VE.wait(m)
            m = VE.mark(cp(adaS[:, :], BK[b][:, :]))
            free[b] = (m,)
            return m

        def ada_end(layer, g, m, b):
            PE.wait(m, in_id, *free[b])
            for q in range(4):
                f = tp(BK[b][:, 128 * q:128 * q + 128], adaS[:, 128 * q:128 * q + 128], ident)
                if q < 3:
                    PE.do(f)
                else:
                    m = PE.mark(f)
            VE.wait(m, in_v)
            dst = adaT[:, layer, 16 * g:16 * g + 16].rearrange("p (j b) -> p j b", b=4)
            bias = vec_(f"ada_b{layer}", 16 * g, 16).rearrange("p (j b) -> p j b", b=4)
            src = BK[b][:, :].rearrange("p (b j r) -> p r j b", b=4, r=32)
            m = VE.mark(tt(dst, src[:, 0], bias, ALU.add))
            if layer == 0 and g == 0:
                m = VE.mark(tt(adaC[:, :].rearrange("p (j b) -> p j b", b=4), src[:, 1], bias, ALU.add))
            free[b] = (m,)
            return m

        def ada_col(layer, i, k):
            return adaT[:, layer, 8 * i + k:8 * i + k + 1]

        def newton_steps(ms, m, n, b, scale=1.0):
            SC.wait(m)
            a = SC.mark(act(yy[:, 0:n], ms, ACT.Ln, bias=eps))
            VE.wait(a)
            v = VE.mark(ts(vp[:, 0:n], ms, EPS, ALU.add))
            free[b] = (v,)
            yield
            SC.wait(a)
            a = SC.mark(act(yy[:, 0:n], yy[:, 0:n], ACT.Exp, scale=-0.5))
            yield
            VE.wait(a)
            z = VE.mark(tt(zz[:, 0:n], yy[:, 0:n], yy[:, 0:n], ALU.mult))
            VE.wait(z)
            z = VE.mark(tt(zz[:, 0:n], zz[:, 0:n], vp[:, 0:n], ALU.mult))
            yield
            VE.wait(z)
            z = VE.mark(ts(zz[:, 0:n], zz[:, 0:n], -0.5 * scale, ALU.mult, 1.5 * scale, ALU.add))
            VE.wait(z)
            yield VE.mark(tt(rr[:, 0:n], yy[:, 0:n], zz[:, 0:n], ALU.mult))

        def newton(*args, **kw):
            return list(newton_steps(*args, **kw))[-1]

        def rstd(src, ready, b0, b1, o):
            A, B, n = BK[b0], BK[b1], 256
            PE.wait(m_ones, m_sums, *free[b0])
            for k in range(8):
                SC.wait(*ready[k])
                m = SC.mark(act(sq[:, k, o:o + n], src(k), ACT.Square))
                PE.wait(m)
                f = mm(A[32 * (k % 4):32 * (k % 4) + 32, 0:n], ones[:, :], sq[:, k, o:o + n], k < 4, k >= 4)
                if k < 7:
                    PE.do(f)
                else:
                    m = PE.mark(f)
            VE.wait(m)
            m = VE.mark(cp(part[:, 0:n], A[:, 0:n]))
            free[b0] = (m,)
            PE.wait(m, *free[b1])
            m = PE.mark(mm(B[:, 0:n], sums[:, :], part[:, 0:n], True, True))
            return newton(B[:, 0:n], m, n, b1)

        a_ready = [[()] * 8, [()] * 8]
        a_free = [()]

        def scaled(src, dst):
            return [VE.mark(tt(dst(k), src(k), rr[:, 0:256], ALU.mult)) for k in range(8)]

        def modulate(t, u, m, o, A, Bv, ks, odd=GP):
            h, x = {}, {}

            def low(k):
                L = odd if k % 2 else VE
                L.wait(h[k], x[k], *a_free[0])
                l = L.mark(tt(AL[:, k, o:o + 256], u(k), AH[:, k, o:o + 256].bitcast(F32), ALU.subtract))
                a_ready[o // 256][k] = (h[k], l)

            for k in ks:
                SC.wait(m[k], m_ab, *a_free[0])
                VE.wait(m[k], m_ab, *a_free[0])
                if Bv is None:
                    h[k] = SC.mark(act(AH[:, k, o:o + 256], t(k), ACT.Copy, scale=A(k)))
                    x[k] = VE.mark(ts(u(k), t(k), A(k), ALU.mult))
                else:
                    h[k] = SC.mark(act(AH[:, k, o:o + 256], t(k), ACT.Identity, scale=A(k), bias=Bv(k)))
                    x[k] = VE.mark(ts(u(k), t(k), A(k), ALU.mult, Bv(k), ALU.add))
                if k > ks[0]:
                    low(k - 1)
            low(ks[-1])

        def mm3(out, wh, wl, xh, xl, start, stop, skip=False):
            PE.do(mm(out, wh, xh, start, False, skip))
            PE.do(mm(out, wh, xl, False, False, skip))
            return mm(out, wl, xh, False, stop, skip)

        def project(out, moving=((0, 0),), between=None):
            j, wh, wl = half()
            for a, o in moving:
                for k in range(8):
                    PE.wait(*a_ready[o // 256][k])
                    f = mm3(out[:, a:a + 256], wh(128 * k), wl(128 * k), AH[:, k, o:o + 256], AL[:, k, o:o + 256],
                            k == 0, k == 7)
                    if k < 7:
                        PE.do(f)
                    else:
                        m = PE.mark(f)
                    if k == 3 and between:
                        between()
            half_free[j] = (m,)
            return m

        def pair(b, together=False):
            if not together:
                return [project(BK[b][:, 256 * c:256 * c + 256]) for c in range(2)][-1]
            prepare(taken[0] + NS)
            ahead[0] = 0
            js = [half() for _ in range(2)]
            ahead[0] = NS
            for k in range(8):
                PE.wait(*a_ready[0][k])
                for c, (j, wh, wl) in enumerate(js):
                    f = mm3(BK[b][:, 256 * c:256 * c + 256], wh(128 * k), wl(128 * k), AH[:, k, 0:256], AL[:, k, 0:256],
                            k == 0 and c == 0, k == 7, True)
                    if k < 7:
                        PE.do(f)
                    else:
                        m = PE.mark(f)
                        half_free[j] = (m,)
            return m

        y_marks = [None] * 4

        def contract(xh, xl, ready, first, last, parts=4):
            j, wh, wl = half()
            PE.wait(*ready)
            for dc in range(8):
                if first and dc % 2 == 0:
                    PE.wait(*free[4 + dc // 2])
                f = mm3(Y(dc), wh(128 * dc), wl(128 * dc), xh, xl, first and dc % 2 == 0, last, True)
                if dc == 7 or (last and dc % 2):
                    y_marks[dc // 2] = PE.mark(f)
                else:
                    PE.do(f)
                if dc == 7:
                    half_free[j] = (y_marks[3],)
                    yield half_free[j]
                elif dc % (8 // parts) == 8 // parts - 1:
                    yield ()

        h_ready = [()] * 8

        def residual(layer, i, chunks=range(8)):
            for dc in chunks:
                VE.wait(y_marks[dc // 2])
                m = VE.mark(stt(hT[:, dc, :], Y(dc), ada_col(layer, i, dc), hT[:, dc, :], ALU.mult, ALU.add))
                h_ready[dc] = (m,)
                if dc % 2:
                    free[4 + dc // 2] = (m,)

        UH = at("UH", [128, 8, 258], F32R, B2 + 78 * KB)
        UL = at("UL", [128, 8, 258], F32R, B2 + 78 * KB + 8256)
        EG = at("EG", [128, 4, 256], F32, B2 + 95 * KB)
        DG = at("DG", [128, 2, 128], F32, B2 + 99 * KB)
        r2 = at("r2", [128, 2], F32, B2 + 100 * KB)
        wb = at("wb", [128, 4], F32, B2 + 100 * KB + 32)
        early_at = (0, 1, 4, 5)
        early_done = []

        def norm_scales(gain, mod=None):
            if not mod:
                return gain, None, ()
            layer, i = mod
            VE.wait((VE.sem, VE.count))
            m = VE.mark(stt(modA[:, 0, :], adaT[:, layer, 8 * i + 8:8 * i + 16], 1.0, gain, ALU.add, ALU.mult))
            return modA[:, 0, :], adaT[:, layer, 8 * i:8 * i + 8], (m,)

        def times_rr(t, k, *marks):
            L = GP if k % 2 else VE
            L.wait(*marks)
            return L.mark(tt(t[:, k, :], t[:, k, :], rr[:, 0:256], ALU.mult))

        def finish(t, product, shift, o, ks):
            def normed(k):
                m = product(k)
                SC.wait(m)
                if shift is None:
                    return m, SC.mark(act(AH[:, k, o:o + 256], t[:, k, :], ACT.Copy))
                return m, SC.mark(act(AH[:, k, o:o + 256], t[:, k, :], ACT.Identity, bias=shift[:, k:k + 1]))

            pending = [normed(k) for k in ks[:2]]
            for i, k in enumerate(ks):
                if i + 2 < len(ks):
                    pending.append(normed(ks[i + 2]))
                VE.wait(*pending[i])
                hi = AH[:, k, o:o + 256].bitcast(F32)
                if shift is None:
                    l = VE.mark(tt(AL[:, k, o:o + 256], t[:, k, :], hi, ALU.subtract))
                else:
                    l = VE.mark(stt(AL[:, k, o:o + 256], t[:, k, :], shift[:, k:k + 1], hi, ALU.add, ALU.subtract))
                a_ready[o // 256][k] = (pending[i][1], l)

        def next_norm(res, gain, shift, ready, fork=()):
            A = lambda k: gain[:, k:k + 1]
            n = 256 if shift is None else 258
            hi, lo, sqr = [], [], []

            def low(k):
                VE.wait(hi[k])
                lo.append(VE.mark(stt(UL[:, k, 0:256], hT[:, k, :], A(k), UH[:, k, 0:256].bitcast(F32),
                                      ALU.mult, ALU.subtract)))

            SC.wait(*ready, *fork)
            for k in range(8):
                residual(*res, (k,))
                SC.wait(*h_ready[k])
                hi.append(SC.mark(act(UH[:, k, 0:256], hT[:, k, :], ACT.Copy, scale=A(k))))
                sqr.append(SC.mark(act(sq[:, k, 0:256], hT[:, k, :], ACT.Square)))
                if k == 1:
                    VE.wait(*fork)
                    if n > 256:
                        wide = shift.unsqueeze(2).to_broadcast([128, 8, 2])
                        a = SC.mark(act(UH[:, :, 256:258], wide, ACT.Copy))
                if k > 1:
                    low(k - 2)
                if k == 2 and n > 256:
                    VE.wait(a)
                    x = VE.mark(tt(UL[:, :, 256:258], wide, UH[:, :, 256:258].bitcast(F32), ALU.subtract))
                    ready = (a, x)
            low(6)
            low(7)
            prepare(taken[0] + 4)
            t = [SC.mark(act(tmp[:, k, :], hT[:, k, :], ACT.Copy, scale=A(k))) for k in range(8)]

            def early(cs, also={}):
                js = [half() for _ in cs]
                PE.wait(*ready)
                for c in cs:
                    PE.wait(*free[early_at[c]])
                for k in range(8):
                    PE.wait(hi[k], lo[k])
                    for c, (j, wh, wl) in zip(cs, js):
                        f = mm3(BK[early_at[c]][:, 0:n], wh(128 * k), wl(128 * k), UH[:, k, 0:n], UL[:, k, 0:n],
                                k == 0, k == 7)
                        if k < 7:
                            PE.do(f)
                        else:
                            m = PE.mark(f)
                            early_done[c:] = [m]
                            half_free[j] = (m,)
                    if k in also:
                        also[k]()

            marks = {}

            def token_sums():
                PE.wait(marks["part"])
                for q in range(2):
                    m = PE.mark(mm(BK[7][:, q:q + 1], part[:, 128 * q:128 * q + 128], sums[:, 0:1], True, True))
                VE.wait(m)
                v = VE.mark(ts(r2[:, :], BK[7][:, 0:2], EPS, ALU.add, 2.0 ** -30, ALU.mult))
                GP.wait(v, m_half)
                g = GP.mark(tt(r2[:, :], r2[:, :], cols[:, 1:2].to_broadcast([128, 2]), ALU.pow))
                GP.wait(g, in_id)
                marks["diag"] = GP.mark(tt(DG[:, :, :], ident.unsqueeze(1).to_broadcast([128, 2, 128]),
                                           r2[:, :].unsqueeze(2).to_broadcast([128, 2, 128]), ALU.mult))

            def spread():
                PE.wait(marks["diag"])
                m = PE.mark(mm(BK[7][:, 0:256], sums[:, :], DG[:, :, :].rearrange("p a b -> p (a b)"), True, True))
                SC.wait(m)
                marks["rr"] = SC.mark(act(rr[:, 0:256], BK[7][:, 0:256], ACT.Copy))
                free[7] = (marks["rr"],)

            ahead[0] = 0
            early((0, 1))
            PE.wait(*free[7])
            for k in range(8):
                PE.wait(sqr[k])
                f = mm(BK[7][32 * (k % 4):32 * (k % 4) + 32, 0:256], ones[:, :], sq[:, k, 0:256], k < 4, k >= 4)
                if k < 7:
                    PE.do(f)
                else:
                    m = PE.mark(f)
            VE.wait(m)
            marks["part"] = VE.mark(cp(part[:, 0:256], BK[7][:, 0:256]))
            early((2,), {2: token_sums})
            lower[0] = (VE,)
            prepare(taken[0] + 3)
            early((3,), {1: spread})
            lower[0] = pattern[0]
            ahead[0] = NS

            finish(tmp, lambda k: times_rr(tmp, k, marks["rr"], t[k]), shift, 0, range(8))
            prepare(taken[0] + NS)
            for c in range(4):
                b = early_at[c]
                VE.wait(early_done[c])
                m = VE.mark(tt(EG[:, c, :], BK[b][:, 0:256], rr[:, 0:256], ALU.mult))
                if n > 256:
                    m = VE.mark(cp(wb[:, c:c + 1], BK[b][:, 256:257]))
                    SC.wait(m)
                    a = SC.mark(act(EG[:, c, :], EG[:, c, :], ACT.Identity, bias=wb[:, c:c + 1]))
                    early_done[c] = a
                else:
                    early_done[c] = m
                free[b] = (m,)

        hk, xk, ck = [lambda k, t=t: t[:, k, :] for t in (hT, tmp, tmc)]
        VE.wait(rstd(hk, [(in_x,)] * 8, 4, 5, 0))
        mx = scaled(hk, xk)
        m = ada_burst(0, range(8), 0)
        lower[0] = (GP, VE)
        prepare(1)
        m_ada = ada_end(0, 0, m, 1)
        VE.wait(m_ada)
        VE.do(stt(modA[:, 0, :], adaT[:, 0, 8:16], 1.0, vec_("nm0"), ALU.add, ALU.mult))
        m_ab = VE.mark(stt(modA[:, 1, :], adaC[:, 8:16], 1.0, vec_("nm0"), ALU.add, ALU.mult))
        for ks, odd in ((range(2), VE), (range(2, 8), GP)):
            modulate(xk, lambda k: sq[:, k, 0:256], mx, 0, lambda k: modA[:, 0, k:k + 1], lambda k: ada_col(0, 0, k), ks, odd)
            prepare(2)
        lower[0] = (VE, GP)

        KH = at("KH", [128, 4, 512], F32R, B2)
        KL = at("KL", [128, 4, 512], F32R, B2 + 8 * KB)
        QS = at("QS", [128, 16, 256], F32R, B2 + 48 * KB)
        sets = [[at(f"{n}{j}", [128, 512], F32, B2 + (76 + 2 * i + 8 * j) * KB)
                 for i, n in enumerate(("qq", "m1", "qr", "qw"))] for j in range(2)]
        VR = at("VR", [128, 4, 256], F32, B2 + 92 * KB)
        set_free, set_n = [(), ()], [0]

        def rows_of(hh):
            return slice(64 * hh, 64 * hh + 64)

        def pieces(x, n):
            return x.rearrange("p (a n) -> p a n", a=n)

        def heads(b, m, wcol, roped, then, stat=None, slow=False):
            i = set_n[0] % 2
            set_n[0] += 1
            qq, m1, qr, w = sets[i]
            n = 256 * roped
            SC.wait(m, *set_free[i])
            s1 = SC.mark(act(qq[:, :], BK[b][:, :], ACT.Square))
            s2 = SC.mark(act(w[:, :], BK[b][:, :], ACT.Copy, scale=wcol))
            free[b] = (s2,)
            GP.wait(s2, in_c, *set_free[i])
            g = GP.mark(tt(pieces(m1[:, 0:n], roped), pieces(w[:, 0:n], roped),
                           cst_("cos").unsqueeze(1).to_broadcast([128, roped, 256]), ALU.mult))
            yield
            b2 = bank(4)
            PE.wait(s2, in_c, *free[b2])
            p2 = PE.mark(mm(BK[b2][:, 0:n], cst_("perm"), w[:, 0:n], True, True))
            if stat is None:
                b1 = bank(4)
                PE.wait(s1, *free[b1])
                p1 = PE.mark(mm(BK[b1][:, :], cst_("blk"), qq[:, :], True, True))
            else:
                stat(s1, qq)
            yield
            if stat is None:
                steps = newton_steps(BK[b1][:, :], p1, 512, b1)
                next(steps)
                if not slow:
                    mr = [*steps][-1]
            VE.wait(p2, *set_free[i])
            x = VE.mark(tt(pieces(qr[:, 0:n], roped), pieces(BK[b2][:, 0:n], roped),
                           cst_("sin").unsqueeze(1).to_broadcast([128, roped, 256]), ALU.mult))
            free[b2] = (x,)
            if slow:
                for mr in steps:
                    yield
            VE.wait(x, g)
            x = VE.mark(tt(qr[:, 0:n], qr[:, 0:n], m1[:, 0:n], ALU.add))
            if stat is None:
                VE.wait(x, mr)
                x = VE.mark(tt(qr[:, 0:n], qr[:, 0:n], rr[:, 0:n], ALU.mult))
                if n < 512:
                    x = VE.mark(tt(qr[:, n:512], w[:, n:512], rr[:, n:512], ALU.mult))
            for y in then(x, qr):
                if slow and not y:
                    yield
            set_free[i] = y

        qs_ready, k_ready, sq_done = [], {}, []
        sb = 4

        def q_stat(P):
            def f(m, qq):
                PE.wait(m, in_c)
                if P == 0:
                    PE.wait(*free[sb])
                for c in range(2):
                    ch = 2 * P + c
                    p = 32 * (ch % 4)
                    o = 256 * (ch // 4)
                    x = PE.mark(mm(BK[sb][p:p + 32, o:o + 256], cst_("hd"), qq[:, 256 * c:256 * c + 256], True, True))
                sq_done.append(x)
            return f

        def q_then(P):
            def f(x, qr):
                SC.wait(x, m_x)
                VE.wait(x, m_x)
                for i in range(4):
                    r0, r1 = rows_of(i % 2), rows_of(1 - i % 2)
                    src = qr[r0, 256 * (i // 2):256 * (i // 2) + 256]
                    a = SC.mark(act(QS[r0, 4 * P + i, :], src, ACT.Copy))
                    VE.wait(a)
                    v = VE.mark(tt(QS[r1, 4 * P + i, :], src, QS[r0, 4 * P + i, :].bitcast(F32), ALU.subtract))
                    qs_ready.append((a, v))
                yield (a, v, sq_done[P])
            return f

        def k_then(c):
            def f(x, qr):
                SC.wait(x)
                VE.wait(x)
                for hh in range(2):
                    r0, r1 = rows_of(hh), rows_of(1 - hh)
                    g = 2 * c + hh
                    a = SC.mark(act(KH[r0, g, :], qr[r0, :], ACT.Copy))
                    a2 = SC.mark(act(KH[r1, g, :], qr[r0, :], ACT.Copy))
                    VE.wait(a)
                    VE.do(tt(KL[r0, g, :], qr[r0, :], KH[r0, g, :].bitcast(F32), ALU.subtract))
                    v = VE.mark(tt(KL[r1, g, :], qr[r0, :], KH[r0, g, :].bitcast(F32), ALU.subtract))
                    k_ready[g] = (a2, v)
                    yield ()
                yield (a2, v)
            return f

        rq, rv, rz = [at(n, [128, 32], F32, B2 + 96 * KB + 128 * i) for i, n in enumerate(("rq", "rv", "rz"))]
        m_rq = []

        def query_scales():
            VE.wait(*sq_done)
            m = VE.mark(cp(part[:, :], BK[sb][:, :]))
            free[sb] = (m,)
            yield
            PE.wait(m, *free[5])
            for i in range(4):
                m = PE.mark(tp(BK[5][:, 128 * i:128 * i + 128], part[:, 128 * i:128 * i + 128], ident))
            VE.wait(m)
            x = VE.mark(ts(rv[:, :].rearrange("p (i j r) -> p i j r", i=4, j=4),
                           BK[5][:, :].rearrange("p (i j r) -> p i j r", i=4, j=4)[:, :, :, 0:2], EPS, ALU.add))
            free[5] = (x,)
            SC.wait(x)
            a = SC.mark(act(rq[:, :], rv[:, :], ACT.Ln))
            SC.wait(a)
            a = SC.mark(act(rq[:, :], rq[:, :], ACT.Exp, scale=-0.5))
            yield
            VE.wait(a)
            x = VE.mark(tt(rz[:, :], rq[:, :], rq[:, :], ALU.mult))
            VE.wait(x)
            x = VE.mark(tt(rz[:, :], rz[:, :], rv[:, :], ALU.mult))
            VE.wait(x)
            x = VE.mark(ts(rz[:, :], rz[:, :], -0.0625, ALU.mult, 0.1875, ALU.add))
            VE.wait(x)
            x = VE.mark(tt(rq[:, :], rq[:, :], rz[:, :], ALU.mult))
            VE.wait(x)
            m_rq.append(VE.mark(ts(rv[:, :], rq[:, :], -1.0, ALU.mult)))

        for P in range(4):
            b = bank(4)
            PE.wait(*free[b])
            if P == 0:
                m = pair(b)
                m_x = (GP.sem, GP.count)
            for c in range(2):
                if P:
                    m = project(BK[b][:, 256 * c:256 * c + 256])
                if (P, c) == (1, 0):
                    m_rr = rstd(ck, [(in_ctx,)] * 8, 4, 5, 256)
                if (P, c) == (1, 1):
                    mc = [SC.mark(act(ck(k), ck(k), ACT.Copy, scale=modA[:, 1, k:k + 1])) for k in range(8)]
                    mc = [times_rr(tmc, k, mc[k], m_rr) for k in range(8)]
                if P > 1:
                    finish(tmc, lambda k: mc[k], adaC[:, 0:8], 256, range(4 * P - 8 + 2 * c, 4 * P - 6 + 2 * c))
                if c:
                    begin(heads(b, m, vec_("qn"), 2, q_then(P), q_stat(P)))
                    last = tasks.pop()
                tick()
            tasks.append(last)
        for c in range(2):
            b = bank(4)
            PE.wait(*free[b])
            m = project(BK[b], ((0, 0), (256, 256)), between=tick)
            begin(heads(b, m, vec_("kn"), 1, k_then(c), slow=c == 1))
            if c == 0:
                tasks.insert(0, query_scales())
        m_v = []
        VE.wait(in_c)
        VE.do(cp(maskb[:, 0, :], cst_("m01")))
        m_maskb = VE.mark(cp(maskb[:, 1, :], cst_("m10")))

        def project_values():
            vb = (6, 7)
            for t in range(2):
                j, wh, wl = half()
                for q in range(4):
                    b = vb[q // 2]
                    if t == 0:
                        PE.wait(*free[b])
                    for kk in range(4):
                        k = 4 * t + kk
                        o = 128 * q
                        PE.wait(*a_ready[q // 2][k])
                        f = mm3(BK[b][:, 256 * (q % 2):256 * (q % 2) + 256], AH[:, k, o:o + 128], AL[:, k, o:o + 128],
                                wh(256 * kk, 256), wl(256 * kk, 256), k == 0 and q % 2 == 0, k == 7, True)
                        if kk < 3 or q < 3:
                            PE.do(f)
                        else:
                            m = PE.mark(f)
                    if q == 3:
                        half_free[j] = (m,)
                    yield
            SC.wait(m)
            for i in range(2):
                x = SC.mark(act(VR[:, 2 * i:2 * i + 2, :], BK[vb[i]][:, :].rearrange("p (a n) -> p a n", a=2), ACT.Copy))
                free[vb[i]] = (x,)
            m_v.extend([m, x])
            yield

        def rcol(t, h, qt):
            i = 16 * (h // 8) + 8 * qt + h % 8
            return t[:, i:i + 1]

        NP = 4
        PR = at("PR", [128, NP, 512], F32, B2 + 76 * KB)
        JK = at("JK", [128, 4, 512], BF16, B2 + 97 * KB)
        PT = at("PT", [128, 4, 4, 256], F32, B2 + 16 * KB)
        OH = at("OH", [128, 2, 256], F32R, B2 + 32 * KB)
        OL = at("OL", [128, 2, 256], F32R, B2 + 34 * KB)
        OT = at("OT", [128, 2, 256], F32, B2 + 36 * KB)
        RB = at("RB", [128, 2, 256], F32, B2 + 38 * KB)
        RD = at("RD", [128, 2, 16], F32, B2 + 96 * KB + 512)
        RX = at("RX", [128, 2, 2, 128], F32, B2 + 101 * KB)
        jk, rb_ready = [], {}
        pr_free, pt_free, o_free, pt_ready, rd_ready = {}, {}, {}, {}, {}
        no_sets, fork = set_free, []

        def attend(h):
            g = h // 4
            nm, su, es = [small[:, h % 4, 2 * i:2 * i + 2] for i in range(3)]
            y = []
            for qt in range(2):
                b = (2 * h + qt) % 3
                PE.wait(*qs_ready[h], *k_ready[g], *free[b], m_maskb)
                q = QS[:, h, 128 * qt:128 * qt + 128]
                PE.do(mm(BK[b][:, :], q, KH[:, g, :], True, False, True))
                PE.do(mm(BK[b][:, :], q, KL[:, g, :], False, False, True))
                o = 128 if qt == 0 else 0
                m = PE.mark(mm(BK[b][:, o:o + 128], identb[:, :], maskb[:, qt, :], False, True, True))
                VE.wait(m, *m_rq, *jk[-4:-3])
                x = VE.mark(ts(JK[:, len(jk) % 4, :], BK[b][:, :], rcol(rv, h, qt), ALU.mult, nsink[:, h:h + 1], ALU.min,
                               accum_out=nm[:, qt:qt + 1]))
                jk.append(x)
                SC.wait(x, *no_sets[0], *pr_free.get((h - 2, qt), ()))
                y.append(SC.mark(act(PR[:, (2 * h + qt) % NP, :], BK[b][:, :], ACT.Exp, scale=rcol(rq, h, qt),
                                     bias=nm[:, qt:qt + 1], accum_out=su[:, qt:qt + 1])))
                yield
            s = SC.mark(act(es, nm, ACT.Exp, bias=vec_("sink", h, 1)))
            for qt in range(2):
                b = (2 * h + qt) % 3
                PE.wait(y[qt])
                for t in range(4):
                    f = tp(BK[b][:, 128 * t:128 * t + 128], PR[:, (2 * h + qt) % NP, 128 * t:128 * t + 128], ident)
                    if t < 3:
                        PE.do(f)
                    else:
                        m = PE.mark(f)
                pr_free[h, qt] = (m,)
                L = VE if qt else SC
                L.wait(m, m_v[0], *pt_free.get(h - 4, ()))
                dst = PT[:, h % 4, :, 128 * qt:128 * qt + 128]
                src = BK[b][:, :].rearrange("p (t n) -> p t n", t=4)
                x = L.mark(cp(dst, src) if qt else act(dst, src, ACT.Copy))
                free[b] = (x,)
                pt_ready[h] = pt_ready.get(h, ()) + (x,)
                if qt == 0:
                    VE.wait(s)
                    x = VE.mark(tt(su, su, es, ALU.add))
                    VE.wait(x)
                    rd_ready[h] = VE.mark(recip(RD[:, :, h], su))
                    if h % 2:
                        VE.wait(rd_ready[h], *pt_free.get(h - 4, ()))
                        rb_ready[h] = VE.mark(cp(RX[:, h // 2 % 2, :, :].rearrange("p q (a n) -> p q a n", a=2),
                                                 RD[:, :, h - 1:h + 1].unsqueeze(3).to_broadcast([128, 2, 2, 64])))
                yield
            if h % 2:
                c = h // 2
                PE.wait(*free[3], rb_ready[h])
                for qt in range(2):
                    PE.do(tp(BK[3][:, 256 + 128 * qt:384 + 128 * qt], RX[:, c % 2, qt, :], ident))
                PE.wait(*pt_ready[h - 1], *pt_ready[h], m_v[1])
                for t in range(4):
                    for hh in range(2):
                        f = mm(BK[3][rows_of(hh), 0:256], VR[:, t, 64 * g:64 * g + 64], PT[:, (2 * c + hh) % 4, t, :],
                               t == 0, t == 3)
                        if t < 3 or hh == 0:
                            PE.do(f)
                        else:
                            m = PE.mark(f)
                pt_free[h - 1] = pt_free[h] = (m,)
                if h == 15:
                    fork.extend((L.sem, L.count) for L in (PE, SC, VE, GP))
                SC.wait(m, *o_free.get(c - 2, ()))
                a = SC.mark(act(RB[:, c % 2, :], BK[3][:, 256:512], ACT.Copy))
                VE.wait(a)
                x = VE.mark(tt(OT[:, c % 2, :], BK[3][:, 0:256], RB[:, c % 2, :], ALU.mult))
                free[3] = (x,)
                yield
                SC.wait(x)
                a = SC.mark(act(OH[:, c % 2, :], OT[:, c % 2, :], ACT.Copy))
                VE.wait(a)
                v = VE.mark(tt(OL[:, c % 2, :], OT[:, c % 2, :], OH[:, c % 2, :].bitcast(F32), ALU.subtract))
                yield
                if h == 13:
                    for _ in range(0):
                        yield
                if h == 15:
                    lower[0], ahead[0] = (GP, VE), NS
                for m in contract(OH[:, c % 2, :], OL[:, c % 2, :], (a, v), c == 0, c == 7):
                    o_free[c] = m
                    yield

        def adaln_rest():
            for n in range(8, 24, 2):
                for _ in range(3 - (n < 8 + 2 * 2)):
                    yield
                m = ada_burst(0, range(n, n + 2), 3)
                if n % 8 == 6:
                    yield
                    m_adas.append(ada_end(0, n // 8, m, 3))
                yield

        m_adas = []
        lower[0], ahead[0] = (GP,), 1
        pv, adas, first = project_values(), adaln_rest(), attend(0)
        for i in range(9):
            if i > 5:
                tick()
            if i > 6:
                next(first)
            next(pv)
        late_keys = tasks.pop()
        tasks.extend((adas, first))
        for h in range(1, 16):
            tasks.append(attend(h))
            for _ in range(2):
                if h > 2:
                    next(late_keys, None)
                tick()
                prepare(taken[0] + (2 if h < 13 else 3))
        while len(m_adas) < 2:
            tick()
        VE.wait(*m_adas)
        after = norm_scales(vec_("nf0"), (0, 3))
        drain()

        AH = at("AH2", [128, 8, 256], F32R, B2 + 8 * KB)
        AL = at("AL2", [128, 8, 256], F32R, B2 + 16 * KB)
        sq = at("sq2", [128, 8, 256], F32, B2 + 24 * KB)
        part, vp, yy, zz, rr = [at(n + "2", [128, 512], F32, B2 + (32 + 2 * i) * KB)
                                for i, n in enumerate(("part", "vp", "yy", "zz", "rr"))]
        adaS = at("adaS2", [128, 512], F32, B2 + 42 * KB)
        acc = [at(f"acc{i}", [128, 2048], F32, B2 + (64 + 14 * i) * KB) for i in range(2)]
        summed = [0]
        ct = at("ct", [128, 2, 4, 256], F32, B2 + 44 * KB)
        mid = at("mid", [128, 2, 512], F32, B2 + 52 * KB)
        MH = at("MH", [128, 2, 512], F32R, B2 + 56 * KB)
        ML = at("ML", [128, 2, 512], F32R, B2 + 60 * KB)
        m_free, ct_free = [(), ()], [(), ()]
        GP.wait(*fork)
        s_c2 = sem("s_c2")
        at_load[first_of_ffn0 + 2] = [(fork, C[:, 0:N2], cst2, s_c2)]
        in_c2 = (s_c2, 16)
        onesb = at("onesb", [128, 128], BF16, B2 + 76 * KB)

        def tables():
            GP.wait((GP.sem, GP.count))
            m = GP.mark(fill(onesb[:, :], 1.0))
            GP.wait(in_c2, m_maskb, m)
            for h in range(8):
                GP.do(ts(slopes[:, h, :], identb[:, :], 2.0 ** -(h + 1), ALU.mult))
                m_tabs[0] = GP.mark(ts(pick[:, h, :], onesb[:, :], cst_("pick", h, 1), ALU.mult))
                yield
            m_tabs[0] = GP.mark(cp(alibi[:, :], cst_("alibi")))

        m_tabs, in_turn = [None], tables()

        def conv_taps(tiles, ready):
            VE.wait(*ready)
            m = [VE.mark(stt(dst[:, 1:256], src[:, 0:255], w(0), dst[:, 1:256], ALU.mult, ALU.add))
                 for dst, src, w in tiles]
            for x, (dst, src, w) in zip(m, tiles):
                VE.wait(x)
                y = VE.mark(stt(dst[:, 0:255], src[:, 1:256], w(2), dst[:, 0:255], ALU.mult, ALU.add))
            return y

        def split_mid(s, x):
            SC.wait(x, *m_free[s])
            a = SC.mark(act(MH[:, s, :], mid[:, s, :], ACT.Copy))
            VE.wait(a)
            v = VE.mark(tt(ML[:, s, :], mid[:, s, :], MH[:, s, :].bitcast(F32), ALU.subtract))
            return (a, v)

        def down(s, ready, first, last):
            for c in range(2):
                for m in contract(MH[:, s, 256 * c:256 * c + 256], ML[:, s, 256 * c:256 * c + 256], ready,
                                  first and c == 0, last and c == 1):
                    if m:
                        m_free[s] = m

        def ffn(layer, scales):
            def tap(chunk):
                return lambda i: vec_(f"conv{layer}", 44 * i + chunk, 1)

            ready, made, conv, gated, product = [None, None], {}, {}, {}, {}
            made[0, 0], made[0, 1] = early_done[1], early_done[3]

            def taps(P, half_u):
                s = P % 2
                SC.wait(made[P, half_u], *ct_free[s])
                if P:
                    src = [BK[2 * s + half_u][:, 256 * c:256 * c + 256] for c in range(2)]
                else:
                    src = [EG[:, 2 * half_u + c, :] for c in range(2)]
                for c in range(2):
                    w = tap(22 * half_u + 2 * P + c)
                    a = SC.mark(act(ct[:, s, 2 * half_u + c, :], src[c], ACT.Copy, scale=w(1)))
                x = conv_taps([(ct[:, s, 2 * half_u + c, :], src[c], tap(22 * half_u + 2 * P + c)) for c in range(2)], (a,))
                if P:
                    free[2 * s + half_u] = (x,)
                conv[P, half_u] = x

            def silu(P):
                g = ct[:, P % 2, 0:2, :].rearrange("p a n -> p (a n)")
                SC.wait(conv[P, 0])
                gated[P] = SC.mark(act(g, g, ACT.Silu))

            def multiply(P):
                s = P % 2
                g, u = [ct[:, s, i:i + 2, :].rearrange("p a n -> p (a n)") for i in (0, 2)]
                VE.wait(gated[P], conv[P, 1], *m_free[s])
                product[P] = VE.mark(tt(mid[:, s, :], g, u, ALU.mult))
                ct_free[s] = (product[P],)

            def split(P):
                ready[P % 2] = split_mid(P % 2, product[P])

            turns = {(1, 0): ((taps, 0, 0), (taps, 0, 1)),
                     (1, 2): ((silu, 0), (multiply, 0), (taps, 1, 0)),
                     (2, 0): ((split, 0), (silu, 1), (taps, 1, 1)),
                     (2, 2): ((multiply, 1), (split, 1), (taps, 2, 0)),
                     (2, 1): ((silu, 2), (taps, 2, 1), (multiply, 2)),
                     (3, 0): ((taps, 3, 0),), (3, 1): ((split, 2), (silu, 3))}

            def turn(P, i):
                rest = (((split, P - 1), (taps, P, 0)), ((silu, P),), ((taps, P, 1), (multiply, P)))[i]
                for f, *x in turns.get((P, i), rest if P > 1 else ()):
                    f(*x)

            for P in range(1, 11):
                s = P % 2
                PE.wait(*free[2 * s])
                made[P, 0] = pair(2 * s, P == 1)
                b1, m1 = 2 * (1 - s) + 1, None
                if layer == 0 and added[0] >= 16 * summed[0] + 16 + 0:
                    m1 = ada_sum(summed[0], b1)
                if P == 1:
                    prepare(taken[0] + NS)
                turn(P, 0)
                if P > 2:
                    down(s, ready[s], False, False)
                    turn(P, 1)
                if m1:
                    ada_end(1, summed[0], m1, b1)
                    summed[0] += 1
                PE.wait(*free[2 * s + 1])
                made[P, 1] = pair(2 * s + 1)
                prepare(taken[0] + NS)
                turn(P, 2)
                if P == 2:
                    down(0, ready[0], True, False)
                    turn(2, 1)
                if layer == 0:
                    next(in_turn, None)
            split(10)
            down(1, ready[1], False, False)
            lower[0] = (GP,)
            after = scales()
            down(0, ready[0], False, True)
            return after

        pattern[0] = (GP, GP, VE)
        next_norm((0, 2), *after, fork)
        after = ffn(0, lambda: norm_scales(vec_("nm1"), (1, 0)))

        next_norm((0, 5), *after)
        gc = at("gc", [128, 2, 512], F32, B2 + 78 * KB)
        cu = at("cu", [128, 2, 512], F32, B2 + 82 * KB)
        before = None
        rot[0] = 1
        for P in range(4):
            s = P % 2
            bs, ms = [], []
            for g in range(3):
                if P == 0 and g < 2:
                    ms.append(early_done[2 * g + 1])
                    bs.append(None)
                    continue
                b = bank()
                bs.append(b)
                PE.wait(*free[b])
                m = pair(b, P == 0)
                ms.append(m)
                if g == 1:
                    SC.wait(m, *ct_free[s])
                    a = SC.mark(act(gc[:, s, :], BK[b][:, :], ACT.Copy))
                    free[b] = (a,)
            g1 = gc[:, s, :]
            if P == 0:
                a, g1 = ms[1], EG[:, 2:4, :].rearrange("p a n -> p (a n)")
            prepare(taken[0] + 3)
            VE.wait(a, ms[2], *ct_free[s])
            x = VE.mark(tt(cu[:, s, :], BK[bs[2]][:, :], g1, ALU.mult))
            free[bs[2]] = (x,)
            SC.wait(x)
            w = [lambda i, c=c: vec_("scconv", 8 * i + 2 * P + c, 1) for c in range(2)]
            for c in range(2):
                a = SC.mark(act(ct[:, s, c, :], cu[:, s, 256 * c:256 * c + 256], ACT.Copy, scale=w[c](1)))
            x = conv_taps([(ct[:, s, c, :], cu[:, s, 256 * c:256 * c + 256], w[c]) for c in range(2)], (a,))
            VE.wait(x, ms[0], *m_free[s])
            g0 = BK[bs[0]][:, :] if P else EG[:, 0:2, :].rearrange("p a n -> p (a n)")
            x = VE.mark(tt(mid[:, s, :], g0, ct[:, s, 0:2, :].rearrange("p a n -> p (a n)"), ALU.mult))
            if P:
                free[bs[0]] = (x,)
            ct_free[s] = (x,)
            now = split_mid(s, x)
            if P == 3:
                b1 = bank()
                m1 = ada_sum(2, b1)
            if before:
                down(1 - s, before, P == 1, False)
            before = now
        lower[0] = (GP,)
        ada_end(1, 2, m1, b1)
        after = norm_scales(vec_("nf1"), (1, 3))
        down(1, before, False, True)
        pattern[0] = (VE, GP)
        next_norm((1, 2), *after)
        after = ffn(1, lambda: norm_scales(vec_("ln1")))

        next_norm((1, 5), *after)
        SC.do(lambda e: e.preload_act_table_set(LN_EXP))

        OT2 = at("OT2", [128, 8, 256], F32, B2)
        QF = at("QF", [128, 8, 256], F32R, B2 + 24 * KB)
        QN = at("QN", [128, 8, 256], F32R, B2 + 44 * KB)
        KNH = at("KNH", [128, 2, 512], F32R, B2 + 52 * KB)
        KNL = at("KNL", [128, 2, 512], F32R, B2 + 56 * KB)
        VN = at("VN", [128, 2, 256], F32, B2 + 60 * KB)
        ZT = at("ZT", [128, 2, 16, 2, 16], F32, B2 + 62 * KB)
        KFH = at("KFH", [128, 8, 256], F32R, B2 + 66 * KB)
        KFL = at("KFL", [128, 8, 256], F32R, B2 + 74 * KB)
        VF = at("VF", [128, 2, 512], F32, B2 + 82 * KB)
        PU = [at("PU0", [128, 4, 512], F32, B2 + 86 * KB), at("PU1", [128, 4, 256], F32, B2 + 86 * KB)]
        PV = [[at(f"PV0{i}", [128, 2, 384], F32, B2 + o * KB) for i, o in enumerate((94, 97, 63))],
              [at(f"PV1{i}", [128, 1, 384], F32, B2 + 90 * KB + 1536 * i) for i in range(3)]]
        o = B2 + 100 * KB
        PC = at("PC", [128, 16, 16], F32, o)
        PL = at("PL", [128, 16, 16], F32, o + KB)
        PCT = at("PCT", [128, 256], F32, o + 2 * KB)
        VCX = at("VCX", [128, 8, 64], F32, B2 + 41 * KB)
        CTB = at("CTB", [128, 256], BF16, B2 + 37 * KB + 512)
        C1 = at("C1", [128, 256], F32, B2 + 32 * KB)
        GG = at("GG", [128, 2, 2, 16], F32, B2 + 33 * KB)
        G2 = at("G2", [128, 2, 2, 16], F32, B2 + 33 * KB + 256)
        GV = at("GV", [128, 8, 16], F32, B2 + 33 * KB + 512)
        KC = at("KC", [128, 2, 2, 16], F32R, B2 + 34 * KB)
        GF = at("GF", [32, 256], F32, B2 + 35 * KB)
        gt = at("gt", [128, 2, 32], F32, B2 + 36 * KB)
        ga = at("ga", [128, 2, 24], F32, B2 + 36 * KB + 256)
        fa = at("fa", [128, 2, 8], F32, B2 + 36 * KB + 512)
        fb = at("fb", [128, 2, 8], F32, B2 + 36 * KB + 576)
        fc = at("fc", [128, 2, 8], F32, B2 + 36 * KB + 640)
        st = at("st", [128, 8, 8], F32, B2 + 36 * KB + 704)
        cs = at("cs", [128, 4, 16], F32, B2 + 37 * KB)
        cr = at("cr", [128, 2, 256], F32, B2 + 38 * KB)

        fork = [(PE.sem, PE.count), (SC.sem, SC.count), (VE.sem, VE.count)]
        GP.wait(*fork)

        def stack(dst_h, dst_l, src, hh, scale, both, L=None):
            r0, r1 = rows_of(hh), rows_of(1 - hh)
            a = SC.mark(act(dst_h[r0], src[r0], ACT.Copy, scale=scale))
            VE.wait(a)
            hi = dst_h[r0].bitcast(F32)
            if both:
                if L is GP:
                    L.wait(a, (L.sem, L.count))
                    L.mark(cp(dst_h[r1], hi))
                else:
                    L.wait(a)
                    a = L.mark(act(dst_h[r1], hi, ACT.Copy))
                v = VE.mark(tt(dst_l[r0], src[r0], hi, ALU.subtract))
                if L is GP:
                    L.wait(v, (L.sem, L.count))
                    return (a, v, L.mark(cp(dst_l[r1], dst_l[r0].bitcast(F32))))
                return (a, VE.mark(tt(dst_l[r1], src[r0], hi, ALU.subtract)))
            if scale != 1.0:
                v = VE.mark(stt(dst_l[r1], src[r0], scale, hi, ALU.mult, ALU.subtract))
            else:
                v = VE.mark(tt(dst_l[r1], src[r0], hi, ALU.subtract))
            return (a, v)

        pb = [0]

        def proj_bank():
            pb[0] += 1
            return pb[0] % 2 if pb[0] > 2 else pb[0] + 1

        z_ready, qn_ready, kn_ready, qf_ready, kf_ready = [], {}, {}, {}, {}

        VE.wait(*fork)
        m_z0 = VE.mark(fill(ZT[:, :, :, :, :].rearrange("p a b c d -> p (a b c d)"), 0.0))
        VE.wait(*early_done, m_z0)
        for kv in range(2):
            for par in range(2):
                for g in range(2):
                    src = EG[rows_of(g), kv, :]
                    lo = src[:, 0:240].rearrange("p (c i r) -> p i c r", i=8, r=2)[:, :, :, par]
                    hi = src[:, 16:256].rearrange("p (c i r) -> p i c r", i=8, r=2)[:, :, :, par]
                    for q, s_ in enumerate((lo, hi)):
                        pe = vec_(f"pe{kv}")[rows_of(g)].rearrange("p (i r) -> p i r", r=2)[:, 8 * q:8 * q + 8, par:par + 1]
                        m = VE.mark(tt(ZT[rows_of(par), kv, 8 * q:8 * q + 8, g, 0:15], s_,
                                       pe.to_broadcast([64, 8, 15]), ALU.add))
        m_z = m

        def compress():
            b = 7
            PE.wait(m_z, *free[b])
            for kv in range(2):
                i = w1_at[kv]
                PE.wait(loaded(i))
                w1 = slot(i)[:, :].rearrange("p (i n) -> p i n", i=16)
                for i16 in range(16):
                    j = i16 % 4
                    f = mm(BK[b][32 * j:32 * j + 32, 128 * kv:128 * kv + 128],
                           ZT[:, kv, i16, :, :].rearrange("p a b -> p (a b)"), w1[:, i16, :], i16 < 4, i16 >= 12)
                    if i16 < 15:
                        PE.do(f)
                    else:
                        m = PE.mark(f)
                raw_free[i] = (m,)
                yield
            VE.wait(m, *fork)
            m = VE.mark(cp(C1[:, :], BK[b][:, 0:256]))
            yield
            PE.wait(m)
            for kv in range(2):
                m = PE.mark(mm(BK[b][:, 32 * kv:32 * kv + 32], C1[:, 128 * kv:128 * kv + 128], sel32, True, True))
            x = BK[b][:, 0:64]
            g2, gg = [t[:, :, :, :].rearrange("p a b c -> p (a b c)") for t in (G2, GG)]
            VE.wait(m)
            m = VE.mark(cp(gg, x))
            free[b] = (m,)
            VE.wait(m)
            m = VE.mark(tt(g2, gg, gg, ALU.mult))
            VE.wait(m)
            m = VE.mark(ts(g2, g2, 0.044715, ALU.mult, 1.0, ALU.add))
            VE.wait(m)
            m = VE.mark(tt(g2, g2, gg, ALU.mult))
            SC.wait(m)
            m = SC.mark(act(g2, g2, ACT.Exp, scale=-2.0 * 0.7978845608028654))
            yield
            VE.wait(m)
            m = VE.mark(ts(g2, g2, 1.0, ALU.add))
            VE.wait(m)
            m = VE.mark(recip(g2, g2))
            VE.wait(m)
            m = VE.mark(tt(gg, gg, g2, ALU.mult))
            VE.wait(m)
            m = VE.mark(cp(GV[:, :, :].rearrange("p (g r) c -> p g r c", g=2),
                           GG[:, 1, :, :].unsqueeze(2).to_broadcast([128, 2, 4, 16])))
            yield
            PE.wait(m, *free[b])
            PE.do(mm(BK[b][:, 0:32], vec_("w2k"), GG[:, 0, :, :].rearrange("p a b -> p (a b)"), True, True))
            m = PE.mark(mm(BK[b][:, 64:128], GV[:, :, :].rearrange("p a b -> p (a b)"), vec_("w2v"), True, True))
            src = BK[b][:, 0:32].rearrange("p (a b) -> p a b", a=2)
            SC.wait(m, *fork)
            a = SC.mark(act(KC[:, :, 0, :], src, ACT.Copy))
            VE.wait(a)
            v = VE.mark(tt(KC[:, :, 1, :], src, KC[:, :, 0, :].bitcast(F32), ALU.subtract))
            VE.wait(in_v)
            x = VE.mark(tt(VCX[:, :, :], BK[b][:, 64:128].unsqueeze(1).to_broadcast([128, 8, 64]),
                           cst_("hrow").unsqueeze(2).to_broadcast([128, 8, 64]), ALU.mult))
            free[b] = (x,)
            kc_ready.extend([a, v, x])

        kc_ready = []

        for c in range(2):
            SC.wait(early_done[2 + c], *fork)
            VE.wait(early_done[2 + c], *fork)
            for g in range(2):
                kn_ready[g] = kn_ready.get(g, ()) + stack(KNH[:, g, 256 * c:256 * c + 256],
                                                          KNL[:, g, 256 * c:256 * c + 256], EG[:, 2 + c, :], g, 1.0, True, GP)
            tick()

        def by_rows(b, out_rows):
            PE.wait(*free[b])
            for t in range(2):
                j, wh, wl = half()
                for q in range(2):
                    if q:
                        tick()
                    for kk in range(4):
                        k = 4 * t + kk
                        PE.wait(*a_ready[0][k])
                        f = mm3(BK[b][:, 256 * q:256 * q + 256], AH[:, k, 128 * q:128 * q + 128],
                                AL[:, k, 128 * q:128 * q + 128], wh(256 * kk, 256), wl(256 * kk, 256),
                                k == 0 and q == 0, k == 7, True)
                        if kk < 3 or q < 1:
                            PE.do(f)
                        else:
                            m = PE.mark(f)
                half_free[j] = (m,)
                tick()
            SC.wait(m, *fork)
            x = SC.mark(act(out_rows, BK[b][:, :].rearrange("p (q n) -> p q n", q=2), ACT.Copy))
            free[b] = (x,)
            return x

        m_vn = by_rows(proj_bank(), VN[:, :, :])

        j, wh, wl = half()
        b = proj_bank()
        PE.wait(*free[b])
        for k in range(8):
            PE.wait(*a_ready[0][k])
            f = mm3(BK[b][0:32, 0:256], wh(32 * k, 32), wl(32 * k, 32), AH[:, k, :], AL[:, k, :], k == 0, k == 7)
            if k < 7:
                PE.do(f)
            else:
                m = PE.mark(f)
        half_free[j] = (m,)

        m_gate, m_ctb = [], []

        def gates(m, b):
            VE.wait(m, *fork)
            m = VE.mark(cp(GF[:, :], BK[b][0:32, 0:256]))
            free[b] = (m,)
            yield
            b = 6
            PE.wait(m, *free[b])
            for q in range(2):
                m = PE.mark(tp(BK[b][:, 32 * q:32 * q + 32], GF[:, 128 * q:128 * q + 128], ident[0:32, 0:32]))
            VE.wait(m)
            m = VE.mark(cp(gt[:, :, :], BK[b][:, 0:64].rearrange("p (q n) -> p q n", q=2)))
            free[b] = (m,)
            SC.wait(m)
            a = SC.mark(act(ga[:, :, :], gt[:, :, 0:24], ACT.Exp, scale=-1.0))
            VE.wait(m, in_v)
            x = VE.mark(tt(fa[:, :, :], gt[:, :, 24:32], vec_("bfg").unsqueeze(1).to_broadcast([128, 2, 8]), ALU.add))
            SC.wait(x)
            y = SC.mark(act(fb[:, :, :], fa[:, :, :], ACT.Abs))
            SC.wait(y)
            y = SC.mark(act(fb[:, :, :], fb[:, :, :], ACT.Exp, scale=-1.0))
            yield
            VE.wait(a)
            m = VE.mark(ts(ga[:, :, :], ga[:, :, :], 1.0, ALU.add))
            VE.wait(m)
            m_gate.append(VE.mark(recip(ga[:, :, :], ga[:, :, :])))
            SC.wait(y)
            y = SC.mark(act(fb[:, :, :], fb[:, :, :], ACT.Ln, bias=1.0))
            VE.wait(y, x)
            m = VE.mark(ts(fa[:, :, :], fa[:, :, :], 0.0, ALU.min))
            VE.wait(m)
            m = VE.mark(tt(fc[:, :, :], fb[:, :, :], fa[:, :, :], ALU.subtract))
            yield
            PE.wait(m, *free[b])
            for q in range(2):
                m = PE.mark(mm(BK[b][0:8, 0:256], fc[:, q, :], cst_("zto", 128 - 128 * q, 256), q == 0, q == 1))
            VE.wait(m, m_ctb0)
            x = VE.mark(cp(CTB[0:8, :], BK[b][0:8, 0:256]))
            VE.wait(x)
            x = VE.mark(tt(cr[0:8, 0, :], BK[b][0:8, 0:256], CTB[0:8, :], ALU.subtract))
            free[b] = (x,)
            VE.wait(x)
            x = VE.mark(cp(CTB[32:40, :], cr[0:8, 0, :]))
            VE.wait(x)
            x = VE.mark(cp(cb[0:8, :], cr[0:8, 0, :]))
            VE.wait(x)
            x = VE.mark(tt(cr[0:8, 1, :], cr[0:8, 0, :], cb[0:8, :], ALU.subtract))
            VE.wait(x)
            m_ctb.append(VE.mark(cp(CTB[64:72, :], cr[0:8, 1, :])))

        cb = at("cb", [128, 256], BF16, B2 + 40 * KB)
        VE.wait(*fork)
        m_ctb0 = VE.mark(fill(CTB[:, :], 0.0))
        tasks.append(compress())
        tasks.append(gates(m, b))

        def queries(c, dst, ready, wait_for):
            b = proj_bank()
            PE.wait(*free[b])
            m = project(BK[b][:, 0:256], between=tick)
            SC.wait(m, *wait_for)
            VE.wait(*wait_for)
            for hh in range(2):
                h = 2 * c + hh
                ready[h] = stack(dst[:, h, :], dst[:, h, :], BK[b][:, 0:256], hh, 0.125, False)
            free[b] = ready[h][-1:]
            tick()

        for c in range(4):
            queries(c, QN, qn_ready, fork)

        def compressed():
            b = 7
            PE.wait(*kc_ready, *free[b])
            for qt in range(2):
                for h in range(8):
                    PE.wait(*qn_ready[h])
                    m = PE.mark(mm(BK[b][:, 256 * qt + 32 * h:256 * qt + 32 * h + 32], QN[:, h, 128 * qt:128 * qt + 128],
                                   KC[:, h // 4, :, :].rearrange("p a b -> p (a b)"), True, True))
                yield
            src = BK[b][:, :].rearrange("p (u a c) -> p u a c", u=16, a=2)
            SC.wait(m)
            a = SC.mark(act(PL[:, :, :], src[:, :, 1, :], ACT.Copy))
            VE.wait(a)
            x = VE.mark(tt(PC[:, :, :], src[:, :, 0, :], PL[:, :, :], ALU.add))
            free[b] = (x,)
            tab = cst_("cbias").rearrange("p (u c) -> p u c", u=16)
            VE.wait(x)
            x = VE.mark(tt(PC[:, :, :], PC[:, :, :], tab, ALU.add))
            VE.wait(x)
            x = VE.mark(red(cs[:, 0, :], PC[:, :, :], ALU.max))
            yield

            def wide(t):
                return t.unsqueeze(2).to_broadcast([128, 16, 16])

            VE.wait(x)
            x = VE.mark(tt(PC[:, :, :], PC[:, :, :], wide(cs[:, 0, :]), ALU.subtract))
            SC.wait(x)
            a = SC.mark(act(PC[:, :, :], PC[:, :, :], ACT.Exp))
            VE.wait(a)
            x = VE.mark(tt(PC[:, :, :], PC[:, :, :], cst_("cmask").rearrange("p (u c) -> p u c", u=16), ALU.mult))
            VE.wait(x)
            x = VE.mark(red(cs[:, 1, :], PC[:, :, :], ALU.add))
            yield
            VE.wait(x)
            x = VE.mark(ts(cs[:, 1, :], cs[:, 1, :], 1e-30, ALU.max))
            VE.wait(x)
            x = VE.mark(recip(cs[:, 1, :], cs[:, 1, :]))
            VE.wait(x, *m_gate)
            x = VE.mark(tt(cs[:, 2, :].rearrange("p (q h) -> p q h", q=2), cs[:, 1, :].rearrange("p (q h) -> p q h", q=2),
                           ga[:, :, 0:24:3], ALU.mult))
            VE.wait(x)
            x = VE.mark(tt(PC[:, :, :], PC[:, :, :], wide(cs[:, 2, :]), ALU.mult))
            yield
            PE.wait(x, *free[b])
            for qt in range(2):
                m = PE.mark(tp(BK[b][:, 128 * qt:128 * qt + 128],
                               PC[:, 8 * qt:8 * qt + 8, :].rearrange("p a b -> p (a b)"), ident))
            SC.wait(m)
            x = SC.mark(act(PCT[:, :], BK[b][:, 0:256], ACT.Copy))
            free[b] = (x,)
            m_pct.append(x)

        m_pct = []

        pu_free, pv_free, pv_ready, ot_ready = {}, {}, {}, {}
        score_banks, turn_banks, exps, scaled_p, part_of = [2, 3], [4, 5], {}, {}, {}

        def unit(u):
            kind, h, qt = u // 16, u % 16 // 2, u % 2
            return kind, h, qt, 2 - kind, 128 * (qt + 1), [st[:, u % 8, 2 * i:2 * i + 2 - kind] for i in range(3)]

        def scores(u):
            kind, h, qt, nb, n, _ = unit(u)
            b = score_banks.pop(0)
            score_banks.append(b)
            PE.wait(*free[b])
            if kind == 0:
                PE.wait(*qn_ready[h], *kn_ready[h // 4], m_tabs[0])
                q = QN[:, h, 128 * qt:128 * qt + 128]
                PE.do(mm(BK[b][:, :], q, KNH[:, h // 4, :], True, False, True))
                PE.do(mm(BK[b][:, :], q, KNL[:, h // 4, :], False, False, True))
                for i in range(2):
                    m = PE.mark(mm(BK[b][:, 256 * i:256 * i + n], slopes[:, h, :], alibi[:, 0:n] if qt else
                                   alibi[:, 128:256], False, i == 1, True))
            else:
                PE.wait(*qf_ready[h], *kf_ready[h], *m_ctb, m_tabs[0])
                q = QF[:, h, 128 * qt:128 * qt + 128]
                PE.do(mm(BK[b][:, 0:256], q, KFH[:, h, :], True, False, True))
                PE.do(mm(BK[b][:, 0:256], q, KFL[:, h, :], False, False, True))
                PE.do(mm(BK[b][:, 0:n], pick[:, h, :], CTB[:, 0:n], False, False, True))
                m = PE.mark(mm(BK[b][:, n - 128:n], identb[:, :], maskb[:, 0, :], False, True, True))
            part_of[u] = (b, m)

        def softmax(u):
            kind, h, qt, nb, n, (nm, su, sc) = unit(u)
            b, m = part_of[u]
            VE.wait(m, *fork2, *pu_free.get(u - 8, ()))
            src = BK[b][:, 0:256 * nb].rearrange("p (i n) -> p i n", i=nb)[:, :, 0:n]
            x = VE.mark(red(nm, src, ALU.max, negate=True))
            SC.wait(x, *fork2, *pu_free.get(u - 4, ()))
            for i in range(nb):
                y = SC.mark(act(PU[kind][:, u % 4, n * i:n * i + n], BK[b][:, 256 * i:256 * i + n], ACT.Exp,
                                bias=nm[:, i:i + 1], accum_out=su[:, i:i + 1]))
            free[b] = (y,)
            exps[u] = y

        def normalise(u):
            kind, h, qt, nb, n, (nm, su, sc) = unit(u)
            VE.wait(exps[u])
            x = VE.mark(recip(sc, su))
            marks = []
            for i in range(nb):
                p = PU[kind][:, u % 4, n * i:n * i + n]
                L = GP if i < on_gp(kind, qt) else VE
                L.wait(x, exps[u], *[(L.sem, L.count)] * (L is GP))
                if kind == 0:
                    L.wait(*m_gate)
                    g = 3 * h + 1 + i
                    marks.append(L.mark(ts(p, p, sc[:, i:i + 1], ALU.mult, ga[:, qt, g:g + 1], ALU.mult)))
                else:
                    marks.append(L.mark(ts(p, p, sc[:, i:i + 1], ALU.mult)))
            scaled_p[u] = marks

        def turn(u):
            kind, h, qt, nb, n, _ = unit(u)
            b = turn_banks.pop(0)
            turn_banks.append(b)
            PE.wait(*scaled_p[u], *free[b])
            nt = qt + 1
            for i in range(nb * nt):
                m = PE.mark(tp(BK[b][:, 128 * i:128 * i + 128], PU[kind][:, u % 4, 128 * i:128 * i + 128], ident))
            pu_free[u] = (m,)
            H = u // 2
            L = SC if qt == 0 else VE
            L.wait(m, *fork2, *pv_free.get(H - 3, ()))
            if H == 8:
                L.wait(*pu_free[15])
            d = PV[kind][H % 3][:, 0:nb, 128 * qt:128 * qt + 128 * nt]
            s_ = BK[b][:, 0:128 * nb * nt].rearrange("p (i n) -> p i n", i=nb)
            x = L.mark(cp(d, s_) if qt else act(d, s_, ACT.Copy))
            free[b] = (x,)
            pv_ready.setdefault(H, []).append(x)

        def values(kind, c):
            H = 8 * kind + 2 * c
            g = c // 2
            nb = 2 - kind
            PE.wait(*pv_ready[H], *pv_ready[H + 1], *free[6])
            if kind == 0:
                PE.wait(*m_pct, m_vn)
                PE.do(mm(BK[6][:, 0:256], VCX[:, 2 * c:2 * c + 2, :].rearrange("p a b -> p (a b)"), PCT[:, :],
                         True, False, True))
            else:
                PE.wait(*m_vf)
            for i in range(nb):
                for t in range(2):
                    for hh in range(2):
                        if kind == 0:
                            v = VN[:, t, 128 * i + 64 * g:128 * i + 64 * g + 64]
                        else:
                            v = VF[:, t, 64 * (2 * c + hh):64 * (2 * c + hh) + 64]
                        p = PV[kind][(H + hh) % 3][:, i, 256:384] if t else PV[kind][(H + hh) % 3][:, i, 0:256]
                        m = PE.mark(mm(BK[6][rows_of(hh), 128 * t:256], v, p, kind == 1 and i == 0 and t == 0,
                                       i == nb - 1 and t == 1, True))
            pv_free[H] = pv_free[H + 1] = (m,)
            SC.wait(m, *fork2)
            x = SC.mark(act(OT2[:, 4 * kind + c, :], BK[6][:, 0:256], ACT.Copy))
            free[6] = (x,)
            ot_ready[4 * kind + c] = x

        ACC = [at(f"ACC{i}", [128, 256], F32, B2 + (32 + i) * KB) for i in range(3)]
        X0 = at("X0", [128, 2, 4, 256], F32R, B2 + 8 * KB)
        TT = at("TT", [128, 2, 1024], F32, B2 + 16 * KB)
        hr = at("hr", [128, 2, 1024], F32, B2)
        rk = at("rk", [128, 2, 2, 2], F32, B2 + 43 * KB + 256)
        x_ready = {}

        def square(kind, c):
            acc, x2, last = [t[:, :] for t in ACC]
            o = OT2[:, 4 * kind + c, :]
            GP.wait(ot_ready[4 * kind + c], *m_pct, *m_ctb, *acc_free, (GP.sem, GP.count))
            if c == 0:
                GP.mark(tt(acc, o, o, ALU.mult))
            elif c < 3:
                x = GP.mark(tt(x2, o, o, ALU.mult))
                GP.wait(x)
                GP.mark(tt(acc, acc, x2, ALU.add))
            else:
                SC.wait(ot_ready[4 * kind + c], *acc_free)
                squares[kind] = ((GP.sem, GP.count), SC.mark(act(last, o, ACT.Square)))

        squares, acc_free, to_square = {}, [], []

        def row_scales(kind, b):
            PE.wait(*squares[kind], *free[b])
            acc, _, last = ACC
            for q in range(2):
                r = slice(128 * q, 128 * q + 128)
                PE.do(mm(BK[b][:, q:q + 1], acc[:, r], ones[:, 0:1], True, False))
                m = PE.mark(mm(BK[b][:, q:q + 1], last[:, r], ones[:, 0:1], False, True))
            acc_free[:] = [m]
            VE.wait(m, *fork2)
            x = VE.mark(ts(rk[:, kind, 0, :], BK[b][:, 0:2], 1.0 / 512.0, ALU.mult, EPS, ALU.add))
            free[b] = (x,)
            GP.wait(x, (GP.sem, GP.count))
            return GP.mark(tt(rk[:, kind, 1, :], rk[:, kind, 0, :], cols[:, 1:2].to_broadcast([128, 2]), ALU.pow))

        def gained(kind, c, h_, l_, *after):
            k = 4 * kind + c
            g = vec_("gn", k, 1)
            SC.wait(ot_ready[k], in_v, *after)
            a = SC.mark(act(h_, OT2[:, k, :], ACT.Copy, scale=g))

            def low():
                VE.wait(a, *after)
                x = VE.mark(stt(l_, OT2[:, k, :], g, h_.bitcast(F32), ALU.mult, ALU.subtract))
                x_ready[k] = (a, x)

            return low

        row_banks = {(0, 0): 0, (0, 1): 1, (1, 0): 7, (1, 1): 5}

        def rows_product(kind, k):
            while 4 * kind + k not in x_ready:
                yield
            PE.wait(*x_ready[4 * kind + k])
            h_, l_ = xs_of(kind, k)
            j, wh, wl = half()
            for (q, n), b in row_banks.items():
                if k == 0:
                    PE.wait(*free[b])
                w, v = wh(512 * n, 512), wl(512 * n, 512)
                r = slice(128 * q, 128 * q + 128)
                PE.do(mm(BK[b][:, :], h_[:, r], w, k == 0, False))
                PE.do(mm(BK[b][:, :], h_[:, r], v, False, False))
                rows_done[q, n] = PE.mark(mm(BK[b][:, :], l_[:, r], w, False, k == 3))
                yield
            half_free[j] = (rows_done[1, 1],)

        rows_done = {}

        def xs_of(kind, c):
            return (QF[:, 2 * c, :], QF[:, 2 * c + 1, :]) if kind else (X0[:, 0, c, :], X0[:, 1, c, :])

        def first_rows():
            done = (PE.sem, PE.count)
            low = None
            for q in range(2):
                for n in range(2):
                    PE.wait(*free[n])
                    for c in range(4):
                        m = PE.mark(tp(BK[n][:, 128 * c:128 * c + 128], hT[:, 4 * n + c, 128 * q:128 * q + 128], ident))
                    if low:
                        low()
                    low = gained(0, 2 * q + n, *xs_of(0, 2 * q + n), done)
                    yield
                    SC.wait(m, done)
                    x = SC.mark(act(TT[:, q, 512 * n:512 * n + 512], BK[n][:, :], ACT.Copy))
                    free[n] = (x,)
                    yield
            low()
            m_rk = row_scales(0, 0)
            yield
            ahead[0] = 0
            lower[0] = (VE, GP)
            score_banks.remove(7)
            turn_banks.remove(5)
            for k in range(4):
                for i, _ in enumerate(rows_product(0, k)):
                    if i == 1 and k:
                        prepare(taken[0] + 3)
                    yield
            for (q, n), b in row_banks.items():
                VE.wait(rows_done[q, n], m_rk, x)
                t = TT[:, q, 512 * n:512 * n + 512]
                y = VE.mark(stt(t, BK[b][:, :], rk[:, 0, 1, q:q + 1], t, ALU.mult, ALU.add))
                free[b] = (y,)
                tt_ready.append(y)
            prepare(taken[0] + 4)
            yield

        tt_ready = []

        def all_heads():
            later = {}
            for s_ in range(32 + 6):
                if s_ < 32:
                    while s_ > 15 and (s_ // 2 - 8 not in kf_ready or s_ // 2 - 8 not in qf_ready):
                        yield
                    scores(s_)
                u = s_ - 1
                if 0 <= u < 32:
                    softmax(u)
                u = s_ - 2
                if 0 <= u < 32:
                    normalise(u)
                u = s_ - 3
                if 0 <= u < 32:
                    turn(u)
                u = s_ - 4
                if 0 <= u < 32 and u % 4 == 3:
                    while not m_pct:
                        yield
                    if u == 3:
                        score_banks.append(7)
                    while u > 15 and len(m_vf) < 2:
                        yield
                    values(u // 16, u % 16 // 4)
                    if u in (15, 31):
                        (fox_done if u == 31 else nsa_done).append((PE.sem, PE.count))
                u = s_ - 5
                if 0 <= u < 32 and u % 4 == 3:
                    kind, c = u // 16, u % 16 // 4
                    to_square.append((kind, c))
                    if kind:
                        later[s_ + 1] = gained(1, c, *xs_of(1, c))
                if to_square and (acc_free or not to_square[0][0]):
                    square(*to_square.pop(0))
                if s_ in later:
                    later[s_]()
                yield

        nsa_done, fox_done, m_vf = [], [], []

        filler_rate = lambda n: 3 if n < 4 else 2

        def on_gp(kind, qt):
            return 1 if kind == 0 and qt else 0

        fork2 = [(PE.sem, PE.count), (SC.sem, SC.count), (VE.sem, VE.count)]
        while not kc_ready:
            tick()
        tasks.append(compressed())
        tasks.append(all_heads())
        lower[0] = (GP,)
        for i in range(2):
            m_vf.append(by_rows(proj_bank(), VF[:, :, 256 * i:256 * i + 256]))

        def keys(c):
            b = proj_bank()
            PE.wait(*free[b])
            m = project(BK[b][:, 0:256], between=tick)
            SC.wait(m)
            for hh in range(2):
                h = 2 * c + hh
                kf_ready[h] = stack(KFH[:, h, :], KFL[:, h, :], BK[b][:, 0:256], hh, 1.0, True, SC)
            free[b] = kf_ready[h][:2]
            tick()

        for c in (0, 2):
            for f in (keys, lambda c: queries(c, QF, qf_ready, fork2)):
                f(c)
                f(c + 1)
        prepare(taken[0] + NS)

        def rows():
            yield from first_rows()
            for k in range(3):
                yield from rows_product(1, k)

        BU = at("BU", [128, 2048], BF16, B2 + 38 * KB)

        def bias_parts():
            src = slot(bias_at)
            GP.wait(*nsa_done, *m_ctb, (GP.sem, GP.count))
            m_bu.append(GP.mark(fill(BU[32:64, :], 0.0)))
            cs = [slice(512 * c, 512 * c + 512) for c in range(4)]
            last = [(loaded(bias_at), *nsa_done, *m_ctb)] * 4

            def down_to(r, c):
                SC.wait(*last[c])
                last[c] = (SC.mark(act(BU[r, cs[c]], src[r, cs[c]], ACT.Copy)),)

            for c in range(4):
                down_to(slice(0, 32), c)
                down_to(slice(64, 128), c)
                yield
            for r in (slice(64, 128), slice(96, 128)):
                for c in range(4):
                    VE.wait(*last[c])
                    last[c] = (VE.mark(tt(src[r, cs[c]], src[r, cs[c]], BU[r, cs[c]], ALU.subtract)),)
                    yield
                for c in range(4):
                    down_to(r, c)
                    yield
            m_bu.extend(last[3])

        m_bu = []
        filler, bias_split = rows(), bias_parts()
        n = 0
        while tasks:
            tick()
            for _ in range(filler_rate(n)):
                next(filler, None)
            if n > 1:
                next(bias_split, None)
                next(bias_split, None)
            n += 1
        for _ in filler:
            pass
        for _ in bias_split:
            pass
        while to_square:
            square(*to_square.pop(0))
        m_rk = row_scales(1, 3)
        heads_done = [(L.sem, L.count) for L in (PE, SC, VE, GP)]

        X3 = at("X3", [128, 3, 2, 1024], BF16, B2 + 8 * KB)
        XS = [at(f"XS{i}", [128, 8, 64], F32, o) for i, o in enumerate((B2 + 20 * KB, B2 + 22 * KB, offset["C"]))]
        G, LI, SG, AC0, AT, YF = [at(n, [128, 512], F32, B2 + (24 + 2 * i) * KB)
                                  for i, n in enumerate(("G", "LI", "SG", "AC0", "AT", "YF"))]
        AC1 = at("AC1", [128, 512], F32, offset["C"] + 2 * KB)
        YH, YL = [at(n, [128, 512], F32R, B2 + (34 + 2 * i) * KB) for i, n in enumerate(("YH", "YL"))]
        X_ = [at(f"X_{i}", [128, 1024], F32, B2 + (32 - 8 * i) * KB) for i in range(2)]
        ST = [at(f"ST{i}", [128, 256], BF16, B2 + 42 * KB + 512 * i) for i in range(3)]
        SE = [at(f"SE{i}", [128, 64], BF16, B2 + 43 * KB + 512 + 128 * i) for i in range(2)]
        BR = at("BR", [128, 32], F32, B2 + 43 * KB + 768)
        CI = at("CI", [128, 32], mybir.dt.int32, B2 + 43 * KB + 896)
        WR = at("WR", [128, 8, 32], F32, B2 + 46 * KB)
        CE = [at(f"CE{i}", [128, 256], F32R, o) for i, o in enumerate((B2 + 44 * KB, B2 + 45 * KB, offset["pick"]))]
        WT = at("WT", [128, 256], F32, offset["pick"] + KB)
        o = offset["slopes"]
        LG, GT, EQ, CU, EX, WW, PO = [at(n, [128, 2, 32], F32, o + 256 * i)
                                      for i, n in enumerate(("LG", "GT", "EQ", "CU", "EX", "WW", "PO"))]
        mx, ss, rt = [at(n, [128, 2, 8], F32, o + 1792 + 64 * i) for i, n in enumerate(("mx", "ss", "rt"))]
        W3 = at("W3", [128, 3, 2, 32], BF16, offset["alibi"])
        MK = at("MK", [128, 2, 32], BF16, offset["alibi"] + 384)
        WS = at("WS", [128, 4], F32, offset["small"])
        ZT16 = at("ZT16", [128, 256], BF16, offset["maskb"])

        s_moe = sem("s_moe")
        in_moe = (s_moe, 32)
        at_load[bias_at] = [(nsa_done, WR[:, :, :], w_router.rearrange("(k p) n -> p k n", p=128), s_moe),
                            (nsa_done, BR[:, :], b_router, s_moe)]

        sel_ready, se_free = {}, {}

        def selector(e):
            GP.wait(*se_free.get(e - 2, ()), m_ones, in_c)
            sel_ready[e] = (GP.mark(tt(SE[e % 2][:, :], sel32[:, e:e + 1].to_broadcast([128, 64]),
                                       ones[:, 0:1].to_broadcast([128, 64]), ALU.mult)),)

        GP.wait(in_moe, *heads_done, (GP.sem, GP.count))
        m_wr = GP.mark(tt(WR[:, :, :], WR[:, :, :], vec_("ln2").unsqueeze(2).to_broadcast([128, 8, 32]), ALU.mult))
        m_zt = GP.mark(cp(ZT16[:, :], cst_("zto", 128, 256)))
        selector(0)
        selector(1)

        GP.wait((GP.sem, GP.count))
        m_0 = GP.mark(fill(ST[2][:, 0:128], 0.0))
        def side(r, s, n):
            return BK[r][n * s:n * s + n, 0:8 * n]

        def bias(e, n=64):
            PE.wait(*sel_ready[e], *m_bu, *free[A], *free[B])
            a = 128 // n
            for i in range(2 * a):
                m = PE.mark(mm(side(A + i // a, i % a, n), SE[e % 2][:, 0:n], BU[:, 8 * n * i:8 * n * i + 8 * n],
                               True, False, True))

        h_marks, x3 = {}, {}
        JQ = [at(f"JQ{i}", [128, 512], BF16, B2 + (36 + i) * KB) for i in range(2)]
        A, B, T, D = 0, 1, 2, 3

        def rows_of_h(q, n):
            b = row_banks[q, n]
            t = TT[:, q, 512 * n:512 * n + 512]
            VE.wait(rows_done[q, n], m_rk, tt_ready[2 * q + n], *heads_done)
            x = VE.mark(stt(hr[:, q, 512 * n:512 * n + 512], BK[b][:, :], rk[:, 1, 1, q:q + 1], t, ALU.mult, ALU.add))
            free[b] = (x,)
            h_marks[q, n] = x
            SC.wait(x, (SC.sem, SC.count), *heads_done)
            a = SC.mark(act(JQ[n][:, :], hr[:, q, 512 * n:512 * n + 512], ACT.Square, accum_out=ss[:, q, n:n + 1]))
            squared[q] = a

        def rms_of_h(q):
            VE.wait(squared[q])
            x = VE.mark(tt(rt[:, q, 0:1], ss[:, q, 0:1], ss[:, q, 1:2], ALU.add))
            VE.wait(x)
            x = VE.mark(ts(rt[:, q, 0:1], rt[:, q, 0:1], 1.0 / 1024.0, ALU.mult, EPS, ALU.add))
            GP.wait(x, (GP.sem, GP.count))
            m_rt[q] = GP.mark(tt(rt[:, q, 1:2], rt[:, q, 0:1], cols[:, 1:2], ALU.pow))

        def columns_of_h(q, n):
            b = (2, 3, 4, 6)[2 * q + n]
            PE.wait(h_marks[q, n], *free[b])
            for c in range(4):
                m = PE.mark(tp(BK[b][:, 128 * c:128 * c + 128], hr[:, q, 128 * (4 * n + c):128 * (4 * n + c) + 128],
                               ident))
            L = VE if n else SC
            L.wait(m, *heads_done)
            dst = hT[:, 4 * n:4 * n + 4, 128 * q:128 * q + 128]
            src = BK[b][:, :].rearrange("p (c n) -> p c n", c=4)
            x = L.mark(cp(dst, src) if n else act(dst, src, ACT.Copy))
            free[b] = (x,)
            h_ready[4 * q + n] = x

        def logits(q, part):
            PE.wait(m_wr, *free[q], *fork)
            for dc in range(4 * part, 4 * part + 4):
                PE.wait(h_ready[4 * q + part])
                m = PE.mark(mm(BK[q][:, 0:32], hT[:, dc, 128 * q:128 * q + 128], WR[:, dc, :], dc == 0, dc == 7))
            return m

        def route(q, m):
            VE.wait(m_rt[q], m)
            x = VE.mark(stt(LG[:, q, :], BK[q][:, 0:32], rt[:, q, 1:2], BR[:, :], ALU.mult, ALU.add))
            free[q] = (x,)
            VE.wait(x)
            x = VE.mark(lambda e: e.max(mx[:, q, :], LG[:, q, :]))
            VE.wait(x)
            VE.do(ts(GT[:, q, :], LG[:, q, :], mx[:, q, 3:4], ALU.is_gt, 0.0, ALU.add, accum_out=rt[:, q, 2:3]))
            g = VE.mark(ts(EQ[:, q, :], LG[:, q, :], mx[:, q, 3:4], ALU.is_equal))
            VE.wait(g)
            x = VE.mark(lambda e: e.tensor_tensor_scan(CU[:, q, :], EQ[:, q, :], ones[:, :], rt[:, q, 2:3], ALU.add,
                                                       ALU.mult))
            VE.wait(x)
            x = VE.mark(stt(EQ[:, q, :], CU[:, q, :], 4.0, EQ[:, q, :], ALU.is_le, ALU.mult))
            VE.wait(x)
            m_sel.append(VE.mark(tt(MK[:, q, :], GT[:, q, :], EQ[:, q, :], ALU.add)))
            x = VE.mark(ts(LG[:, q, :], LG[:, q, :], mx[:, q, 0:1], ALU.subtract))
            SC.wait(x)
            m_ex.append(SC.mark(act(EX[:, q, :], LG[:, q, :], ACT.Exp)))

        def x3_first(q, c=slice(0, 1024)):
            SC.wait(m_rt[q], *(fork if q else heads_done))
            x3.setdefault((0, q), []).append(SC.mark(act(X3[:, 0, q, c], hr[:, q, c], ACT.Copy, scale=rt[:, q, 1:2])))

        def x3_rest(q, p, c=slice(0, 1024)):
            L = GP if (p, q) == (2, 0) else VE
            L.wait(x3[p - 1, q][-1], *[(L.sem, L.count)] * (L is GP))
            hi = X3[:, p - 1, q, c]
            if p == 1:
                x = VE.mark(stt(X_[q][:, c], hr[:, q, c], rt[:, q, 1:2], hi, ALU.mult, ALU.subtract))
            else:
                x = L.mark(tt(X_[q][:, c], X_[q][:, c], hi, ALU.subtract))
            SC.wait(x)
            x3.setdefault((p, q), []).append(SC.mark(act(X3[:, p, q, c], X_[q][:, c], ACT.Copy)))

        m_rt, m_sel, m_ex, squared = {}, [], [], {}
        ab = (slice(0, 512), slice(512, 1024))
        pieces = rows_product(1, 3)
        for n in range(2):
            next(pieces)
            rows_of_h(0, n)
        columns_of_h(0, 0)
        for n in range(2):
            next(pieces)
            rows_of_h(1, n)
        w_out_done = fork = [(PE.sem, PE.count)]
        rms_of_h(0)
        columns_of_h(0, 1)
        logits(0, 0)
        columns_of_h(1, 0)
        rms_of_h(1)
        columns_of_h(1, 1)
        x3_first(0)
        m0 = logits(0, 1)
        x3_rest(0, 1)
        for c in ab:
            x3_first(1, c)
        logits(1, 0)
        m1 = logits(1, 1)
        h_free = (m1,)
        PE.wait(m_0, *m_bu)
        for b in range(4, 8):
            PE.wait(*free[b])
            m_zero = PE.mark(mm(BK[b][:, :], ST[2][:, 0:128], BU[:, 0:512], True, False, True))
        route(0, m0)
        x3_rest(0, 2)
        route(1, m1)
        bias(0)
        x3_rest(1, 1, ab[0])
        PE.wait(*m_sel, m_zt, *free[3])
        tri, one = ZT16[:, 0:128], ZT16[:, 128:256]
        PE.do(mm(BK[3][:, 0:32], tri, MK[:, 0, :], True, True, True))
        PE.do(mm(BK[3][:, 32:64], one, MK[:, 0, :], False, False, True))
        PE.do(mm(BK[3][:, 32:64], tri, MK[:, 1, :], False, True, True))
        for q in range(2):
            m = PE.mark(mm(BK[3][:, 64:96], one, MK[:, q, :], False, q == 1, True))

        VE.wait(m)
        m_po = VE.mark(tt(PO[:, :, :], BK[3][:, 0:64].rearrange("p (q n) -> p q n", q=2), MK[:, :, :], ALU.mult))
        m_ci = VE.mark(cp(CI[:, :], BK[3][:, 64:96]))
        free[3] = (m_ci,)
        m_ww, m_w3 = [], []

        def weights():
            VE.wait(*m_ex)
            x = VE.mark(tt(WW[:, :, :], EX[:, :, :], MK[:, :, :], ALU.mult))
            VE.wait(x)
            x = VE.mark(red(rt[:, :, 3], WW[:, :, :], ALU.add))
            VE.wait(x)
            x = VE.mark(recip(rt[:, :, 4], rt[:, :, 3]))
            VE.wait(x)
            x = VE.mark(tt(WW[:, :, :], WW[:, :, :], rt[:, :, 4:5].to_broadcast([128, 2, 32]), ALU.mult))
            m_ww.append(x)
            for p in range(3):
                VE.wait(x)
                x = VE.mark(cp(W3[:, p, :, :], WW[:, :, :] if p == 0 else LG[:, :, :]))
                if p < 2:
                    VE.wait(x)
                    x = VE.mark(tt(LG[:, :, :], LG[:, :, :] if p else WW[:, :, :], W3[:, p, :, :], ALU.subtract))
            m_w3.append(x)

        st_free, ce_free, xs_free, ac_free = [[()] * 3 for _ in range(4)]
        one_free = {"AT": (), "Y": (), "G": (), "LI": (), "SG": ()}
        ce_ready, xs_ready, ac_ready, st_ready, ws_ready = [[()] * 3 for _ in range(5)]

        def onehot(e, first, n, u):
            VE.wait(m_po, in_c2, *st_free[u])
            shape = [128, 2, 128 // n, n]
            x = VE.mark(tt(ST[u][:, :].rearrange("p (q a s) -> p q a s", q=2, s=n),
                           cst_("iota", first, n).unsqueeze(1).unsqueeze(1).to_broadcast(shape),
                           PO[:, :, e:e + 1].unsqueeze(3).to_broadcast(shape), ALU.is_equal))
            st_ready[u] = (x,)

        def gather(u, n=64):
            PE.wait(*st_ready[u], *free[T])
            for p in range(3):
                for k in range(8):
                    for q in range(2):
                        PE.wait(x3[p, q][k // 4 if q else 0])
                        m = PE.mark(mm(BK[T][:, n * k:n * k + n], X3[:, p, q, 128 * k:128 * k + 128],
                                       ST[u][:, 128 * q:128 * q + n],
                                       p == 0 and k == 0 and q == 0, p == 2 and q == 1, True))
            VE.wait(m, *xs_free[u])
            x = VE.mark(tt(XS[u][:, :, 0:n], BK[T][:, 0:8 * n].rearrange("p (k n) -> p k n", k=8),
                           vec_("ln2").unsqueeze(2).to_broadcast([128, 8, n]), ALU.mult))
            free[T] = (x,)
            xs_ready[u] = (x,)

        def turn_onehot(e, u):
            PE.wait(*st_ready[u], *free[T])
            s = [ST[u][:, 128 * q:128 * q + 128] for q in range(2)]
            for q in range(2):
                PE.do(mm(BK[T][:, 128 * q:128 * q + 128], s[q], identb[:, :], q == 0, True, True))
            PE.wait(*m_w3)
            for i in range(6):
                m = PE.mark(mm(BK[T][:, 256:257], s[i % 2], W3[:, i // 2, i % 2, e:e + 1], False, i == 5, True))
            st_free[u] = (m,)
            SC.wait(m, *ce_free[u])
            SC.do(act(CE[u][:, :], BK[T][:, 0:256], ACT.Copy))
            x = SC.mark(act(WS[:, u:u + 1], BK[T][:, 256:257], ACT.Copy))
            free[T] = (x,)
            ce_ready[u] = (x,)

        def up(e, k, u, n=64):
            i = up_at[e, k]
            PE.wait(loaded(i), *xs_ready[u])
            a = 128 // n
            for c in range(2 * a):
                m = PE.mark(mm(side(A + c // a, c % a, n), XS[u][:, k, 0:n], slot(i)[:, 8 * n * c:8 * n * c + 8 * n],
                               False, k == 7, True))
            raw_free[i] = (m,)
            if k == 7:
                xs_free[u] = (m,)
            return m

        def swiglu(m, g_, li, sg, w=512):
            VE.wait(m, *one_free["G"])
            g = VE.mark(ts(g_[:, 0:w], BK[A][:, 0:w], 7.0, ALU.min))
            free[A] = (g,)
            SC.wait(g, *one_free["SG"])
            s = SC.mark(act(sg[:, 0:w], g_[:, 0:w], ACT.Sigmoid, scale=1.702))
            VE.wait(*one_free["LI"])
            x = VE.mark(ts(li[:, 0:w], BK[B][:, 0:w], 7.0, ALU.min, -7.0, ALU.max))
            free[B] = (x,)
            return g, s, x

        def swiglu_end(marks, u, ac, g_, li, sg, w=512):
            g, s, x = marks
            VE.wait(g, x)
            x = VE.mark(stt(li[:, 0:w], li[:, 0:w], 1.0, g_[:, 0:w], ALU.add, ALU.mult))
            VE.wait(x, s, *ce_ready[u], *ac_free[u // 2])
            y = VE.mark(stt(ac[:, 0:w], li[:, 0:w], WS[:, u:u + 1], sg[:, 0:w], ALU.mult, ALU.mult))
            one_free["G"], one_free["LI"], one_free["SG"] = (x, s), (y,), (y,)
            ac_ready[u // 2] = (y,)

        def turn(v, w=512):
            PE.wait(*ac_ready[v], *free[T])
            for q in range(w // 128):
                m = PE.mark(tp(BK[T][:, 128 * q:128 * q + 128], (AC0, AC1)[v][:, 128 * q:128 * q + 128], ident))
            ac_free[v] = (m,)
            SC.wait(m, *one_free["AT"])
            x = SC.mark(act(AT[:, 0:w], BK[T][:, 0:w], ACT.Copy))
            free[T] = (x,)
            return x

        def down_expert(e, ready, meanwhile=None, n=64):
            PE.wait(ready, *free[D])
            a, w = 128 // n, 8 * n
            for k in range(8):
                i = down_at[e, k // 2]
                PE.wait(loaded(i))
                o = 128 * (k % (w // 128)) + n * (k // (w // 128))
                for c in range(a):
                    s = 1024 * (k % 2) + w * c
                    m = PE.mark(mm(side(D, c, n), AT[:, o:o + n], slot(i)[:, s:s + w], k == 0, k == 7, True))
                raw_free[i] = (m,)
            one_free["AT"] = (m,)
            if meanwhile:
                next(meanwhile)
            SC.wait(m, *one_free["Y"])
            x = SC.mark(act(YH[:, 0:w], BK[D][:, 0:w], ACT.Copy))
            VE.wait(x, *one_free["Y"])
            y = VE.mark(tt(YL[:, 0:w], BK[D][:, 0:w], YH[:, 0:w].bitcast(F32), ALU.subtract))
            free[D] = (y,)
            if meanwhile:
                next(meanwhile, None)
            return (x, y)

        def combine(u, ready, last=False, n=64):
            PE.wait(*ready, *ce_ready[u])
            w = 8 * n
            for c0 in range(512 // w):
                for q in range(2):
                    for h_ in range(2):
                        c = c0 + 512 // w * h_
                        r = slice(n * c, n * c + n)
                        for y in (YH, YL):
                            m = PE.mark(mm(BK[4 + 2 * q + h_][:, w * c0:w * c0 + w], CE[u][r, 128 * q:128 * q + 128],
                                           y[r, 0:w], False, last and y is YL, True))
                PE.wait(m)
            one_free["Y"] = ce_free[u] = (m,)
            return m

        sooner = {}
        MORE = ((64, 32), (96, 64), (160, 64), (224, 32))

        def more_tokens(e, i=0):
            first, n = MORE[i]
            before = free[T]
            for k in range(8):
                if up_at[e, k] in (sooner if i else raw_free):
                    sooner.setdefault(up_at[e, k], []).append((e, first, raw_free[up_at[e, k]]))
            with Branch((PE, SC, VE), count, first):
                kept = {k: one_free[k] for k in ("G", "LI", "SG")}
                onehot(e, first, n, 2)
                gather(2, n)
                turn_onehot(e, 2)
                bias(e, n)
                for k in range(8):
                    m = up(e, k, 2, n)
                one_free["G"], one_free["LI"], one_free["SG"] = one_free["AT"], one_free["Y"], ac_free[1]
                marks = swiglu(m, AT, YF, AC1, 8 * n)
                swiglu_end(marks, 2, AC1, AT, YF, AC1, 8 * n)
                one_free["AT"], one_free["Y"] = one_free["G"], one_free["LI"]
                combine(2, down_expert(e, turn(1, 8 * n), None, n), False, n)
                if i + 1 < len(MORE):
                    more_tokens(e, i + 1)
                one_free.update(kept)
            free[T] = (*before, *free[T])

        def bias_down():
            PE.wait(*m_ww, *free[T])
            for q in range(2):
                m = PE.mark(mm(BK[T][32:64, 128 * q:128 * q + 128], WW[:, q, :], ident, q == 0, True, True))
            VE.wait(m)
            x = VE.mark(cp(WT[32:64, :], BK[T][32:64, 0:256]))
            free[T] = (x,)
            PE.wait(x)
            for q in range(2):
                for n in range(2):
                    m = PE.mark(mm(BK[4 + 2 * q + n][:, :], WT[32:64, 128 * q:128 * q + 128],
                                   slot(bias_at)[32:64, 512 * n:512 * n + 512], False, False, True))
            raw_free[bias_at] = (m,)

        PQ = [slot(pt_at)[:, 512:1536], slot(wple_at)[:, 0:1024]]

        def ple_products():
            PE.wait(loaded(wple_at), loaded(pt_at))
            for q in range(2):
                for n, b in enumerate((T, D)):
                    PE.wait(*free[b])
                    for k in range(2):
                        m = PE.mark(mm(BK[b][:, :], slot(pt_at)[:, 256 * k + 128 * q:256 * k + 128 * q + 128],
                                       slot(wple_at)[:, 1024 * k + 512 * n:1024 * k + 512 * n + 512], k == 0, k == 1))
                    SC.wait(m)
                    x = SC.mark(act(PQ[q][:, 512 * n:512 * n + 512], BK[b][:, :], ACT.Copy))
                    free[b] = (x,)
                    pq_ready.append(x)

        pq_ready = []
        count = {}
        GH, GL = {}, {}

        def split_gate():
            for n in range(8):
                if n in (2, 6):
                    yield
                i = gate_at[n // 2]
                c = slice(1024 * (n % 2), 1024 * (n % 2) + 1024)
                GH[n], GL[n] = slot(kept_ups[n // 2], F32R)[:, c], slot(i, F32R)[:, c]
                SC.wait(loaded(i), last_up)
                a_ = SC.mark(act(GH[n], slot(i)[:, c], ACT.Copy))
                L = GP if n in (4, 5, 7) else VE
                L.wait(a_, last_up)
                x = L.mark(tt(GL[n], slot(i)[:, c], GH[n].bitcast(F32), ALU.subtract))
                gate_ready.append((a_, x))

        gate_ready, gate_parts = [], split_gate()
        kept_ups = [up_at[NE - 1, k] for k in range(8)
                    if place[up_at[NE - 1, k]] not in [place[i] for i in (*gate_at, lnf_at)]]

        def counts(e, lines=(PE, SC, VE)):
            for L in lines:
                L.wait(m_ci)
                L.do(lambda x, L=L: count.__setitem__(id(L), x.value_load(CI[0:1, e:e + 1], min_val=0, max_val=256)))

        onehot(0, 0, 64, 0)
        x3_rest(1, 1, ab[1])
        st_free[2] = (m_zero,)
        for c in ab:
            x3_rest(1, 2, c)
        gather(0)
        weights()
        for e in range(NE + 1):
            u, w = e % 2, 1 - e % 2
            if 0 < e < NE:
                bias(e)
            near = e == NE - 1
            if e < NE - 1:
                up(e, 0, u)
                up(e, 1, u)
            if e == 0:
                turn_onehot(0, 0)
            if e:
                swiglu_end(marks, w, AC0, G, LI, SG)
                x = turn(0)
            if e < NE - 1:
                up(e, 2, u)
            if e:
                y = down_expert(e - 1, x, gate_parts if e == NE else None)
            if e == NE:
                y_done = combine(w, y, True)
                break
            if e == 0:
                bias_down()
            if near:
                for k in range(3):
                    up(e, k, u)
            up(e, 3, u)
            if 0 < e < NE - 1:
                onehot(e + 1, 0, 64, w)
                gather(w)
            up(e, 4, u)
            if e == NE - 2:
                ple_products()
            for k in range(5, 8):
                if near and k == 6:
                    combine(w, y)
                m = up(e, k, u)
            marks = swiglu(m, G, LI, SG)
            if e and not near:
                combine(w, y)
            if e == 0:
                onehot(e + 1, 0, 64, w)
                gather(w)
            if e + 1 < NE:
                turn_onehot(e + 1, w)
            counts(e)
            more_tokens(e)
            last_up = (PE.sem, PE.count)
            se_free[e] = (last_up,)
            if e + 2 < NE:
                selector(e + 2)

        UH = at("UH", [128, 8, 256], F32R, B2 + 8 * KB)
        UL = at("UL", [128, 8, 256], F32R, B2 + 16 * KB)
        fork = [(PE.sem, PE.count), (SC.sem, SC.count), (VE.sem, VE.count)]

        def row_rstd(j, q, ready):
            VE.wait(*ready)
            x = VE.mark(tt(rt[:, q, j:j + 1], ss[:, q, 0:1], ss[:, q, 1:2], ALU.add))
            VE.wait(x)
            x = VE.mark(ts(rt[:, q, j:j + 1], rt[:, q, j:j + 1], 1.0 / 1024.0, ALU.mult, EPS, ALU.add))
            GP.wait(x, (GP.sem, GP.count))
            return GP.mark(tt(rt[:, q, j + 1:j + 2], rt[:, q, j:j + 1], cols[:, 1:2], ALU.pow))

        VE.wait(*fork)
        SC.wait(*fork)
        junk = (G, LI, AC0, AC1)
        u_ready = {}
        for q in range(2):
            for n in range(2):
                VE.wait(y_done)
                x = VE.mark(tt(hr[:, q, 512 * n:512 * n + 512], BK[4 + 2 * q + n][:, :], hr[:, q, 512 * n:512 * n + 512],
                               ALU.add))
                free[4 + 2 * q + n] = (x,)
                SC.wait(x)
                a = SC.mark(act(junk[2 * q + n][:, :], hr[:, q, 512 * n:512 * n + 512], ACT.Square,
                                accum_out=ss[:, q, n:n + 1]))
                PE.wait(x, *free[0], *free[1], *free[2], *free[3])
                for c in range(4):
                    k = 4 * n + c
                    m = PE.mark(tp(BK[k // 2][:, 256 * (k % 2) + 128 * q:256 * (k % 2) + 128 * q + 128],
                                   hr[:, q, 128 * k:128 * k + 128], ident))
                    u_ready[k] = (m,)
        m_rt = [row_rstd(5, q, (a,)) for q in range(2)]
        k_order = (0, 2, 1, 3, 4, 6, 5, 7)
        for k in k_order:
            src = BK[k // 2][:, 256 * (k % 2):256 * (k % 2) + 256]
            g = vec_("lnp", k, 1)
            SC.wait(*u_ready[k], *(u_ready[k - 1] if k % 2 else u_ready[k + 1]))
            a = SC.mark(act(UH[:, k, :], src, ACT.Copy, scale=g))
            VE.wait(a)
            x = VE.mark(stt(UL[:, k, :], src, g, UH[:, k, :].bitcast(F32), ALU.mult, ALU.subtract))
            u_ready[k] = (a, x)
        next(gate_parts, None)
        out_ready = []

        def res(q, c):
            return slot(kept_ups[4])[:, 1024 * q + c.start:1024 * q + c.stop]

        VE.wait(*pq_ready, loaded(lnf_at))
        SC.wait(*m_rt)
        for q in range(2):
            for n in range(2):
                b = 4 + 2 * q + n
                c = slice(512 * n, 512 * n + 512)
                h_, l_, t = hr[:, q, c], slot(lnf_at)[:, c], junk[2 * q + n][:, :]
                PE.wait(*free[b])
                for k in k_order:
                    PE.wait(*u_ready[k], *gate_ready[k])
                    m = PE.mark(mm3(BK[b][:, :], UH[:, k, 128 * q:128 * q + 128], UL[:, k, 128 * q:128 * q + 128],
                                    GH[k][:, c], GL[k][:, c], k == 0, k == 7))
                SC.wait(m)
                a = SC.mark(act(t, BK[b][:, :], ACT.Sigmoid, scale=rt[:, q, 6:7]))
                VE.wait(a)
                x = VE.mark(tt(t, t, PQ[q][:, c], ALU.mult))
                VE.wait(x)
                x = VE.mark(tt(h_, h_, t, ALU.add))
                SC.wait(x)
                a = SC.mark(act(t, h_, ACT.Square, accum_out=ss[:, q, n:n + 1]))
                VE.wait(x)
                x = VE.mark(tt(res(q, c), h_, l_, ALU.mult))
            m_rt = row_rstd(3, q, (a,))
            VE.wait(m_rt, x)
            SC.wait(m_rt, x)
            r0, r1 = res(q, slice(0, 512)), res(q, slice(512, 1024))
            out_ready.append((SC.mark(act(r1, r1, ACT.Copy, scale=rt[:, q, 4:5])),
                              VE.mark(ts(r0, r0, rt[:, q, 4:5], ALU.mult))))

        last_in = {r: first for rs, first in (((NR, NR + 1, NR + 6), nsa_done), (range(NR + 2, NR + 6), fox_done), (range(NR + 7, NR + 11), w_out_done),
                                              ((NR + 11,), h_free)) for r in rs}
        read, last_of = set(), {}

        def wait_free(i):
            def later(x, levels):
                if levels:
                    (e, limit, marks), *rest = levels
                    for s, v in marks:
                        x.wait_ge(s, v)
                    with x.If(count[id(SP)] > limit):
                        later(x, rest)
                else:
                    for s, v in raw_free[i]:
                        x.wait_ge(s, v)

            if i in sooner:
                e = sooner[i][0][0]
                if e not in read:
                    counts(e, (SP,))
                    read.add(e)
                SP.do(lambda x: later(x, sooner[i]))
            else:
                SP.wait(*raw_free[i])

        for i, (pieces, value) in enumerate(loads):
            r = place[i]
            if r in last_of:
                wait_free(last_of[r])
            else:
                SP.wait(*last_in.get(r, ()))
            last_of[r] = i
            if i in at_load:
                for marks, d, src, sm in at_load[i]:
                    SP.wait(*marks)
                    SP.do(lambda e, d=d, src=src, sm=sm: e.dma_start(d, src).then_inc(sm, 16))
            for view, src in pieces:
                d = view(slots[F32][r][:, :])
                SP.do(lambda e, d=d, src=src, r=r: e.dma_start(d, src).then_inc(s_raw[r], 16))

        s_out = sem("s_out")
        for q in range(2):
            SP.wait(*out_ready[q])
            SP.do(lambda e, q=q: e.dma_start(out[0, 128 * q:128 * q + 128, :], res(q, slice(0, 1024))).then_inc(s_out, 16))
        SP.wait((s_out, 32))

        block = ctx.enter_context(nc.Block())

        @block.tensor
        def _(e):
            PE.run(e)

        @block.scalar
        def _(e):
            SC.run(e)

        @block.vector
        def _(e):
            VE.run(e)

        @block.gpsimd
        def _(e):
            GP.run(e)

        @block.sync
        def _(e):
            SP.run(e)


def pack(inputs):
    f = {k: np.asarray(v) for k, v in inputs.items()}

    def chunks(v):
        return v.reshape(-1, 128).T

    def rows(v):
        return np.broadcast_to(v.reshape(1, -1), (128, v.size))

    i = np.arange(128)
    cid = np.concatenate([np.eye(128), i[:, None] % 32 == np.arange(32)[None]], 1).astype(np.float32)
    cst1, cst2 = np.zeros((128, N1), np.float32), np.zeros((128, N2), np.float32)

    def c(name):
        if name in CST1:
            return cst1[:, CST1[name][0]:CST1[name][1]]
        return cst2[:, CST2[name][0]:CST2[name][1]]

    c("blk")[:] = (i[:, None] // 64 == i[None] // 64) / 64.0
    c("perm")[:] = i[:, None] == (i[None] ^ 32)
    t = np.arange(256)
    inv = np.power(np.float32(10000.0), -np.arange(16, dtype=np.float32) / np.float32(16.0))
    ang = np.concatenate([(t // 64).astype(np.float32)[None] * inv[:, None],
                          (t % 64).astype(np.float32)[None] * inv[:, None]], 0)
    c("cos")[:] = np.tile(np.cos(ang), (4, 1))
    c("sin")[:] = np.tile(np.concatenate([-np.sin(ang), np.sin(ang)], 0), (2, 1))
    c("m01")[:] = np.where(i[None] <= i[:, None], 0.0, NEG)
    c("m10")[:] = np.where(i[None] >= i[:, None], 0.0, NEG)
    c("hd")[:] = (i[:, None] // 64 == np.arange(32)[None]) / 64.0
    c("zto")[:, 128:256] = i[:, None] <= i[None]
    c("zto")[:, 256:384] = 1.0
    end = np.arange(16) * 16 + 31
    for qt in range(2):
        seen = (end[None] <= (128 * qt + i)[:, None]) & (np.arange(16) < 15)[None]
        for h in range(8):
            u = 16 * (8 * qt + h)
            c("cmask")[:, u:u + 16] = seen
            c("cbias")[:, u:u + 16] = np.where(seen, -2.0 ** -(h + 1) * ((128 * qt + i)[:, None] - end[None]), NEG)
    c("hrow")[:] = i[:, None] // 16 == np.arange(8)[None]
    c("alibi")[:] = np.where(t[None] <= 128 + i[:, None], t[None] - 128 - i[:, None], NEG)
    c("iota")[:] = t[None] + 1.0
    c("pick")[:] = (i[:, None] % 32 == np.arange(8)[None]) & (i[:, None] < 96)

    vec = np.zeros((128, NVEC), np.float32)

    def v(name):
        a, b = VEC[name]
        return vec[:, a:b]

    cc = v("cc").reshape(128, 8, 32)
    cc[:, :, 0] = chunks(f["c"][0])
    cc[:, :, 1] = chunks(f["c_ctx"])
    for l in range(2):
        v(f"nm{l}")[:] = chunks(f["norm_mix"][l])
        v(f"nf{l}")[:] = chunks(f["norm_ffn"][l])
        v(f"ada_b{l}")[:] = chunks(f["ada_b"][l])
        v(f"conv{l}")[:] = np.concatenate([chunks(f["ffn_conv"][l, j]) for j in range(3)], 1)
    v("scconv")[:] = np.concatenate([chunks(f["sc_conv"][0, j]) for j in range(3)], 1)
    v("qn")[:, 0] = np.tile(f["win_q_norm"][0], 2)
    v("kn")[:, 0] = np.tile(f["win_k_norm"][0], 2)
    v("sink")[:] = rows(f["win_sink"][0])
    v("ln1")[:] = chunks(f["ln1_2"][0])
    v("ln2")[:] = chunks(f["ln2_2"][0])
    v("lnp")[:] = chunks(f["ln_ple_2"][0])
    v("lnf")[:] = chunks(f["ln_f_2"])
    v("gn")[:] = np.concatenate([chunks(f["gn_nsa_2"][0]), chunks(f["gn_fox_2"][0])], 1)

    for n, x in enumerate("kv"):
        v(f"pe{n}")[:] = np.tile(f[f"pe_cmp_{x}_2"][0].T, (2, 1))
    v("bfg")[:] = rows(f["b_fg_2"][0])
    v("w2k")[:] = np.tile(f["w_cmp2_k_2"][0], (1, 2))
    v("w2v")[:] = f["w_cmp2_v_2"][0]

    def T(x):
        return np.ascontiguousarray(x.T.reshape(-1, 128, x.shape[0]).transpose(1, 0, 2))

    return dict(xT=T(f["x"][0]), ctxT=T(f["ctx"][0]), cid=cid, cst1=cst1, cst2=cst2, vec=vec, ada_w=f["ada_w"],
                w_qkv=f["win_w_qkv"][0], w_o=f["win_w_o"][0], w_up=f["ffn_w_up"], w_down=f["ffn_w_down"],
                sc_in=f["sc_w_in"][0], sc_out=f["sc_w_out"][0], w_in=f["w_in_2"][0],
                w_cmp1=np.stack([f["w_cmp1_k_2"][0], f["w_cmp1_v_2"][0]]), w_out=f["w_out_2"][0],
                moe_up=f["w_up_2"][0], moe_down=f["w_down_2"][0], b_up=f["b_up_2"][0], b_down=f["b_down_2"][0],
                w_router=f["w_router_2"][0], b_router=np.ascontiguousarray(rows(f["b_router_2"][0])),
                pT=T(f["p_2"][0, 0]), w_ple=f["w_ple_2"][0], w_gate=f["w_ple_gate_2"][0],
                ln_f=np.ascontiguousarray(rows(f["ln_f_2"])))


def kernel(**inputs):
    import concourse.bacc as bacc
    from concourse.bass_utils import run_bass_kernel_spmd

    nc = bacc.Bacc("TRN2", target_bir_lowering=False, num_devices=1)
    arrays = {n: np.ascontiguousarray(a) for n, a in pack(inputs).items()}
    args = {n: nc.dram_tensor(n, a.shape, mybir.dt.from_np(a.dtype), kind="ExternalInput").ap()
            for n, a in arrays.items()}
    out = nc.dram_tensor("out", (1, 256, 1024), F32, kind="ExternalOutput").ap()
    program(nc, out=out, **args)
    return run_bass_kernel_spmd(nc, [arrays], core_ids=[0]).results[0]["out"]
```
